# Optimizing a Trainium2 kernel written in Bass

```python
import jax, jax.numpy as jnp
from jax import lax
import numpy as np

D_MODEL = 1024
BATCH = 1
SEQ = 512
DEPTH = 2

HEAD_DIM = 64
ROT_DIM = HEAD_DIM // 4
ROPE_THETA = 500000.0
RMS_EPS = 1e-6
Q_BLOCK = 128
MACARON_WEIGHT = 0.5
D_FF = 2816

A_HEADS = 8
A_KV_RANK = 128
IDX_HEADS = 8
IDX_DIM = 64
TOPK_MAX = 256

B_GROUPS = ((128, 1), (512, 4), (2048, 16))
B_HEADS_PER_GROUP = 4
B_HEADS = B_HEADS_PER_GROUP * len(B_GROUPS)

C_HEADS = 4
C_HEAD_K = 64
C_HEAD_V = 128
C_ALPHA_RANK = 16
C_GATE_TAU = 16.0
C_CHUNK = 64

N_BRANCH = 3
IN_SIZES = (A_HEADS * HEAD_DIM, A_KV_RANK, IDX_HEADS * IDX_DIM, IDX_DIM, IDX_HEADS,
            3 * B_HEADS * HEAD_DIM,
            C_HEADS * C_HEAD_K, C_HEADS * C_HEAD_K, C_HEADS * C_HEAD_V, C_HEADS * C_HEAD_V,
            C_ALPHA_RANK)
D_IN = sum(IN_SIZES)

kernel_name = 'hybrid_dsa_dilated_gla_macaron'

def rms_norm(x, g):
    xf = x.astype(jnp.float32)
    y = xf * lax.rsqrt(jnp.mean(xf * xf, axis=-1, keepdims=True) + RMS_EPS)
    return (y * g.astype(jnp.float32)).astype(x.dtype)

def swiglu(x, w_in, w_out):
    gate, up = jnp.split(x @ w_in, 2, axis=-1)
    return (jax.nn.silu(gate) * up) @ w_out

def rope_tables(positions, rot_dim):
    inv_freq = ROPE_THETA ** (-jnp.arange(0, rot_dim, 2, dtype=jnp.float32) / rot_dim)
    ang = positions.astype(jnp.float32)[..., None] * inv_freq
    return jnp.cos(ang), jnp.sin(ang)

def partial_rope(x, cos, sin):
    half = cos.shape[-1]
    c = cos[:, :, None, :]
    s = sin[:, :, None, :]
    x1 = x[..., :half].astype(jnp.float32)
    x2 = x[..., half:2 * half].astype(jnp.float32)
    rot = jnp.concatenate([x1 * c - x2 * s, x2 * c + x1 * s], axis=-1).astype(x.dtype)
    return jnp.concatenate([rot, x[..., 2 * half:]], axis=-1)

def to_blocks(a):
    b, s = a.shape[:2]
    a = a.reshape((b, s // Q_BLOCK, Q_BLOCK) + a.shape[2:])
    return jnp.moveaxis(a, 1, 0)

def from_blocks(a):
    a = jnp.moveaxis(a, 0, 1)
    return a.reshape((a.shape[0], a.shape[1] * a.shape[2]) + a.shape[3:])

def dsa_attention(q, k, v, q_idx, k_idx, w_idx, top_k):
    seq = q.shape[1]
    key_pos = jnp.arange(seq, dtype=jnp.int32)
    k_idx_f = k_idx.astype(jnp.float32)
    scale = HEAD_DIM ** -0.5
    idx_scale = IDX_DIM ** -0.5
    head_w_scale = IDX_HEADS ** -0.5

    def block(args):
        qb, qib, wb, tb = args
        logits = jnp.einsum('bqhd,bsd->bqhs', qib.astype(jnp.float32), k_idx_f) * idx_scale
        score = jnp.einsum('bqhs,bqh->bqs', jax.nn.relu(logits),
                           wb.astype(jnp.float32) * head_w_scale)
        causal = key_pos[None, :] <= tb[:, None]
        score = jnp.where(causal[None], score, -jnp.inf)
        _, sel = lax.top_k(score, top_k)
        ks = jax.vmap(lambda kk, ii: kk[ii])(k, sel)
        vs = jax.vmap(lambda vv, ii: vv[ii])(v, sel)
        s = jnp.einsum('bqhd,bqkhd->bqhk', qb.astype(jnp.float32),
                       ks.astype(jnp.float32)) * scale
        valid = sel <= tb[None, :, None]
        s = jnp.where(valid[:, :, None, :], s, -jnp.inf)
        p = jax.nn.softmax(s, axis=-1)
        return jnp.einsum('bqhk,bqkhd->bqhd', p, vs.astype(jnp.float32)).astype(qb.dtype)

    pos_blocks = key_pos.reshape(seq // Q_BLOCK, Q_BLOCK)
    out = lax.map(block, (to_blocks(q), to_blocks(q_idx), to_blocks(w_idx), pos_blocks))
    return from_blocks(out)

def dilated_attention(q, k, v):
    seq = q.shape[1]
    hpg = B_HEADS_PER_GROUP
    scale = HEAD_DIM ** -0.5
    k_groups = [k[:, :, g * hpg:(g + 1) * hpg] for g in range(len(B_GROUPS))]
    v_groups = [v[:, :, g * hpg:(g + 1) * hpg] for g in range(len(B_GROUPS))]

    def block(args):
        qb, tb = args
        outs, lses = [], []
        for g, (window, dil) in enumerate(B_GROUPS):
            n_keys = window // dil + 1
            idx = tb[:, None] - dil * jnp.arange(n_keys, dtype=jnp.int32)[None, :]
            valid = idx >= 0
            idx_c = jnp.maximum(idx, 0)
            kg = jnp.take(k_groups[g], idx_c, axis=1).astype(jnp.float32)
            vg = jnp.take(v_groups[g], idx_c, axis=1).astype(jnp.float32)
            qg = qb[:, :, g * hpg:(g + 1) * hpg].astype(jnp.float32)
            s = jnp.einsum('bqhd,bqjhd->bqhj', qg, kg) * scale
            s = jnp.where(valid[None, :, None, :], s, -jnp.inf)
            lse = jax.nn.logsumexp(s, axis=-1)
            p = jnp.exp(s - lse[..., None])
            outs.append(jnp.einsum('bqhj,bqjhd->bqhd', p, vg))
            lses.append(lse)
        wgt = jax.nn.softmax(jnp.stack(lses, axis=0), axis=0)
        o = jnp.sum(wgt[..., None] * jnp.stack(outs, axis=0), axis=0)
        return o.astype(qb.dtype)

    pos_blocks = jnp.arange(seq, dtype=jnp.int32).reshape(seq // Q_BLOCK, Q_BLOCK)
    return from_blocks(lax.map(block, (to_blocks(q), pos_blocks)))

def gla_chunked(q, k, v, log_alpha):
    bsz, seq, nh, dk = q.shape
    dv = v.shape[-1]
    csz = min(C_CHUNK, seq)
    nc = seq // csz
    f32 = jnp.float32
    q = q.astype(f32).reshape(bsz, nc, csz, nh, dk) * dk ** -0.5
    k = k.astype(f32).reshape(bsz, nc, csz, nh, dk)
    v = v.astype(f32).reshape(bsz, nc, csz, nh, dv)
    b = jnp.cumsum(log_alpha.astype(f32).reshape(bsz, nc, csz, nh, dk), axis=2)
    b_last = b[:, :, -1]
    q_dec = q * jnp.exp(b)
    k_dec = k * jnp.exp(-b)
    attn = jnp.einsum('bnthd,bnshd->bnhts', q_dec, k_dec)
    attn = jnp.where(jnp.tril(jnp.ones((csz, csz), dtype=bool)), attn, 0.0)
    o_intra = jnp.einsum('bnhts,bnshv->bnthv', attn, v)
    k_to_end = k * jnp.exp(b_last[:, :, None] - b)
    kv = jnp.einsum('bnshk,bnshv->bnhkv', k_to_end, v)
    decay = jnp.exp(b_last)

    def step(state, inp):
        kv_n, dec_n = inp
        return dec_n[..., None] * state + kv_n, state

    init = jnp.zeros((bsz, nh, dk, dv), f32)
    _, s_prev = lax.scan(step, init, (jnp.moveaxis(kv, 1, 0), jnp.moveaxis(decay, 1, 0)))
    s_prev = jnp.moveaxis(s_prev, 0, 1)
    o_inter = jnp.einsum('bnthk,bnhkv->bnthv', q_dec, s_prev)
    return (o_intra + o_inter).reshape(bsz, seq, nh, dv)

def hybrid_mixer(u, cos, sin, top_k, w_in, a_kv_norm_g, a_w_kv_up, c_w_alpha_up, c_b_alpha,
                 c_norm_g, w_branch_a, w_branch_b, w_branch_c, w_gate, b_gate, w_out):
    bsz, seq, d = u.shape
    split_points = np.cumsum(IN_SIZES)[:-1].tolist()
    (a_q, a_ckv, i_q, i_k, i_w, b_qkv, c_q, c_k, c_v, c_g, c_a) = jnp.split(
        u @ w_in, split_points, axis=-1)

    q_a = partial_rope(a_q.reshape(bsz, seq, A_HEADS, HEAD_DIM), cos, sin)
    kv_a = (rms_norm(a_ckv, a_kv_norm_g) @ a_w_kv_up).reshape(bsz, seq, A_HEADS, 2, HEAD_DIM)
    k_a = partial_rope(kv_a[..., 0, :], cos, sin)
    v_a = kv_a[..., 1, :]
    q_i = partial_rope(i_q.reshape(bsz, seq, IDX_HEADS, IDX_DIM), cos, sin)
    k_i = partial_rope(i_k[:, :, None, :], cos, sin)[:, :, 0]
    y_a = dsa_attention(q_a, k_a, v_a, q_i, k_i, i_w, top_k).reshape(bsz, seq, A_HEADS * HEAD_DIM)

    qkv_b = b_qkv.reshape(bsz, seq, 3, B_HEADS, HEAD_DIM)
    q_b = partial_rope(qkv_b[:, :, 0], cos, sin)
    k_b = partial_rope(qkv_b[:, :, 1], cos, sin)
    y_b = dilated_attention(q_b, k_b, qkv_b[:, :, 2]).reshape(bsz, seq, B_HEADS_PER_GROUP * HEAD_DIM)

    log_alpha = jax.nn.log_sigmoid((c_a @ c_w_alpha_up + c_b_alpha).astype(jnp.float32)) / C_GATE_TAU
    o_c = gla_chunked(c_q.reshape(bsz, seq, C_HEADS, C_HEAD_K),
                      c_k.reshape(bsz, seq, C_HEADS, C_HEAD_K),
                      c_v.reshape(bsz, seq, C_HEADS, C_HEAD_V),
                      log_alpha.reshape(bsz, seq, C_HEADS, C_HEAD_K))
    o_c = rms_norm(o_c.astype(u.dtype), c_norm_g) * jax.nn.silu(c_g.reshape(bsz, seq, C_HEADS, C_HEAD_V))
    y_c = o_c.reshape(bsz, seq, C_HEADS * C_HEAD_V)

    gates = jax.nn.sigmoid(u @ w_gate + b_gate).reshape(bsz, seq, N_BRANCH, d)
    merged = (gates[:, :, 0] * (y_a @ w_branch_a)
              + gates[:, :, 1] * (y_b @ w_branch_b)
              + gates[:, :, 2] * (y_c @ w_branch_c))
    return merged @ w_out

def setup_inputs(seed: int = 0) -> dict:
    key = jax.random.key(seed)
    ks = jax.random.split(key, 24)

    def nrm(i, shape, fan_in):
        return jax.random.normal(ks[i], shape, jnp.float32) * fan_in ** -0.5

    def gain(i, n):
        return 1.0 + 0.02 * jax.random.normal(ks[i], (DEPTH, n), jnp.float32)

    x = jax.random.normal(ks[0], (BATCH, SEQ, D_MODEL), jnp.float32)
    positions = (jax.random.randint(ks[1], (BATCH, 1), 0, 4096, dtype=jnp.int32)
                 + jnp.arange(SEQ, dtype=jnp.int32)[None, :])
    return {
        'x': x,
        'positions': positions,
        'ffn1_pre_g': gain(2, D_MODEL),
        'ffn1_w_in': nrm(3, (DEPTH, D_MODEL, 2 * D_FF), D_MODEL),
        'ffn1_w_out': nrm(4, (DEPTH, D_FF, D_MODEL), D_FF),
        'ffn1_post_g': gain(5, D_MODEL),
        'mix_pre_g': gain(6, D_MODEL),
        'w_in': nrm(7, (DEPTH, D_MODEL, D_IN), D_MODEL),
        'a_kv_norm_g': gain(8, A_KV_RANK),
        'a_w_kv_up': nrm(9, (DEPTH, A_KV_RANK, 2 * A_HEADS * HEAD_DIM), A_KV_RANK),
        'c_w_alpha_up': nrm(10, (DEPTH, C_ALPHA_RANK, C_HEADS * C_HEAD_K), C_ALPHA_RANK),
        'c_b_alpha': 0.1 * jax.random.normal(ks[11], (DEPTH, C_HEADS * C_HEAD_K), jnp.float32),
        'c_norm_g': gain(12, C_HEAD_V),
        'w_branch_a': nrm(13, (DEPTH, A_HEADS * HEAD_DIM, D_MODEL), A_HEADS * HEAD_DIM),
        'w_branch_b': nrm(14, (DEPTH, B_HEADS_PER_GROUP * HEAD_DIM, D_MODEL), B_HEADS_PER_GROUP * HEAD_DIM),
        'w_branch_c': nrm(15, (DEPTH, C_HEADS * C_HEAD_V, D_MODEL), C_HEADS * C_HEAD_V),
        'w_gate': nrm(16, (DEPTH, D_MODEL, N_BRANCH * D_MODEL), D_MODEL),
        'b_gate': 0.02 * jax.random.normal(ks[17], (DEPTH, N_BRANCH * D_MODEL), jnp.float32),
        'w_out': nrm(18, (DEPTH, D_MODEL, D_MODEL), D_MODEL),
        'mix_post_g': gain(19, D_MODEL),
        'ffn2_pre_g': gain(20, D_MODEL),
        'ffn2_w_in': nrm(21, (DEPTH, D_MODEL, 2 * D_FF), D_MODEL),
        'ffn2_w_out': nrm(22, (DEPTH, D_FF, D_MODEL), D_FF),
        'ffn2_post_g': gain(23, D_MODEL),
    }

def reference(x, positions, ffn1_pre_g, ffn1_w_in, ffn1_w_out, ffn1_post_g, mix_pre_g, w_in,
              a_kv_norm_g, a_w_kv_up, c_w_alpha_up, c_b_alpha, c_norm_g, w_branch_a, w_branch_b,
              w_branch_c, w_gate, b_gate, w_out, mix_post_g, ffn2_pre_g, ffn2_w_in, ffn2_w_out,
              ffn2_post_g):
    top_k = min(TOPK_MAX, x.shape[1] // 4)
    cos, sin = rope_tables(positions, ROT_DIM)
    h = x
    for l in range(DEPTH):
        f1 = swiglu(rms_norm(h, ffn1_pre_g[l]), ffn1_w_in[l], ffn1_w_out[l])
        h = h + MACARON_WEIGHT * rms_norm(f1, ffn1_post_g[l])
        m = hybrid_mixer(rms_norm(h, mix_pre_g[l]), cos, sin, top_k, w_in[l], a_kv_norm_g[l],
                         a_w_kv_up[l], c_w_alpha_up[l], c_b_alpha[l], c_norm_g[l], w_branch_a[l],
                         w_branch_b[l], w_branch_c[l], w_gate[l], b_gate[l], w_out[l])
        h = h + rms_norm(m, mix_post_g[l])
        f2 = swiglu(rms_norm(h, ffn2_pre_g[l]), ffn2_w_in[l], ffn2_w_out[l])
        h = h + MACARON_WEIGHT * rms_norm(f2, ffn2_post_g[l])
    return h


_drawn_inputs = setup_inputs


def setup_inputs(seed=0):
    import zlib

    import numpy as np

    out = dict(_drawn_inputs(seed))
    spreads = {}
    factors = {'a_kv_norm_g': 4.195, 'b_gate': 4.453, 'ffn2_pre_g': 3.085, 'ffn2_post_g': 3.991}
    for name, (base, spread) in spreads.items():
        noise = np.random.default_rng([zlib.crc32(name.encode()), seed]).standard_normal(out[name].shape)
        drawn = base * np.exp(spread * noise) if base else spread * noise
        out[name] = __import__('jax').numpy.asarray(drawn.astype(out[name].dtype))
    for name, factor in factors.items():
        out[name] = (out[name] * factor).astype(out[name].dtype)
    return out
```

```python
from contextlib import ExitStack

import numpy as np
import concourse.bass as bass
from concourse import mybir

F32 = mybir.dt.float32
F32R = mybir.dt.float32r
I32 = mybir.dt.int32
ALU = mybir.AluOpType
ACT = mybir.ActivationFunctionType
AX = mybir.AxisListType

P = 128
DEPTH, SEQ, DM, DFF = 2, 512, 1024, 2816
HD, ROT, THETA, EPS = 64, 16, 500000.0, 1e-6
A_HEADS, B_HEADS, C_HEADS, GROUPS = 8, 4, 4, 3
TOPK = min(256, SEQ // 4)
KD = DM // P
KF = DFF // P
NB = SEQ // P
CH = 64
NEG = -1.0e30
TAKEN = -3.0e38
TAU = 16.0
SIZES = (512, 128, 512, 64, 8, 2304, 256, 256, 512, 512, 16)
OFF = [0] + np.cumsum(SIZES).tolist()

FFN_IN, FFN_OUT, PROJ, MERGE, WOUT = 2 * KF, 3 * KD, 44, 5 * KD, KD
S_FFN = (0, FFN_IN + FFN_OUT + PROJ + MERGE + WOUT)
S_PROJ = FFN_IN + FFN_OUT
S_MERGE = S_PROJ + PROJ
S_WOUT = S_MERGE + MERGE
NS = 2 * (FFN_IN + FFN_OUT) + PROJ + MERGE + WOUT
RAW, PAIR = 4, 2
OUT_SLABS = (8, 8, 6)
MERGE_SLABS = (8, 8, 8, 8, 2)

V_PRE, V_POST = (0, 16, 32), (8, 24, 40)
V_KVN, V_CN, V_BA, V_BG = 48, 49, 50, 52
NV = V_BG + 24

(C_ID, C_ROT, C_ONE, C_CAU, C_G0, C_G1, C_G2, C_GLA) = (0, 128, 256, 384, 512, 768, 1280, 1792)
C_FREQ, C_EPS, C_EPS4, C_UNIT = 2304, 2305, 2306, 2307
NCST = 2308

ROPED = 25
NFM = 34
N_IN = KD + 4


def constants():
    c = np.zeros((P, NCST), np.float32)
    c[:, C_ID:C_ID + P] = np.eye(P)
    for base in (0, HD):
        for d in range(ROT // 2):
            c[base + d + ROT // 2, C_ROT + base + d] = -1.0
            c[base + d, C_ROT + base + d + ROT // 2] = 1.0
            f = np.float32(THETA) ** np.float32(-2.0 * d / ROT)
            c[base + d, C_FREQ] = f
            c[base + d + ROT // 2, C_FREQ] = f
    c[:, C_ONE:C_ONE + P] = 1.0
    q, k = np.arange(P)[:, None], np.arange(P)[None, :]
    causal = k <= q
    c[:, C_CAU:C_CAU + P] = np.where(causal, 0, NEG)
    c[:, C_G0:C_G0 + P] = np.where(k >= q, 0, NEG)
    c[:, C_G0 + P:C_G0 + 2 * P] = np.where(causal, 0, NEG)
    for col, dil in ((C_G1, 4), (C_G2, 16)):
        same = (q - k) % dil == 0
        for b in range(3):
            c[:, col + b * P:col + (b + 1) * P] = np.where(same, 0, NEG)
        c[:, col + 3 * P:col + 4 * P] = np.where(same & causal, 0, NEG)
    intra = (q <= k) & (q // CH == k // CH)
    c[:, C_GLA:C_GLA + 4 * P] = np.tile(intra, (1, 4))
    c[:, C_EPS], c[:, C_EPS4], c[:, C_UNIT] = EPS, 4 * EPS, 1.0
    return c


def proj_plan():
    steps = [("fm", 8, [("misc", 0)]), ("fm", 8, [("ckv", 0)])]
    steps += [("fm", 8, [("iq", t)]) for t in range(4)]
    steps += [("fm", 8, [("aq", t)]) for t in range(4)]
    steps += [("ka", 4, [("ak", t) for t in range(4)]), ("va", 4, [])]
    steps += [("fm", 8, [("bq", t)]) for t in range(6)]
    steps += [("fm", 8, [("bk", t)]) for t in range(6)]
    steps += [("tm", 8, [("vb", 0, 512, k)]) for k in range(4)]
    steps += [("tm", 4, [("vb", 512, 256, k)]) for k in range(4)]
    steps += [("fm", 8, [("cq", t)]) for t in range(2)]
    steps += [("fm", 8, [("ck", t)]) for t in range(2)]
    steps += [("fm", 8, [("cg", t)]) for t in range(4)]
    steps += [("tm", 8, [("vc", 0, 512, k)]) for k in range(4)]
    assert len(steps) == PROJ
    return steps


def attention_items(kind):
    items = []
    if kind == "a":
        for h in range(A_HEADS):
            for b in range(NB):
                items.append((h, b, [(h // 2, h // 2, h % 2, 0, b + 1, None, h * HD)]))
        return items
    for h in range(B_HEADS):
        for b in range(NB):
            segs = []
            for g in range(GROUPS):
                head = g * B_HEADS + h
                first = max(b - 1, 0) if g == 0 else 0
                n = b + 1 - first
                end = (C_G0 + 2 * P, C_G1 + 4 * P, C_G2 + 4 * P)[g]
                segs.append((head // 2, head // 2, head % 2, first, n, end - n * P, head * HD))
            items.append((h, b, segs))
    return items


def groups_of(segs):
    blocks, col = [], 0
    for (_, _, _, first, n, _, vcol) in segs:
        for j in range(n):
            blocks.append((col, first + j, vcol))
            col += P
    return [blocks[i:i + 4] for i in range(0, len(blocks), 4)]


ITEMS = {"a": attention_items("a"), "b": attention_items("b")}
ITEM0 = {"a": 0, "b": len(ITEMS["a"])}
NITEM = len(ITEMS["a"]) + len(ITEMS["b"])
NGRP = {k: sum(len(groups_of(s)) for _, _, s in ITEMS[k]) for k in "ab"}
GRP0 = {"a": 0, "b": NGRP["a"]}
NGRPS = NGRP["a"] + NGRP["b"]
HEAD0 = {"a": 0, "b": A_HEADS}
NHEAD = A_HEADS + B_HEADS
NIDX = NB * 8


class Lane:

    def __init__(self, eng, order, name, per):
        self.eng, self.order, self.name, self.per = eng, order, name, per
        self.turns, self.n, self.last = 0, 0, None

    def ready(self):
        if self.last is not None:
            self.eng.wait_ge(*self.last)

    def settle(self):
        self.ready()
        self.n += 1
        self.eng.sem_inc(self.order, 1)
        self.last = (self.order, self.turns + self.n)

    def did(self, ins, sem=None, value=None):
        if sem is None:
            sem, self.n = self.order, self.n + 1
            value = self.turns + self.n
        ins.then_inc(sem, 1)
        self.last = (sem, value)

    def fence(self):
        if self.last is None or self.last[0] is not self.order:
            self.settle()

    def loop(self, key, count):
        return _Loop(self, (self.name, key), count)


class _Loop:
    def __init__(self, lane, key, count):
        self.lane, self.key, self.count = lane, key, count

    def __enter__(self):
        lane = self.lane
        lane.fence()
        self.turns, self.n = lane.turns, lane.n
        self.cm = lane.eng.Fori(0, self.count)
        i = self.cm.__enter__()
        lane.turns = self.turns + i * lane.per.get(self.key, 0)
        lane.last = (lane.order, lane.turns + lane.n)
        return i

    def __exit__(self, *exc):
        lane = self.lane
        lane.fence()
        lane.per[self.key] = lane.n - self.n
        self.cm.__exit__(*exc)
        lane.turns, lane.n = self.turns, self.n + self.count * lane.per[self.key]
        lane.last = (lane.order, lane.turns + lane.n)


def trunk_kernel(nc, xT, positions, consts, vecs, walpha, w_in1, w_out1, w_proj, w_merge, w_wout,
                 w_in2, w_out2, outT, per):
    ctx = ExitStack()
    with ctx:
        def sb(name, shape, dt=F32, scope=ctx):
            return scope.enter_context(nc.sbuf_tensor(name, shape, dt))

        def sem(name):
            return ctx.enter_context(nc.semaphore(name))

        h = sb("h", [P, KD, SEQ])
        xhi = sb("xhi", [P, KD, SEQ], F32R)
        with ExitStack() as s:
            f = sb("f", [P, KD, SEQ], F32, s)
        xlo = sb("xlo", [P, KD, SEQ], F32R)
        wraw = sb("wraw", [P, RAW, 1024])
        whi = sb("whi", [P, PAIR, 1024], F32R)
        wlo = sb("wlo", [P, PAIR, 1024], F32R)
        cst = sb("cst", [P, NCST])
        cosT = sb("cosT", [P, SEQ])
        sinT = sb("sinT", [P, SEQ])
        vec2 = sb("vec2", [P, DEPTH, NV])
        vec = sb("vec", [P, NV])
        bgate = sb("bgate", [P, 12])
        wal2 = sb("wal2", [P, DEPTH, 256])
        wal = sb("wal", [P, 256])
        sq = sb("sq", [P, 2, SEQ])
        acc = sb("acc", [P, SEQ])
        std = sb("std", [P, SEQ])
        rstd = sb("rstd", [P, SEQ])
        xt = sb("xt", [P, 2, SEQ])

        with ExitStack() as s:
            hidhi = sb("hidhi", [P, KF, SEQ], F32R, s)
            hidlo = sb("hidlo", [P, KF, SEQ], F32R, s)
            silu = sb("silu", [P, 2, SEQ], F32, s)
            hf = sb("hf", [P, 1, SEQ], F32, s)
        with ExitStack() as s:
            gate = sb("gate", [P, 3, SEQ], F32, s)
        yf = sb("yf", [P, 10, SEQ])
        misc = sb("misc", [P, SEQ])
        with ExitStack() as s:
            iq = sb("iq", [P, 4, SEQ], F32, s)
            ik = sb("ik", [P, 1, SEQ], F32, s)
            aq = sb("aq", [P, 4, SEQ], F32, s)
            ak = sb("ak", [P, 4, SEQ], F32, s)
            va = sb("va", [P, NB, 512], F32, s)
            widx = sb("widx", [P, NB * 8], F32, s)
            relu = sb("relu", [P, 2, SEQ], F32, s)
            score = sb("score", [P, NB, SEQ], F32, s)
            top8 = sb("top8", [P, 8], F32, s)
            with ExitStack() as t:
                ckv = sb("ckv", [P, SEQ], F32, t)
                ckvhi = sb("ckvhi", [P, SEQ], F32R, t)
                ckvlo = sb("ckvlo", [P, SEQ], F32R, t)
                xr_a = sb("xr_a", [P, 2, SEQ], F32, t)
                rt_a = sb("rt_a", [P, SEQ], F32, t)
            prob_a = sb("prob_a", [P, 2, 512], F32, s)
            pt_a = sb("pt_a", [P, 2, 512], F32, s)
            st_a = sb("st_a", [P, 2, 16], F32, s)
        with ExitStack() as s:
            bq = sb("bq", [P, 6, SEQ], F32, s)
            bk = sb("bk", [P, 6, SEQ], F32, s)
            vb = sb("vb", [P, NB, 768], F32, s)
            xr_b = sb("xr_b", [P, 2, SEQ], F32, s)
            rt_b = sb("rt_b", [P, SEQ], F32, s)
            prob_b = sb("prob_b", [P, 2, 1280], F32, s)
            pt_b = sb("pt_b", [P, 2, 512], F32, s)
            st_b = sb("st_b", [P, 2, 16], F32, s)
        with ExitStack() as s:
            cq = sb("cq", [P, 2, SEQ], F32, s)
            ck = sb("ck", [P, 2, SEQ], F32, s)
            cg = sb("cg", [P, 4, SEQ], F32, s)
            vc = sb("vc", [P, NB, 512], F32, s)
            la = sb("la", [P, 2, SEQ], F32, s)
            lb = sb("lb", [P, 2, SEQ], F32, s)
            keep = sb("keep", [P, SEQ], F32, s)
            qdec = sb("qdec", [P, 2, SEQ], F32, s)
            kdec = sb("kdec", [P, 2, SEQ], F32, s)
            kend = sb("kend", [P, 2, SEQ], F32, s)
            dec = sb("dec", [P, 2, 8], F32, s)
            kendT = sb("kendT", [P, NB, 256], F32, s)
            attT = sb("attT", [P, NB, 2, 256], F32, s)
            state = sb("state", [P, 8, 2, P], F32, s)
        with ExitStack() as s:
            yhi = sb("yhi", [P, 10, SEQ], F32R, s)
            ylo = sb("ylo", [P, 10, SEQ], F32R, s)
            mghi = sb("mghi", [P, KD, SEQ], F32R, s)
            mglo = sb("mglo", [P, KD, SEQ], F32R, s)
        PS = ctx.enter_context(nc.psum_tensor("PS", [P, 8, 512], F32))

        ident = cst[:, C_ID:C_ID + P]
        onesm = cst[:, C_ONE:C_ONE + P]

        raw_loaded = [sem(f"raw_loaded{i}") for i in range(RAW)]
        w_hi = sem("w_hi")
        w_ready = sem("w_ready")
        step_done = sem("step_done")
        consts_in = sem("consts_in")
        order_v, order_s, order_p = sem("order_v"), sem("order_s"), sem("order_p")
        tables = sem("tables")
        tables_done = sem("tables_done")
        layer_vecs = sem("layer_vecs")
        h_new = sem("h_new")
        hsq = sem("hsq")
        hsq_added = sem("hsq_added")
        stat_mm = sem("stat_mm")
        std_ready = sem("std_ready")
        x_ready = sem("x_ready")
        x_f32, x_hi = sem("x_f32"), sem("x_hi")
        silu_ready = sem("silu_ready")
        ffn_read = sem("ffn_read")
        hid_ready = sem("hid_ready")
        fsq = sem("fsq")
        f_read = sem("f_read")
        fm_copied = sem("fm_copied")
        rot_mm = sem("rot_mm")
        roped = sem("roped")
        tm_copied = sem("tm_copied")
        ckv_f32, ckv_sum, ckv_std = sem("ckv_f32"), sem("ckv_sum"), sem("ckv_std")
        ckv_n, ckv_h, ckv_ready = sem("ckv_n"), sem("ckv_h"), sem("ckv_ready")
        widx_mm, widx_ready = sem("widx_mm"), sem("widx_ready")
        ik_copied = sem("ik_copied")
        idx_mm, idx_relu, idx_added = sem("idx_mm"), sem("idx_relu"), sem("idx_added")
        bias_ready = sem("bias_ready")
        score_mm = sem("score_mm")
        score_read = sem("score_read")
        exp_ready = sem("exp_ready")
        prob_ready = sem("prob_ready")
        turn_mm = sem("turn_mm")
        turned = sem("turned")
        head_mm = sem("head_mm")
        head_read = sem("head_read")
        alpha_mm, alpha_abs, alpha_log, alpha_min = (sem("alpha_mm"), sem("alpha_abs"),
                                                     sem("alpha_log"), sem("alpha_min"))
        decay_sum, decay_exp, decay_ready = sem("decay_sum"), sem("decay_exp"), sem("decay_ready")
        decay_e = sem("decay_e")
        kend_mm, kend_T = sem("kend_mm"), sem("kend_T")
        kv_mm, kv_read = sem("kv_mm"), sem("kv_read")
        att_mm, att_ready = sem("att_mm"), sem("att_ready")
        o_mm, o_sq, o_sum, o_std, o_done = (sem("o_mm"), sem("o_sq"), sem("o_sum"), sem("o_std"),
                                            sem("o_done"))
        y_hi, y_ready = sem("y_hi"), sem("y_ready")
        gate_bias = sem("gate_bias")
        gated = sem("gated")
        merged = sem("merged")
        out_done = sem("out_done")

        def at(li, per_layer, n):
            return li * per_layer + (n + 1)

        def past(li, per_layer, n):
            return li * per_layer + (n + 2)

        block = ctx.enter_context(nc.Block())

        @block.sync
        def _(sp):
            sp.dma_start(cst[:, :], consts).then_inc(consts_in, 16)
            sp.dma_start(acc[:, :].bitcast(I32),
                         positions.to_broadcast([P, SEQ])).then_inc(consts_in, 16)
            sp.dma_start(vec2[:, :, :], vecs).then_inc(consts_in, 16)
            sp.dma_start(wal2[96:112, :, :], walpha).then_inc(consts_in, 16)
            for k in range(KD):
                sp.dma_start(h[:, k, :], xT[k * P:(k + 1) * P, :]).then_inc(consts_in, 16)

            def load(li, s, src, i=0, per_iter=0):
                n = src.shape[-1]
                sp.wait_ge(w_ready, at(li, NS, s) + i * per_iter)
                sp.dma_start(wraw[:, s % RAW, 0:n], src).then_inc(raw_loaded[s % RAW], 16)

            def ffn(li, s0, w1, w2):
                with sp.Fori(0, FFN_IN // RAW) as i:
                    for c in range(RAW):
                        load(li, s0 + c, w1[li, i * RAW + c, :, :], i, RAW)
                with sp.Fori(0, 2) as i:
                    for m in range(4):
                        for c in range(3):
                            load(li, s0 + FFN_IN + 3 * m + c,
                                 w2[li, i * 4 + m, :, c * 1024:c * 1024 + OUT_SLABS[c] * P], i, 12)

            with sp.Fori(0, DEPTH) as li:
                ffn(li, S_FFN[0], w_in1, w_out1)
                for j, (_, slabs, _) in enumerate(proj_plan()):
                    load(li, S_PROJ + j, w_proj[li, j, :, 0:slabs * P])
                with sp.Fori(0, 2) as i:
                    for m in range(4):
                        for c in range(5):
                            load(li, S_MERGE + 5 * m + c,
                                 w_merge[li, i * 4 + m, :, c * 1024:c * 1024 + MERGE_SLABS[c] * P],
                                 i, 20)
                with sp.Fori(0, 2) as i:
                    for c in range(4):
                        load(li, S_WOUT + c, w_wout[li, i * 4 + c, :, :], i, 4)
                ffn(li, S_FFN[1], w_in2, w_out2)
            for c in range(PAIR):
                load(DEPTH, c, w_in1[0, c, :, :])
            for k in range(KD):
                sp.wait_ge(h_new, 8 * 3 * DEPTH + k + 1)
                sp.dma_start(outT[k * P:(k + 1) * P, :], h[:, k, :]).then_inc(out_done, 16)
            sp.wait_ge(out_done, 16 * KD)

        @block.gpsimd
        def _(pool):
            lane = Lane(pool, order_p, "pool", per)
            pool.sem_inc(w_ready, RAW)

            def split(li, s, slabs, i=0, per_iter=0):
                n = slabs * P
                pool.wait_ge(w_hi, at(li, NS, s) + i * per_iter)
                nc.gpsimd.tensor_tensor(wlo[:, s % PAIR, 0:n], wraw[:, s % RAW, 0:n],
                                        whi[:, s % PAIR, 0:n].bitcast(F32),
                                        ALU.subtract).then_inc(w_ready, 1)

            def ffn(li, s0):
                with pool.Fori(0, FFN_IN // RAW) as i:
                    for c in range(RAW):
                        split(li, s0 + c, 8, i, RAW)
                with pool.Fori(0, 2) as i:
                    for m in range(4):
                        for c in range(3):
                            split(li, s0 + FFN_IN + 3 * m + c, OUT_SLABS[c], i, 12)

            with pool.Fori(0, DEPTH) as li:
                ffn(li, S_FFN[0])
                for j, (_, slabs, _) in enumerate(proj_plan()):
                    split(li, S_PROJ + j, slabs)
                with pool.Fori(0, 2) as i:
                    for m in range(4):
                        for c in range(5):
                            split(li, S_MERGE + 5 * m + c, MERGE_SLABS[c], i, 20)
                with pool.Fori(0, 2) as i:
                    for c in range(4):
                        split(li, S_WOUT + c, 8, i, 4)
                ffn(li, S_FFN[1])
            for c in range(PAIR):
                split(DEPTH, c, 8)

        @block.scalar
        def _(act):
            lane = Lane(act, order_s, "act", per)
            did, ready = lane.did, lane.ready
            act.sem_inc(gated, 1)

            def hi(li, s, slabs, i=0, per_iter=0):
                n, slot = slabs * P, s % RAW
                loads = li * (NS // RAW) + i * (per_iter // RAW) + s // RAW
                act.wait_ge(raw_loaded[slot], (loads + 1) * 16)
                act.wait_ge(step_done, at(li, NS, s) + i * per_iter)
                ready()
                did(nc.scalar.activation(whi[:, s % PAIR, 0:n], wraw[:, slot, 0:n], ACT.Copy),
                    w_hi, at(li, NS, s) + i * per_iter)

            def wait_step(li, s, i=0, per_iter=0):
                act.wait_ge(step_done, at(li, NS, s) + i * per_iter + PAIR)

            def prenorm(li, p):
                for k in range(KD):
                    act.wait_ge(h_new, at(li, 24, 8 * p + k))
                    act.wait_ge(hsq_added, past(li, 24, 8 * p + max(k - 1, 0) - 1))
                    ready()
                    did(nc.scalar.activation(sq[:, k % 2, :], h[:, k, :], ACT.Square),
                        hsq, at(li, 24, 8 * p + k))
                spread(li, 2 * p, C_EPS, 1.0)
                for k in range(KD):
                    act.wait_ge(x_f32, at(li, 24, 8 * p + k))
                    ready()
                    did(nc.scalar.activation(xhi[:, k, :], xt[:, k % 2, :], ACT.Copy),
                        x_hi, at(li, 24, 8 * p + k))

            def spread(li, z, eps, scale):
                act.wait_ge(stat_mm, at(li, 6, z))
                ready()
                did(nc.scalar.activation(std[:, :], PS[:, 0, :], ACT.Sqrt,
                                         bias=cst[:, eps:eps + 1], scale=scale / DM),
                    std_ready, at(li, 6, z))

            def f_square(li, q, m, i, bank):
                act.wait_ge(f_read, at(li, 24, 8 * q + m) + i * 4 + 2)
                ready()
                did(nc.scalar.activation(sq[:, m % 2, :], PS[:, bank, :], ACT.Square),
                    fsq, at(li, 24, 8 * q + m) + i * 4)

            def ffn(li, fi, next_slabs):
                s0 = S_FFN[fi]
                with lane.loop(f"ffn_in{fi}", FFN_IN // 4) as i:
                    for c in range(4):
                        wait_step(li, s0 + c, i, 4)
                        hi(li, s0 + c + 2, 8, i, 4)
                        if c % 2 == 0:
                            act.wait_ge(hid_ready, past(li, 2 * KF, fi * KF + c // 2 - 1) + i * 2)
                            ready()
                            did(nc.scalar.activation(silu[:, c // 2, :], PS[:, c, :], ACT.Silu),
                                silu_ready, at(li, 2 * KF, fi * KF + c // 2) + i * 2)
                with lane.loop(f"ffn_out{fi}", 2) as i:
                    for m in range(4):
                        for c in range(3):
                            n = 3 * m + c
                            wait_step(li, s0 + FFN_IN + n, i, 12)
                            hi(li, s0 + FFN_IN + n + 2, OUT_SLABS[(n + 2) % 3], i, 12)
                        f_square(li, 2 * fi, m, i, 4 + m)
                spread(li, 4 * fi + 1, C_EPS4, 4.0)

            plan = proj_plan()

            def roll(li, j):
                wait_step(li, S_PROJ + j)
                hi(li, S_PROJ + j + 2, plan[j + 2][1] if j + 2 < PROJ else 8)

            class Fm:
                tile = 0
                rope = 0

            def copy_fm(li, kind, t, bank, xr):
                c = Fm.tile
                Fm.tile += 1
                ready()
                if kind in ("iq", "aq", "ak", "bq", "bk"):
                    r = Fm.rope
                    Fm.rope += 1
                    act.wait_ge(roped, at(li, ROPED, r))
                    ins = nc.scalar.activation(xr[:, r % 2, :], PS[:, bank, :], ACT.Copy)
                elif kind == "misc":
                    Fm.rope += 1
                    ins = nc.scalar.activation(misc[:, :], PS[:, bank, :], ACT.Copy)
                elif kind == "ckv":
                    ins = nc.scalar.activation(ckv[:, :], PS[:, bank, :], ACT.Copy)
                elif kind == "cq":
                    ins = nc.scalar.activation(cq[:, t, :], PS[:, bank, :], ACT.Copy, scale=HD ** -0.5)
                elif kind == "ck":
                    ins = nc.scalar.activation(ck[:, t, :], PS[:, bank, :], ACT.Copy)
                else:
                    ins = nc.scalar.activation(cg[:, t, :], PS[:, bank, :], ACT.Silu)
                did(ins, fm_copied, at(li, NFM, c))

            def copy_tm(li, g, dest, col, n):
                for b in range(NB):
                    ready()
                    did(nc.scalar.activation(dest[:, b, col:col + n], PS[:, b, 0:n], ACT.Copy),
                        tm_copied, at(li, 16, 4 * g + b))

            def attention(li, kind, prob, pt, st):
                items, i0, g0 = ITEMS[kind], ITEM0[kind], GRP0[kind]

                def exponentials(n):
                    col = 0
                    act.wait_ge(score_read, at(li, NITEM, i0 + n))
                    for g, seg in enumerate(items[n][2]):
                        w = seg[4] * P
                        ready()
                        ins = nc.scalar.activation(prob[:, n % 2, col:col + w],
                                                   prob[:, n % 2, col:col + w], ACT.Exp,
                                                   bias=st[:, n % 2, 3:4], scale=-1.0,
                                                   accum_out=st[:, n % 2, 4 + g:5 + g])
                        if g == len(items[n][2]) - 1:
                            did(ins, exp_ready, at(li, NITEM, i0 + n))
                        else:
                            did(ins)
                        col += w

                grp = g0
                exponentials(0)
                for n in range(len(items)):
                    if n + 1 < len(items):
                        exponentials(n + 1)
                    for blocks in groups_of(items[n][2]):
                        w = len(blocks) * P
                        act.wait_ge(turn_mm, at(li, NGRPS, grp))
                        ready()
                        did(nc.scalar.activation(pt[:, grp % 2, 0:w], PS[:, 3 + grp % 2, 0:w],
                                                 ACT.Copy), turned, at(li, NGRPS, grp))
                        grp += 1

            act.wait_ge(tables, 1)
            did(nc.scalar.activation(sinT[:, :], xt[:, 0, :], ACT.Sin), tables_done, 1)
            ready()
            did(nc.scalar.activation(cosT[:, :], xt[:, 1, :], ACT.Sin), tables_done, 2)
            hi(0, 0, 8)
            hi(0, 1, 8)
            with lane.loop("layer", DEPTH) as li:
                prenorm(li, 0)
                ffn(li, 0, 8)
                prenorm(li, 1)
                Fm.tile = Fm.rope = 0
                for j in range(10):
                    kind, t = plan[j][2][0]
                    roll(li, j)
                    copy_fm(li, kind, t, 5 + j % 3, xr_a)
                    if kind == "ckv":
                        ready()
                        did(nc.scalar.activation(sq[:, 0, :], ckv[:, :], ACT.Square), ckv_f32,
                            at(li, 1, 0))
                    if j == 3:
                        act.wait_ge(roped, at(li, ROPED, 0) + 2)
                        act.dma_start(ik[HD:P, 0, :], ik[0:HD, 0, :]).then_inc(ik_copied, 16)
                    if j == 4:
                        act.wait_ge(ckv_sum, at(li, 1, 0))
                        ready()
                        did(nc.scalar.activation(std[:, :], PS[:, 0, :], ACT.Sqrt,
                                                 bias=cst[:, C_EPS:C_EPS + 1], scale=1.0 / P),
                            ckv_std, at(li, 1, 0))
                    if j == 6:
                        act.wait_ge(ckv_n, at(li, 1, 0))
                        ready()
                        did(nc.scalar.activation(ckvhi[:, :], ckv[:, :], ACT.Copy), ckv_h,
                            at(li, 1, 0))
                roll(li, 10)
                for t in range(4):
                    copy_fm(li, "ak", t, t, xr_a)
                roll(li, 11)
                copy_tm(li, 0, va, 0, 512)
                for n in range(NIDX):
                    w = (n // 8 + 1) * P
                    act.wait_ge(idx_mm, at(li, NIDX, n))
                    if n >= 2:
                        act.wait_ge(idx_added, at(li, NIDX, n - 2))
                    ready()
                    did(nc.scalar.activation(relu[:, n % 2, 0:w], PS[:, n % 3, 0:w], ACT.Relu,
                                             scale=HD ** -0.5), idx_relu, at(li, NIDX, n))
                attention(li, "a", prob_a, pt_a, st_a)
                for j in range(12, 32):
                    roll(li, j)
                    if j < 24:
                        kind, t = plan[j][2][0]
                        if j == 12:
                            act.wait_ge(head_read, at(li, NHEAD, A_HEADS - 1))
                        copy_fm(li, kind, t, 5 + j % 3, xr_b)
                    elif j == 27:
                        copy_tm(li, 1, vb, 0, 512)
                    elif j == 31:
                        copy_tm(li, 2, vb, 512, 256)
                attention(li, "b", prob_b, pt_b, st_b)
                for j in range(32, PROJ):
                    roll(li, j)
                    if j < 40:
                        kind, t = plan[j][2][0]
                        if j == 32:
                            act.wait_ge(head_read, at(li, NHEAD, NHEAD - 1))
                        copy_fm(li, kind, t, 5 + j % 3, None)
                    elif j == 43:
                        copy_tm(li, 3, vc, 0, 512)
                act.wait_ge(alpha_mm, at(li, 1, 0))
                for t in range(2):
                    ready()
                    did(nc.scalar.activation(la[:, t, :], PS[:, 6 + t, :], ACT.Abs,
                                             bias=vec[:, V_BA + t:V_BA + t + 1]),
                        alpha_abs, at(li, 2, t))
                for t in range(2):
                    ready()
                    did(nc.scalar.activation(la[:, t, :], la[:, t, :], ACT.Exp, scale=-1.0))
                for t in range(2):
                    ready()
                    did(nc.scalar.activation(la[:, t, :], la[:, t, :], ACT.Ln,
                                             bias=cst[:, C_UNIT:C_UNIT + 1]),
                        alpha_log, at(li, 2, t))
                act.wait_ge(decay_sum, at(li, 2, 1))
                for t in range(2):
                    ready()
                    did(nc.scalar.activation(qdec[:, t, :], lb[:, t, :], ACT.Exp, scale=1 / TAU))
                    ready()
                    did(nc.scalar.activation(kdec[:, t, :], lb[:, t, :], ACT.Exp, scale=-1 / TAU))
                    ready()
                    did(nc.scalar.activation(kend[:, t, :], kend[:, t, :], ACT.Exp, scale=-1 / TAU))
                    ready()
                    did(nc.scalar.activation(
                        dec[:, t, :], lb[:, t, :].rearrange("p (n c) -> p n c", c=CH)[:, :, CH - 1],
                        ACT.Exp, scale=1 / TAU), decay_exp, at(li, 2, t))
                for b in range(NB):
                    act.wait_ge(kend_mm, at(li, NB, b))
                    ready()
                    did(nc.scalar.activation(kendT[:, b, :], PS[:, 6 + b % 2, 0:256], ACT.Copy),
                        kend_T, at(li, NB, b))
                for hh in range(C_HEADS):
                    act.wait_ge(o_mm, at(li, 1, 0))
                    if hh >= 2:
                        act.wait_ge(o_sum, at(li, C_HEADS, hh - 2))
                    ready()
                    did(nc.scalar.activation(sq[:, hh % 2, :], PS[:, hh, :], ACT.Square),
                        o_sq, at(li, C_HEADS, hh))
                for hh in range(C_HEADS):
                    act.wait_ge(o_sum, at(li, C_HEADS, hh))
                    if hh >= 1:
                        act.wait_ge(o_done, at(li, C_HEADS, hh - 1))
                    ready()
                    did(nc.scalar.activation(std[:, :], PS[:, 4 + hh, :], ACT.Sqrt,
                                             bias=cst[:, C_EPS:C_EPS + 1], scale=1.0 / P),
                        o_std, at(li, C_HEADS, hh))
                act.wait_ge(o_done, at(li, C_HEADS, 3))
                for t in range(10):
                    ready()
                    did(nc.scalar.activation(yhi[:, t, :], yf[:, t, :], ACT.Copy), y_hi,
                        at(li, 10, t))
                with lane.loop("merge", 2) as i:
                    act.wait_ge(gate_bias, at(li, 2, 0) + i)
                    for m in range(4):
                        for c in range(5):
                            n = 5 * m + c
                            wait_step(li, S_MERGE + n, i, 20)
                            hi(li, S_MERGE + n + 2, MERGE_SLABS[(n + 2) % 5], i, 20)
                            if c < 3:
                                act.wait_ge(merged, past(li, KD, m - 1) + i * 4)
                                ready()
                                did(nc.scalar.activation(
                                    gate[:, c, :], PS[:, c, :], ACT.Sigmoid,
                                    bias=bgate[:, 3 * m + c:3 * m + c + 1]),
                                    gated, past(li, 24, 3 * m + c) + i * 12)
                with lane.loop("wout", 2) as i:
                    for m in range(4):
                        wait_step(li, S_WOUT + m, i, 4)
                        hi(li, S_WOUT + m + 2, 8, i, 4)
                        f_square(li, 1, m, i, 4 + m)
                spread(li, 3, C_EPS, 1.0)
                prenorm(li, 2)
                ffn(li, 1, 8)

        @block.tensor
        def _(pe):
            pe.sem_inc(step_done, PAIR)
            pe.wait_ge(consts_in, 16 * N_IN)
            plan = proj_plan()

            def mm3(out, ahi, alo, bhi, blo, start, stop):
                nc.tensor.matmul(out, ahi, blo, start=start, stop=False)
                nc.tensor.matmul(out, alo, bhi, start=False, stop=False)
                return nc.tensor.matmul(out, ahi, bhi, start=False, stop=stop)

            def want(li, s, i=0, per_iter=0):
                pe.wait_ge(w_ready, at(li, NS, s) + i * per_iter + RAW)

            def slab(s, k):
                return whi[:, s % PAIR, k * P:(k + 1) * P], wlo[:, s % PAIR, k * P:(k + 1) * P]

            def column(s, bank, slabs, khi, klo, k0=0, first=True, last=True, w0=0):
                for k in range(slabs):
                    a, b = slab(s, w0 + k)
                    ins = mm3(PS[:, bank, :], a, b, khi[:, k0 + k, :], klo[:, k0 + k, :],
                              first and k == 0, last and k == slabs - 1)
                return ins

            def sum_rows(bank, src):
                return nc.tensor.matmul(PS[:, bank, :], onesm, src, start=True, stop=True)

            def prenorm(li, p):
                pe.wait_ge(hsq_added, past(li, 24, 8 * p + 7))
                sum_rows(0, acc[:, :]).then_inc(stat_mm, 1)

            def postnorm(li, q):
                pe.wait_ge(f_read, at(li, 24, 8 * q + 7) + 4)
                sum_rows(0, acc[:, :]).then_inc(stat_mm, 1)

            def ffn(li, fi):
                s0 = S_FFN[fi]
                with pe.Fori(0, FFN_IN // 4) as i:
                    for c in range(4):
                        if c == 0:
                            pe.wait_ge(x_ready, at(li, 24, 16 * fi + 7))
                        want(li, s0 + c, i, 4)
                        if c % 2 == 0:
                            pe.wait_ge(ffn_read, at(li, 2 * KF, fi * KF + c // 2) + i * 2)
                        column(s0 + c, c, 8, xhi, xlo).then_inc(step_done, 1)
                with pe.Fori(0, 2) as i:
                    for m in range(4):
                        pe.wait_ge(f_read, at(li, 24, 16 * fi + m) + i * 4)
                        for c in range(3):
                            s = s0 + FFN_IN + 3 * m + c
                            want(li, s, i, 12)
                            pe.wait_ge(hid_ready, past(li, 2 * KF, fi * KF + 8 * c + OUT_SLABS[c] - 1))
                            column(s, 4 + m, OUT_SLABS[c], hidhi, hidlo, 8 * c, c == 0,
                                   c == 2).then_inc(step_done, 1)
                postnorm(li, 2 * fi)

            with pe.Fori(0, DEPTH) as li:
                pe.wait_ge(layer_vecs, li + 1)
                prenorm(li, 0)
                ffn(li, 0)
                prenorm(li, 1)
                pe.wait_ge(x_ready, at(li, 24, 15))
                bank_user = {}
                tile, rope, pending = 0, 0, []

                def rotate():
                    c, r, src = pending.pop(0)
                    pe.wait_ge(fm_copied, at(li, NFM, c))
                    pe.wait_ge(roped, at(li, ROPED, r) + 1)
                    nc.tensor.matmul(PS[:, 4, :], cst[:, C_ROT:C_ROT + P], src, start=True,
                                     stop=True).then_inc(rot_mm, 1)

                def fm_step(j, xr):
                    nonlocal tile, rope
                    kind, t = plan[j][2][0]
                    bank = 5 + j % 3
                    want(li, S_PROJ + j)
                    if bank in bank_user:
                        pe.wait_ge(fm_copied, at(li, NFM, bank_user[bank]))
                    column(S_PROJ + j, bank, 8, xhi, xlo).then_inc(step_done, 1)
                    while pending:
                        rotate()
                    bank_user[bank] = tile
                    if kind in ("iq", "aq", "bq", "bk"):
                        pending.append((tile, rope, xr[:, rope % 2, :]))
                        rope += 1
                    elif kind == "misc":
                        pending.append((tile, rope, misc[:, :]))
                        rope += 1
                    tile += 1

                def tm_step(j, n, k2):
                    s = S_PROJ + j
                    want(li, s)
                    for b in range(NB):
                        for kk in range(2):
                            k = 2 * k2 + kk
                            w = slice(kk * n, (kk + 1) * n)
                            ins = mm3(PS[:, b, 0:n], xhi[:, k, b * P:(b + 1) * P],
                                      xlo[:, k, b * P:(b + 1) * P], whi[:, s % PAIR, w],
                                      wlo[:, s % PAIR, w], k == 0, k == KD - 1)
                    ins.then_inc(step_done, 1)

                def attention(kind, q, kk, v, prob, pt):
                    items, i0, g0 = ITEMS[kind], ITEM0[kind], GRP0[kind]
                    grp, before = g0, None

                    def banks(n):
                        return [n % 3] if kind == "a" else [0, 1, 2]

                    def scores(n):
                        back = 3 if kind == "a" else 1
                        if n >= back:
                            pe.wait_ge(score_read, at(li, NITEM, i0 + n - back))
                        _, b, segs = items[n]
                        for bank, (qt, kt, half, first, nblk, _, _) in zip(banks(n), segs):
                            r = slice(half * HD, half * HD + HD)
                            ins = nc.tensor.matmul(
                                PS[:, bank, 0:nblk * P], q[r, qt, b * P:(b + 1) * P],
                                kk[r, kt, first * P:(first + nblk) * P], start=True, stop=True)
                        ins.then_inc(score_mm, 1)

                    def weigh(state):
                        hd, b, g, blocks, first, last = state
                        pe.wait_ge(turned, at(li, NGRPS, g))
                        half, bank = hd % 2, 5 + hd % 2
                        if first and b == 0 and hd >= 2:
                            pe.wait_ge(head_read, at(li, NHEAD, HEAD0[kind] + hd - 2))
                        for x, (_, kb, vcol) in enumerate(blocks):
                            ins = nc.tensor.matmul(
                                PS[half * HD:half * HD + HD, bank, b * P:(b + 1) * P],
                                v[:, kb, vcol:vcol + HD], pt[:, g % 2, x * P:(x + 1) * P],
                                start=first and x == 0, stop=last and x == len(blocks) - 1)
                        if last and b == NB - 1:
                            ins.then_inc(head_mm, 1)

                    scores(0)
                    for n, (hd, b, segs) in enumerate(items):
                        if n + 1 < len(items):
                            scores(n + 1)
                        pe.wait_ge(prob_ready, at(li, NITEM, i0 + n))
                        gs = groups_of(segs)
                        for x, blocks in enumerate(gs):
                            if grp - g0 >= 2:
                                pe.wait_ge(turned, at(li, NGRPS, grp - 2))
                            for y, (col, _, _) in enumerate(blocks):
                                ins = nc.tensor.matmul(
                                    PS[:, 3 + grp % 2, y * P:(y + 1) * P],
                                    prob[:, n % 2, col:col + P], ident, start=True, stop=True,
                                    is_transpose=True)
                            ins.then_inc(turn_mm, 1)
                            if before is not None:
                                weigh(before)
                            before = (hd, b, grp, blocks, x == 0, x == len(gs) - 1)
                            grp += 1
                    weigh(before)

                for j in range(10):
                    fm_step(j, xr_a)
                    if j == 2:
                        pe.wait_ge(ckv_f32, at(li, 1, 0))
                        sum_rows(0, sq[:, 0, :]).then_inc(ckv_sum, 1)
                    if j == 3:
                        for b in range(NB):
                            ins = nc.tensor.matmul(PS[:, 1, b * 8:(b + 1) * 8],
                                                   misc[64:72, b * P:(b + 1) * P],
                                                   cst[64:72, C_ID + 64:C_ID + 72],
                                                   start=True, stop=True)
                        ins.then_inc(widx_mm, 1)
                while pending:
                    rotate()
                s = S_PROJ + 10
                want(li, s)
                pe.wait_ge(ckv_ready, at(li, 1, 0))
                pe.wait_ge(widx_ready, at(li, 1, 0))
                for t in range(4):
                    a, b = slab(s, t)
                    ins = mm3(PS[:, t, :], a, b, ckvhi[:, :], ckvlo[:, :], True, True)
                ins.then_inc(step_done, 1)
                for t in range(4):
                    pending.append((tile, rope, xr_a[:, rope % 2, :]))
                    rotate()
                    tile, rope = tile + 1, rope + 1
                s = S_PROJ + 11
                want(li, s)
                for b in range(NB):
                    ins = mm3(PS[:, b, :], ckvhi[:, b * P:(b + 1) * P], ckvlo[:, b * P:(b + 1) * P],
                              whi[:, s % PAIR, 0:512], wlo[:, s % PAIR, 0:512], True, True)
                ins.then_inc(step_done, 1)
                pe.wait_ge(tm_copied, at(li, 16, 3))
                pe.wait_ge(roped, at(li, ROPED, 12) + 2)
                pe.wait_ge(ik_copied, (li + 1) * 16)
                for n in range(NIDX):
                    b, hd = n // 8, n % 8
                    r = slice((hd % 2) * HD, (hd % 2) * HD + HD)
                    if n >= 3:
                        pe.wait_ge(idx_relu, at(li, NIDX, n - 3))
                    nc.tensor.matmul(PS[:, n % 3, 0:(b + 1) * P], iq[r, hd // 2, b * P:(b + 1) * P],
                                     ik[r, 0, 0:(b + 1) * P], start=True,
                                     stop=True).then_inc(idx_mm, 1)
                pe.wait_ge(idx_relu, at(li, NIDX, NIDX - 1))
                attention("a", aq, ak, va, prob_a, pt_a)
                pe.wait_ge(head_read, at(li, NHEAD, A_HEADS - 1))
                for j in range(12, 24):
                    fm_step(j, xr_b)
                while pending:
                    rotate()
                pe.wait_ge(score_read, at(li, NITEM, ITEM0["b"] - 1))
                pe.wait_ge(turned, at(li, NGRPS, GRP0["b"] - 1))
                for j in range(24, 28):
                    tm_step(j, 512, j - 24)
                pe.wait_ge(tm_copied, at(li, 16, 7))
                for j in range(28, 32):
                    tm_step(j, 256, j - 28)
                pe.wait_ge(tm_copied, at(li, 16, 11))
                pe.wait_ge(roped, at(li, ROPED, ROPED - 1) + 2)
                pe.wait_ge(fm_copied, at(li, NFM, tile - 1))
                attention("b", bq, bk, vb, prob_b, pt_b)
                pe.wait_ge(head_read, at(li, NHEAD, NHEAD - 1))
                bank_user.clear()
                for j in range(32, 40):
                    fm_step(j, None)
                pe.wait_ge(score_read, at(li, NITEM, NITEM - 1))
                for j in range(40, 44):
                    tm_step(j, 512, j - 40)
                pe.wait_ge(fm_copied, at(li, NFM, NFM - 1))
                for t in range(2):
                    ins = nc.tensor.matmul(PS[:, 6 + t, :], wal[96:112, t * P:(t + 1) * P],
                                           misc[96:112, :], start=True, stop=True)
                ins.then_inc(alpha_mm, 1)
                pe.wait_ge(decay_ready, at(li, 2, 1))
                pe.wait_ge(tm_copied, at(li, 16, 15))
                for b in range(NB):
                    if b >= 2:
                        pe.wait_ge(kend_T, at(li, NB, b - 2))
                    for t in range(2):
                        ins = nc.tensor.matmul(PS[:, 6 + b % 2, t * P:(t + 1) * P],
                                               kend[:, t, b * P:(b + 1) * P], ident, start=True,
                                               stop=True, is_transpose=True)
                    ins.then_inc(kend_mm, 1)
                pe.wait_ge(kend_T, at(li, NB, NB - 1))

                def key_value(n):
                    r = slice((n % 2) * CH, (n % 2) * CH + CH)
                    if n >= 2:
                        pe.wait_ge(kv_read, at(li, 7, n - 2))
                    for pr in range(2):
                        ins = nc.tensor.matmul(PS[:, 6 + n % 2, pr * 256:(pr + 1) * 256],
                                               kendT[r, n // 2, pr * P:(pr + 1) * P],
                                               vc[r, n // 2, pr * 256:(pr + 1) * 256],
                                               start=True, stop=True)
                    ins.then_inc(kv_mm, 1)

                for b in range(NB):
                    for n in (2 * b, 2 * b + 1):
                        if n < 7:
                            key_value(n)
                    if b >= 1:
                        pe.wait_ge(att_ready, at(li, NB, b - 1))
                    for hd in range(C_HEADS):
                        r = slice((hd % 2) * HD, (hd % 2) * HD + HD)
                        t = slice(b * P, (b + 1) * P)
                        ins = nc.tensor.matmul(PS[:, 4 + hd % 2, (hd // 2) * P:(hd // 2 + 1) * P],
                                               kdec[r, hd // 2, t], qdec[r, hd // 2, t],
                                               start=True, stop=True)
                    ins.then_inc(att_mm, 1)
                for b in range(NB):
                    pe.wait_ge(att_ready, at(li, NB, b))
                    if b == 0:
                        pe.wait_ge(kv_read, at(li, 7, 6))
                    for hd in range(C_HEADS):
                        r = slice((hd % 2) * HD, (hd % 2) * HD + HD)
                        ins = nc.tensor.matmul(PS[:, hd, b * P:(b + 1) * P],
                                               vc[:, b, hd * P:(hd + 1) * P],
                                               attT[:, b, hd % 2, (hd // 2) * P:
                                                    (hd // 2 + 1) * P],
                                               start=True, stop=False, skip_group_check=True)
                        for n in (2 * b, 2 * b + 1):
                            if n == 0:
                                continue
                            ins = nc.tensor.matmul(PS[:, hd, n * CH:(n + 1) * CH],
                                                   state[r, n, hd // 2, :],
                                                   qdec[r, hd // 2, n * CH:(n + 1) * CH],
                                                   start=False, stop=n % 2 == 1,
                                                   skip_group_check=True)
                ins.then_inc(o_mm, 1)
                for hd in range(C_HEADS):
                    pe.wait_ge(o_sq, at(li, C_HEADS, hd))
                    sum_rows(4 + hd, sq[:, hd % 2, :]).then_inc(o_sum, 1)
                with pe.Fori(0, 2) as i:
                    for m in range(4):
                        pe.wait_ge(y_ready, at(li, 10, 9))
                        s = S_MERGE + 5 * m
                        for c in range(3):
                            want(li, s + c, i, 20)
                            pe.wait_ge(gated, past(li, 24, 3 * m + max(c - 2, 0) - 1) + i * 12)
                            column(s + c, c, 8, xhi, xlo).then_inc(step_done, 1)
                        pe.wait_ge(merged, past(li, KD, m - 1) + i * 4)
                        want(li, s + 3, i, 20)
                        column(s + 3, 3, 4, yhi, ylo, 0)
                        column(s + 3, 5, 4, yhi, ylo, 6, w0=4).then_inc(step_done, 1)
                        want(li, s + 4, i, 20)
                        column(s + 4, 4, 2, yhi, ylo, 4).then_inc(step_done, 1)
                with pe.Fori(0, 2) as i:
                    for m in range(4):
                        pe.wait_ge(merged, past(li, KD, KD - 1))
                        s = S_WOUT + m
                        pe.wait_ge(f_read, at(li, 24, 8 + m) + i * 4)
                        want(li, s, i, 4)
                        column(s, 4 + m, 8, mghi, mglo).then_inc(step_done, 1)
                postnorm(li, 1)
                prenorm(li, 2)
                ffn(li, 1)

        @block.vector
        def _(dve):
            lane = Lane(dve, order_v, "dve", per)
            did, ready = lane.did, lane.ready
            TT, TS, STT = (nc.vector.tensor_tensor, nc.vector.tensor_scalar,
                           nc.vector.scalar_tensor_tensor)
            dve.sem_inc(hsq_added, 1)
            dve.sem_inc(hid_ready, 1)
            dve.sem_inc(merged, 1)
            dve.sem_inc(ffn_read, 2)
            dve.sem_inc(f_read, 4)
            dve.sem_inc(roped, 2)
            dve.wait_ge(consts_in, 16 * N_IN)

            def wait_step(li, s, i=0, per_iter=0):
                dve.wait_ge(step_done, at(li, NS, s) + i * per_iter + PAIR)

            ang, turns = sq[:, 0, :], sq[:, 1, :]
            TWO_PI = 2 * np.pi
            C1 = 6.28125
            C2 = float(np.float32(round((TWO_PI - C1) * 2 ** 20) / 2 ** 20))
            C3 = TWO_PI - C1 - C2
            MAGIC = 1.5 * 2.0 ** 23
            did(nc.vector.tensor_copy(ang, acc[:, :].bitcast(I32)))
            ready()
            did(TS(ang, ang, cst[:, C_FREQ:C_FREQ + 1], None, ALU.mult))
            ready()
            did(TS(turns, ang, 1 / TWO_PI, MAGIC, ALU.mult, ALU.add))
            ready()
            did(TS(turns, turns, -MAGIC, None, ALU.add))
            for part in (C1, C2, C3):
                ready()
                did(STT(out=ang, in0=turns, scalar=-part, in1=ang, op0=ALU.mult, op1=ALU.add))
            LIM = 3.1415925
            ready()
            did(TS(xt[:, 0, :], ang, LIM, -LIM, ALU.min, ALU.max))
            ready()
            did(TS(ang, ang, np.pi / 2, None, ALU.add))
            ready()
            did(TS(turns, ang, np.pi, -TWO_PI, ALU.is_gt, ALU.mult))
            ready()
            did(TT(ang, ang, turns, ALU.add))
            ready()
            did(TS(xt[:, 1, :], ang, LIM, -LIM, ALU.min, ALU.max), tables, 1)
            dve.wait_ge(tables_done, 2)
            dve.sem_inc(h_new, 8)

            def prenorm(li, p):
                ready()
                did(nc.vector.memset(acc[:, :], 0.0))
                for k in range(KD):
                    dve.wait_ge(hsq, at(li, 24, 8 * p + k))
                    ready()
                    did(TT(acc[:, :], acc[:, :], sq[:, k % 2, :], ALU.add),
                        hsq_added, past(li, 24, 8 * p + k))
                inverse(li, 2 * p)
                g = V_PRE[p]

                def scaled(k):
                    ready()
                    did(STT(out=xt[:, k % 2, :], in0=h[:, k, :], scalar=vec[:, g + k:g + k + 1],
                            in1=rstd[:, :], op0=ALU.mult, op1=ALU.mult),
                        x_f32, at(li, 24, 8 * p + k))

                scaled(0)
                for k in range(KD):
                    if k + 1 < KD:
                        scaled(k + 1)
                    dve.wait_ge(x_hi, at(li, 24, 8 * p + k))
                    ready()
                    did(TT(xlo[:, k, :], xt[:, k % 2, :], xhi[:, k, :].bitcast(F32), ALU.subtract),
                        x_ready, at(li, 24, 8 * p + k))

            def inverse(li, z):
                dve.wait_ge(std_ready, at(li, 6, z))
                ready()
                did(nc.vector.reciprocal(rstd[:, :], std[:, :]))

            def f_tile(li, q, m, i, bank, s, s_iter):
                dve.wait_ge(fsq, at(li, 24, 8 * q + m) + i * 4)
                ready()
                did(TT(acc[:, :], acc[:, :], sq[:, m % 2, :], ALU.add))
                ready()
                did(TS(f[:, bass.ds(i * 4 + m, 1), :], PS[:, bank:bank + 1, :], 1.0, None, ALU.mult),
                    f_read, at(li, 24, 8 * q + m) + i * 4 + 4)

            def postnorm(li, q):
                inverse(li, 2 * q + 1)
                g = V_POST[q]
                for k in range(KD):
                    ready()
                    did(STT(out=f[:, k, :], in0=f[:, k, :], scalar=vec[:, g + k:g + k + 1],
                            in1=rstd[:, :], op0=ALU.mult, op1=ALU.mult))
                    ready()
                    did(TT(h[:, k, :], h[:, k, :], f[:, k, :], ALU.add),
                        h_new, at(li, 24, 8 * (q + 1) + k))

            def ffn(li, fi):
                s0 = S_FFN[fi]
                with lane.loop(f"ffn_in{fi}", FFN_IN // 4) as i:
                    for c in range(2):
                        t = fi * KF + c
                        wait_step(li, s0 + 2 * c + 1, i, 4)
                        dve.wait_ge(silu_ready, at(li, 2 * KF, t) + i * 2)
                        ready()
                        did(TT(hf[:, 0, :], silu[:, c, :], PS[:, 2 * c + 1, :], ALU.mult),
                            ffn_read, at(li, 2 * KF, t) + i * 2 + 2)
                        j = i * 2 + c
                        ready()
                        did(TS(hidhi[:, bass.ds(j, 1), :], hf[:, :, :], 1.0, None, ALU.mult))
                        ready()
                        did(TT(hidlo[:, bass.ds(j, 1), :], hf[:, :, :],
                               hidhi[:, bass.ds(j, 1), :].bitcast(F32), ALU.subtract),
                            hid_ready, past(li, 2 * KF, t) + i * 2)
                ready()
                did(nc.vector.memset(acc[:, :], 0.0))
                with lane.loop(f"ffn_out{fi}", 2) as i:
                    for m in range(4):
                        f_tile(li, 2 * fi, m, i, 4 + m, s0 + FFN_IN + 3 * m + 2, 12)
                postnorm(li, 2 * fi)

            rope_n = [0]

            def rope(li, c, dest, src, bank, rt, rows=P):
                r = rope_n[0]
                rope_n[0] += 1
                dve.wait_ge(fm_copied, at(li, NFM, c))
                ready()
                did(TT(dest, src, cosT[0:rows, :], ALU.mult))
                dve.wait_ge(rot_mm, at(li, ROPED, r))
                ready()
                did(TT(rt[0:rows, :], PS[0:rows, bank, :], sinT[0:rows, :], ALU.mult))
                ready()
                did(TT(dest, dest, rt[0:rows, :], ALU.add), roped, at(li, ROPED, r) + 2)

            def attention(li, kind, prob, st, y0):
                items, i0 = ITEMS[kind], ITEM0[kind]
                grp_end = []
                grp = GRP0[kind]
                for _, _, segs in items:
                    grp += len(groups_of(segs))
                    grp_end.append(grp - 1)

                def masked(n):
                    hd, b, segs = items[n]
                    dve.wait_ge(score_mm, at(li, NITEM, i0 + n))
                    if n >= 2:
                        dve.wait_ge(turn_mm, at(li, NGRPS, grp_end[n - 2]))
                    col = 0
                    for g, (_, _, _, first, nblk, mask, _) in enumerate(segs):
                        w = nblk * P
                        bank = n % 3 if kind == "a" else g
                        m = score[:, b, 0:w] if mask is None else cst[:, mask:mask + w]
                        lane.settle()
                        one = len(segs) == 1
                        ins = nc.vector.tensor_tensor_reduce(
                            out=prob[:, n % 2, col:col + w], in0=PS[:, bank, 0:w], in1=m,
                            scale=-(HD ** -0.5), scalar=3.0e38, op0=ALU.add, op1=ALU.min,
                            accum_out=st[:, n % 2, 3:4] if one else st[:, n % 2, g:g + 1])
                        if one:
                            did(ins, score_read, at(li, NITEM, i0 + n))
                        else:
                            did(ins)
                        col += w
                    if not one:
                        ready()
                        did(nc.vector.tensor_reduce(st[:, n % 2, 3:4], st[:, n % 2, 0:3], AX.X,
                                                    ALU.min), score_read, at(li, NITEM, i0 + n))

                def normal(n):
                    hd, b, segs = items[n]
                    w = sum(s[4] for s in segs) * P
                    dve.wait_ge(exp_ready, at(li, NITEM, i0 + n))
                    total = st[:, n % 2, 4:5]
                    if len(segs) > 1:
                        ready()
                        did(nc.vector.tensor_reduce(st[:, n % 2, 7:8], st[:, n % 2, 4:7], AX.X,
                                                    ALU.add))
                        total = st[:, n % 2, 7:8]
                    ready()
                    did(nc.vector.reciprocal(st[:, n % 2, 8:9], total))
                    ready()
                    did(TS(prob[:, n % 2, 0:w], prob[:, n % 2, 0:w], st[:, n % 2, 8:9], None,
                           ALU.mult), prob_ready, at(li, NITEM, i0 + n))

                def take_head(hd):
                    r = slice((hd % 2) * HD, (hd % 2) * HD + HD)
                    dve.wait_ge(head_mm, at(li, NHEAD, HEAD0[kind] + hd))
                    ready()
                    did(nc.vector.tensor_copy(yf[r, y0 + hd // 2, :], PS[r, 5 + hd % 2, :]),
                        head_read, at(li, NHEAD, HEAD0[kind] + hd))

                masked(0)
                for n in range(len(items)):
                    if n + 1 < len(items):
                        masked(n + 1)
                    normal(n)
                    if n % NB == 0 and n:
                        take_head(n // NB - 1)
                take_head(len(items) // NB - 1)

            with lane.loop("layer", DEPTH) as li:
                ready()
                did(TS(vec[:, :], vec2[:, bass.ds(li, 1), :].rearrange("p a n -> p (a n)"), 1.0,
                       None, ALU.mult))
                ready()
                did(TS(wal[96:112, :], wal2[96:112, bass.ds(li, 1), :].rearrange(
                    "p a n -> p (a n)"), 1.0, None, ALU.mult), layer_vecs, at(li, 1, 0))
                prenorm(li, 0)
                ffn(li, 0)
                prenorm(li, 1)
                rope_n[0] = 0
                rope(li, 0, ik[0:HD, 0, :], misc[0:HD, :], 4, rt_a, HD)
                for t in range(4):
                    if t == 1:
                        dve.wait_ge(widx_mm, at(li, 1, 0))
                        ready()
                        did(TS(widx[:, :], PS[:, 1, 0:32], 8 ** -0.5, None, ALU.mult),
                            widx_ready, at(li, 1, 0))
                        dve.wait_ge(ckv_std, at(li, 1, 0))
                        ready()
                        did(nc.vector.reciprocal(rstd[:, :], std[:, :]))
                        ready()
                        did(STT(out=ckv[:, :], in0=ckv[:, :], scalar=vec[:, V_KVN:V_KVN + 1],
                                in1=rstd[:, :], op0=ALU.mult, op1=ALU.mult), ckv_n, at(li, 1, 0))
                    rope(li, 2 + t, iq[:, t, :], xr_a[:, (1 + t) % 2, :], 4, rt_a)
                rope(li, 6, aq[:, 0, :], xr_a[:, 5 % 2, :], 4, rt_a)
                dve.wait_ge(ckv_h, at(li, 1, 0))
                ready()
                did(TT(ckvlo[:, :], ckv[:, :], ckvhi[:, :].bitcast(F32), ALU.subtract), ckv_ready,
                    at(li, 1, 0))
                for t in range(1, 4):
                    rope(li, 6 + t, aq[:, t, :], xr_a[:, (5 + t) % 2, :], 4, rt_a)
                for t in range(4):
                    rope(li, 10 + t, ak[:, t, :], xr_a[:, (9 + t) % 2, :], 4, rt_a)
                for n in range(NIDX):
                    b, hd = n // 8, n % 8
                    w = (b + 1) * P
                    dve.wait_ge(idx_relu, at(li, NIDX, n))
                    ready()
                    wcol = widx[:, b * 8 + hd:b * 8 + hd + 1]
                    if hd == 0:
                        ins = TS(score[:, b, 0:w], relu[:, n % 2, 0:w], wcol, None, ALU.mult)
                    else:
                        ins = STT(out=score[:, b, 0:w], in0=relu[:, n % 2, 0:w], scalar=wcol,
                                  in1=score[:, b, 0:w], op0=ALU.mult, op1=ALU.add)
                    did(ins, idx_added, at(li, NIDX, n))
                    if hd < 7:
                        continue
                    cau = cst[:, C_CAU:C_CAU + P]
                    if b == 0:
                        ready()
                        did(nc.vector.tensor_copy(score[:, 0, 0:P], cau))
                        continue
                    ready()
                    did(TT(score[:, b, b * P:w], score[:, b, b * P:w], cau, ALU.add))
                    for _ in range(TOPK // 8):
                        lane.settle()
                        did(nc.vector.max(top8[:, :], score[:, b, 0:w]))
                        lane.settle()
                        did(nc.vector.match_replace(score[:, b, 0:w], top8[:, :], score[:, b, 0:w],
                                                    TAKEN))
                    ready()
                    did(TS(score[:, b, 0:w], score[:, b, 0:w], -1.0e38, NEG, ALU.is_gt, ALU.mult))
                attention(li, "a", prob_a, st_a, 0)
                for t in range(6):
                    rope(li, 14 + t, bq[:, t, :], xr_b[:, (13 + t) % 2, :], 4, rt_b)
                for t in range(6):
                    rope(li, 20 + t, bk[:, t, :], xr_b[:, (19 + t) % 2, :], 4, rt_b)
                attention(li, "b", prob_b, st_b, 4)
                dve.wait_ge(fm_copied, at(li, NFM, NFM - 1))
                ready()
                did(nc.vector.memset(keep[:, :], 1.0))
                ready()
                did(nc.vector.memset(keep[:, :].rearrange("p (n c) -> p n c", c=CH)[:, :, 0], 0.0))
                for t in range(2):
                    dve.wait_ge(alpha_abs, at(li, 2, t))
                    ready()
                    did(TS(lb[:, t, :], PS[:, 6 + t, :], vec[:, V_BA + t:V_BA + t + 1], 0.0,
                           ALU.add, ALU.min))
                    dve.wait_ge(alpha_log, at(li, 2, t))
                    ready()
                    did(TT(la[:, t, :], lb[:, t, :], la[:, t, :], ALU.subtract))
                    ready()
                    did(nc.vector.tensor_tensor_scan(lb[:, t, :], keep[:, :], la[:, t, :], 0.0,
                                                     ALU.mult, ALU.add))
                    for n in range(8):
                        c = slice(n * CH, (n + 1) * CH)
                        ready()
                        ins = TS(kend[:, t, c], lb[:, t, c], lb[:, t, (n + 1) * CH - 1:(n + 1) * CH],
                                 None, ALU.subtract)
                        if n < 7:
                            did(ins)
                        else:
                            did(ins, decay_sum, at(li, 2, t))
                for t in range(2):
                    dve.wait_ge(decay_exp, at(li, 2, t))
                    ready()
                    did(TT(qdec[:, t, :], qdec[:, t, :], cq[:, t, :], ALU.mult))
                    ready()
                    did(TT(kdec[:, t, :], kdec[:, t, :], ck[:, t, :], ALU.mult))
                    ready()
                    did(TT(kend[:, t, :], kend[:, t, :], ck[:, t, :], ALU.mult), decay_ready,
                        at(li, 2, t))

                def next_state(n):
                    dve.wait_ge(kv_mm, at(li, 7, n))
                    for pr in range(2):
                        for half in range(2):
                            r = slice(half * HD, half * HD + HD)
                            kv = PS[r, 6 + n % 2, pr * 256 + half * P:pr * 256 + (half + 1) * P]
                            ready()
                            if n == 0:
                                ins = nc.vector.tensor_copy(state[r, 1, pr, :], kv)
                            else:
                                ins = STT(out=state[r, n + 1, pr, :], in0=state[r, n, pr, :],
                                          scalar=dec[r, pr, n:n + 1], in1=kv, op0=ALU.mult,
                                          op1=ALU.add)
                            if pr == 1 and half == 1:
                                did(ins, kv_read, at(li, 7, n))
                            else:
                                did(ins)

                def mask_scores(b):
                    dve.wait_ge(att_mm, at(li, NB, b))
                    ready()
                    did(TT(attT[:, b, :, :], PS[:, 4:6, 0:256],
                           cst[:, C_GLA:C_GLA + 512].rearrange("p (a n) -> p a n", a=2), ALU.mult), att_ready, at(li, NB, b))

                for b in range(NB):
                    for n in (2 * b, 2 * b + 1):
                        if n < 7:
                            next_state(n)
                    mask_scores(b)
                for hd in range(C_HEADS):
                    dve.wait_ge(o_std, at(li, C_HEADS, hd))
                    ready()
                    did(nc.vector.reciprocal(rstd[:, :], std[:, :]))
                    ready()
                    did(STT(out=yf[:, 6 + hd, :], in0=PS[:, hd, :], scalar=vec[:, V_CN:V_CN + 1],
                            in1=rstd[:, :], op0=ALU.mult, op1=ALU.mult))
                    ready()
                    did(TT(yf[:, 6 + hd, :], yf[:, 6 + hd, :], cg[:, hd, :], ALU.mult), o_done,
                        at(li, C_HEADS, hd))
                for t in range(10):
                    dve.wait_ge(y_hi, at(li, 10, t))
                    ready()
                    did(TT(ylo[:, t, :], yf[:, t, :], yhi[:, t, :].bitcast(F32), ALU.subtract),
                        y_ready, at(li, 10, t))
                with lane.loop("merge", 2) as i:
                    ready()
                    did(TS(bgate[:, :], vec[:, bass.ds(i * 12 + V_BG, 12)], 1.0, None, ALU.mult),
                        gate_bias, at(li, 2, 0) + i)
                    for m in range(4):
                        wait_step(li, S_MERGE + 5 * m + 4, i, 20)
                        dve.wait_ge(gated, past(li, 24, 3 * m + 2) + i * 12)
                        for c in range(3):
                            ready()
                            did(TT(gate[:, c, :], gate[:, c, :], PS[:, 3 + c, :], ALU.mult))
                        for c in (1, 2):
                            ready()
                            did(TT(gate[:, 0, :], gate[:, 0, :], gate[:, c, :], ALU.add))
                        j = i * 4 + m
                        ready()
                        did(TS(mghi[:, bass.ds(j, 1), :], gate[:, 0:1, :], 1.0, None, ALU.mult))
                        ready()
                        did(TT(mglo[:, bass.ds(j, 1), :], gate[:, 0:1, :],
                               mghi[:, bass.ds(j, 1), :].bitcast(F32), ALU.subtract),
                            merged, past(li, KD, m) + i * 4)
                ready()
                did(nc.vector.memset(acc[:, :], 0.0))
                with lane.loop("wout", 2) as i:
                    for m in range(4):
                        f_tile(li, 1, m, i, 4 + m, S_WOUT + m, 4)
                postnorm(li, 1)
                prenorm(li, 2)
                ffn(li, 1)


def columns(w, tiles, kt):
    d = w.shape[0]
    w = w.reshape(d, kt, P, tiles, P).transpose(0, 3, 2, 1, 4)
    return np.ascontiguousarray(w).reshape(d, tiles, P, kt * P)


def rows(w, n, k2):
    d, r, _ = w.shape
    w = w.reshape(d, r // P // k2, k2, P, n).transpose(0, 1, 3, 2, 4)
    return np.ascontiguousarray(w).reshape(d, r // P // k2, P, k2 * n)


def ffn_in(w):
    w = columns(np.asarray(w), 2 * KF, KD).reshape(DEPTH, 2, KF, P, KD * P)
    return np.ascontiguousarray(w.transpose(0, 2, 1, 3, 4)).reshape(DEPTH, 2 * KF, P, KD * P)


def layout(x, positions, ffn1_pre_g, ffn1_w_in, ffn1_w_out, ffn1_post_g, mix_pre_g, w_in,
           a_kv_norm_g, a_w_kv_up, c_w_alpha_up, c_b_alpha, c_norm_g, w_branch_a, w_branch_b,
           w_branch_c, w_gate, b_gate, w_out, mix_post_g, ffn2_pre_g, ffn2_w_in, ffn2_w_out,
           ffn2_post_g):
    w = np.asarray(w_in)
    part = [w[:, :, OFF[i]:OFF[i + 1]] for i in range(len(SIZES))]
    aq, ackv, iq, ik, iw, bqkv, cq, ck, cv, cg, ca = part
    z = np.zeros
    misc = np.concatenate([ik, iw, z((DEPTH, DM, 24), w.dtype), ca, z((DEPTH, DM, 16), w.dtype)], 2)
    kv = np.asarray(a_w_kv_up).reshape(DEPTH, 1, P, A_HEADS, 2, HD)
    wk = kv[..., 0, :].reshape(DEPTH, 1, P, 512)
    wv = kv[..., 1, :].reshape(DEPTH, 1, P, 512)
    bq, bk, bv = bqkv[:, :, :768], bqkv[:, :, 768:1536], bqkv[:, :, 1536:]
    parts = [columns(np.concatenate([misc, ackv, iq, aq], 2), 10, KD), wk, wv,
             columns(np.concatenate([bq, bk], 2), 12, KD), rows(bv[:, :, :512], 512, 2),
             rows(bv[:, :, 512:], 256, 2), columns(np.concatenate([cq, ck, cg], 2), 8, KD),
             rows(cv, 512, 2)]
    proj = np.concatenate([np.concatenate([p, z(p.shape[:3] + (1024 - p.shape[3],), w.dtype)], 3)
                           for p in parts], 1)
    gates = columns(np.asarray(w_gate), 24, KD).reshape(DEPTH, 3, KD, P, KD * P)
    merge = np.concatenate([gates[:, 0], gates[:, 1], gates[:, 2],
                            columns(np.asarray(w_branch_a), KD, 4),
                            columns(np.asarray(w_branch_c), KD, 4),
                            columns(np.asarray(w_branch_b), KD, 2)], 3)

    def vec(g):
        return np.asarray(g).reshape(DEPTH, -1, P).transpose(2, 0, 1)

    bg = np.asarray(b_gate).reshape(DEPTH, 3, KD, P).transpose(3, 0, 2, 1).reshape(P, DEPTH, 24)
    vecs = np.concatenate([vec(ffn1_pre_g), vec(ffn1_post_g), vec(mix_pre_g), vec(mix_post_g),
                           vec(ffn2_pre_g), vec(ffn2_post_g), vec(a_kv_norm_g), vec(c_norm_g),
                           vec(c_b_alpha), bg], 2)
    arrays = {
        "xT": np.asarray(x)[0].T, "positions": np.asarray(positions), "consts": constants(),
        "vecs": vecs, "walpha": np.asarray(c_w_alpha_up).transpose(1, 0, 2),
        "w_in1": ffn_in(ffn1_w_in), "w_out1": columns(np.asarray(ffn1_w_out), KD, KF),
        "w_proj": proj, "w_merge": merge, "w_wout": columns(np.asarray(w_out), KD, KD),
        "w_in2": ffn_in(ffn2_w_in), "w_out2": columns(np.asarray(ffn2_w_out), KD, KF),
    }
    return {k: np.ascontiguousarray(v) for k, v in arrays.items()}


def kernel(**inputs):
    import concourse.bacc as bacc
    from concourse.bass_utils import run_bass_kernel_spmd

    arrays = layout(**inputs)

    def build(per):
        nc = bacc.Bacc("TRN2", target_bir_lowering=False, num_devices=1)
        args = [nc.dram_tensor(f"in_{k}", v.shape, mybir.dt.from_np(v.dtype),
                               kind="ExternalInput").ap() for k, v in arrays.items()]
        out = nc.dram_tensor("outT", (DM, SEQ), F32, kind="ExternalOutput").ap()
        trunk_kernel(nc, *args, out, per)
        return nc

    per = {}
    build(per)
    nc = build(per)
    r = run_bass_kernel_spmd(nc, [{f"in_{k}": v for k, v in arrays.items()}], core_ids=[0])
    return r.results[0]["outT"].T[None]
```

```python
from contextlib import ExitStack

import numpy as np
import concourse.bass as bass
from concourse import mybir

F32 = mybir.dt.float32
F32R = mybir.dt.float32r
I32 = mybir.dt.int32
ALU = mybir.AluOpType
ACT = mybir.ActivationFunctionType
AX = mybir.AxisListType

P = 128
DEPTH, SEQ, DM, DFF = 2, 512, 1024, 2816
HD, ROT, THETA, EPS = 64, 16, 500000.0, 1e-6
A_HEADS, B_HEADS, C_HEADS, GROUPS = 8, 4, 4, 3
TOPK = min(256, SEQ // 4)
KD = DM // P
KF = DFF // P
NB = SEQ // P
CH = 64
NEG = -1.0e30
TAKEN = -3.0e38
TAU = 16.0
SIZES = (512, 128, 512, 64, 8, 2304, 256, 256, 512, 512, 16)
OFF = [0] + np.cumsum(SIZES).tolist()

FFN_IN, FFN_OUT, PROJ, MERGE_A, MERGE_BC, WOUT = 2 * KF, 3 * KD, 44, 2 * KD, 3 * KD, KD
S_PROJ = FFN_IN + FFN_OUT
S_MA = S_PROJ + PROJ
S_MBC = S_MA + MERGE_A
S_WOUT = S_MBC + MERGE_BC
S_FFN = (0, S_WOUT + WOUT)
NS = S_FFN[1] + FFN_IN + FFN_OUT
RAW, PAIR = 4, 2
PROBS = 3
OUT_SLABS = (8, 8, 6)
A_SLABS = (8, 4)
BC_SLABS = (8, 8, 6)

V_PRE, V_POST = (0, 16, 32), (8, 24, 40)
V_KVN, V_CN, V_BA, V_BG = 48, 49, 50, 52
NV = V_BG + 24

(C_ID, C_ROT, C_ONE, C_CAU, C_G0, C_G1, C_G2, C_GLA) = (0, 128, 256, 384, 512, 768, 1280, 1792)
C_FREQ, C_EPS, C_EPS4, C_UNIT = 2304, 2305, 2306, 2307
NCST = 2308

ROPED = 25
NFM = 34
N_IN = KD + 4


def constants():
    c = np.zeros((P, NCST), np.float32)
    c[:, C_ID:C_ID + P] = np.eye(P)
    for base in (0, HD):
        for d in range(ROT // 2):
            c[base + d + ROT // 2, C_ROT + base + d] = -1.0
            c[base + d, C_ROT + base + d + ROT // 2] = 1.0
            f = np.float32(THETA) ** np.float32(-2.0 * d / ROT)
            c[base + d, C_FREQ] = f
            c[base + d + ROT // 2, C_FREQ] = f
    c[:, C_ONE:C_ONE + P] = 1.0
    q, k = np.arange(P)[:, None], np.arange(P)[None, :]
    causal = k <= q
    c[:, C_CAU:C_CAU + P] = np.where(causal, 0, NEG)
    c[:, C_G0:C_G0 + P] = np.where(k >= q, 0, NEG)
    c[:, C_G0 + P:C_G0 + 2 * P] = np.where(causal, 0, NEG)
    for col, dil in ((C_G1, 4), (C_G2, 16)):
        same = (q - k) % dil == 0
        for b in range(3):
            c[:, col + b * P:col + (b + 1) * P] = np.where(same, 0, NEG)
        c[:, col + 3 * P:col + 4 * P] = np.where(same & causal, 0, NEG)
    intra = (q <= k) & (q // CH == k // CH)
    c[:, C_GLA:C_GLA + 4 * P] = np.tile(intra, (1, 4))
    c[:, C_EPS], c[:, C_EPS4], c[:, C_UNIT] = EPS, 4 * EPS, 1.0
    return c


def proj_plan():
    steps = [("fm", 8, ("misc", 0))]
    steps += [("fm", 8, ("iq", t)) for t in range(4)]
    steps += [("fm", 8, ("ckv", 0))]
    steps += [("fm", 8, ("aq", t)) for t in range(4)]
    steps += [("ka", 4, None), ("va", 4, None)]
    steps += [("fm", 8, ("cq", t)) for t in range(2)]
    steps += [("fm", 8, ("ck", t)) for t in range(2)]
    steps += [("fm", 8, ("cg", t)) for t in range(4)]
    steps += [("tm", 8, None)] * 4
    steps += [("fm", 8, ("bq", t)) for t in range(6)]
    steps += [("fm", 8, ("bk", t)) for t in range(6)]
    steps += [("tm", 8, None)] * 4 + [("tm", 4, None)] * 4
    assert len(steps) == PROJ
    return steps


J_CKV, J_AQ, J_KA, J_VA, J_C, J_VC, J_B, J_VB = 5, 6, 10, 11, 12, 20, 24, 36


def finished(steps, blocks, per_item):
    done, total = {}, 0
    for j, n in zip(steps, blocks):
        total += n
        done[j] = -(-total // per_item) - 1
    return done


DECAY_AT = 3

IDX_FILL, A_FILL, B_FILL = 2, 3, 6
IDX_DONE = finished(range(J_CKV, J_C), (8, 8, 8, 8, 8, 4, 4), IDX_FILL)
A_DONE = finished(range(J_B, J_VB), (8,) * 12, A_FILL)
B_DONE = finished(range(MERGE_A), A_SLABS * KD, B_FILL)


def rope_at(j):
    return min(A_DONE[j] + 2, A_HEADS * NB)


def attention_items(kind):
    items = []
    if kind == "a":
        for h in range(A_HEADS):
            for b in range(NB):
                items.append((h, b, [(h // 2, h // 2, h % 2, 0, b + 1, None, h * HD)]))
        return items
    for h in range(B_HEADS):
        for b in range(NB):
            segs = []
            for g in range(GROUPS):
                head = g * B_HEADS + h
                first = max(b - 1, 0) if g == 0 else 0
                n = b + 1 - first
                end = (C_G0 + 2 * P, C_G1 + 4 * P, C_G2 + 4 * P)[g]
                segs.append((head // 2, head // 2, head % 2, first, n, end - n * P, head * HD))
            items.append((h, b, segs))
    return items


def groups_of(segs):
    blocks, col = [], 0
    for (_, _, _, first, n, _, vcol) in segs:
        for j in range(n):
            blocks.append((col, first + j, vcol))
            col += P
    return [blocks[i:i + 4] for i in range(0, len(blocks), 4)]


ITEMS = {"a": attention_items("a"), "b": attention_items("b")}
ITEM0 = {"a": 0, "b": len(ITEMS["a"])}
NITEM = len(ITEMS["a"]) + len(ITEMS["b"])
NGRP = {k: sum(len(groups_of(s)) for _, _, s in ITEMS[k]) for k in "ab"}
GRP0 = {"a": 0, "b": NGRP["a"]}
TURN = {"a": (2, 3), "b": (3, 7)}
NGRPS = NGRP["a"] + NGRP["b"]
HEAD0 = {"a": 0, "b": A_HEADS}
NHEAD = A_HEADS + B_HEADS
NIDX = NB * 8


class Lane:

    def __init__(self, eng, order, name, per):
        self.eng, self.order, self.name, self.per = eng, order, name, per
        self.turns, self.n, self.last = 0, 0, None

    def ready(self):
        if self.last is not None:
            self.eng.wait_ge(*self.last)

    def settle(self):
        self.ready()
        self.n += 1
        self.eng.sem_inc(self.order, 1)
        self.last = (self.order, self.turns + self.n)

    def did(self, ins, sem=None, value=None):
        if sem is None:
            sem, self.n = self.order, self.n + 1
            value = self.turns + self.n
        ins.then_inc(sem, 1)
        self.last = (sem, value)

    def fence(self):
        if self.last is None or self.last[0] is not self.order:
            self.settle()

    def loop(self, key, count):
        return _Loop(self, (self.name, key), count)


class _Loop:
    def __init__(self, lane, key, count):
        self.lane, self.key, self.count = lane, key, count

    def __enter__(self):
        lane = self.lane
        lane.fence()
        self.turns, self.n = lane.turns, lane.n
        self.cm = lane.eng.Fori(0, self.count)
        i = self.cm.__enter__()
        lane.turns = self.turns + i * lane.per.get(self.key, 0)
        lane.last = (lane.order, lane.turns + lane.n)
        return i

    def __exit__(self, *exc):
        lane = self.lane
        lane.fence()
        lane.per[self.key] = lane.n - self.n
        self.cm.__exit__(*exc)
        lane.turns, lane.n = self.turns, self.n + self.count * lane.per[self.key]
        lane.last = (lane.order, lane.turns + lane.n)


def trunk_kernel(nc, xT, positions, consts, vecs, walpha, w_in1, w_out1, w_proj, w_ma, w_mbc, w_wout,
                 w_in2, w_out2, outT, per):
    ctx = ExitStack()
    with ctx:
        def sb(name, shape, dt=F32, scope=ctx):
            return scope.enter_context(nc.sbuf_tensor(name, shape, dt))

        def sem(name):
            return ctx.enter_context(nc.semaphore(name))

        h = sb("h", [P, KD, SEQ])
        xhi = sb("xhi", [P, KD, SEQ], F32R)
        with ExitStack() as s:
            f = sb("f", [P, KD, SEQ], F32, s)
        xlo = sb("xlo", [P, KD, SEQ], F32R)
        wraw = sb("wraw", [P, RAW, 1024])
        whi = sb("whi", [P, PAIR, 1024], F32R)
        wlo = sb("wlo", [P, PAIR, 1024], F32R)
        cst = sb("cst", [P, NCST])
        cosT = sb("cosT", [P, SEQ])
        sinT = sb("sinT", [P, SEQ])
        vec2 = sb("vec2", [P, DEPTH, NV])
        vec = sb("vec", [P, NV])
        bgate = sb("bgate", [P, 12])
        wal2 = sb("wal2", [P, DEPTH, 256])
        wal = sb("wal", [P, 256])
        sq = sb("sq", [P, 2, SEQ])
        acc = sb("acc", [P, SEQ])
        std = sb("std", [P, SEQ])
        rstd = sb("rstd", [P, SEQ])
        xt = sb("xt", [P, 2, SEQ])
        last = sb("last", [P, 2, 8])
        dec = sb("dec", [P, 2, 8])
        ms = sb("ms", [P, C_HEADS * NB])
        inv = sb("inv", [P, C_HEADS * NB])

        with ExitStack() as s:
            hidhi = sb("hidhi", [P, KF, SEQ], F32R, s)
            hidlo = sb("hidlo", [P, KF, SEQ], F32R, s)
            silu = sb("silu", [P, 2, SEQ], F32, s)
            hf = sb("hf", [P, 1, SEQ], F32, s)
        misc = sb("misc", [P, SEQ])
        with ExitStack() as s:
            yhi = sb("yhi", [P, 4, SEQ], F32R, s)
            ylo = sb("ylo", [P, 4, SEQ], F32R, s)
        cq = sb("cq", [P, 2, SEQ])
        ck = sb("ck", [P, 2, SEQ])
        vc = sb("vc", [P, NB, 512])
        with ExitStack() as s:
            mghi = sb("mghi", [P, KD, SEQ], F32R, s)
            mglo = sb("mglo", [P, KD, SEQ], F32R, s)
        part = sb("part", [P, KD, SEQ])
        aq = part[:, 4:KD, :]
        cg = sb("cg", [P, 4, SEQ])
        with ExitStack() as s:
            iq = sb("iq", [P, 4, SEQ], F32, s)
            ik = sb("ik", [P, 1, SEQ], F32, s)
            relu = sb("relu", [P, 2, SEQ], F32, s)
            ckv = sb("ckv", [P, SEQ], F32, s)
            ckvhi = sb("ckvhi", [P, SEQ], F32R, s)
            ckvlo = sb("ckvlo", [P, SEQ], F32R, s)
            widx = sb("widx", [P, NB * 8], F32, s)
        bq = sb("bq", [P, 6, SEQ])
        bk = sb("bk", [P, 6, SEQ])
        with ExitStack() as s:
            ak = sb("ak", [P, 4, SEQ], F32, s)
            va = sb("va", [P, NB, 512], F32, s)
            score = sb("score", [P, NB, SEQ], F32, s)
            prob_a = sb("prob_a", [P, PROBS, 512], F32, s)
            st_a = sb("st_a", [P, PROBS, 16], F32, s)
            top8 = sb("top8", [P, 8], F32, s)
        with ExitStack() as s:
            ybhi = sb("ybhi", [P, 2, SEQ], F32R, s)
            yblo = sb("yblo", [P, 2, SEQ], F32R, s)
        vb = sb("vb", [P, NB, 768])
        with ExitStack() as s:
            kendT = sb("kendT", [P, NB, 256], F32, s)
            state = sb("state", [P, 8, 2, P], F32, s)
        prob_b = sb("prob_b", [P, PROBS, 1280])
        st_b = sb("st_b", [P, PROBS, 16])
        xr, rt, turn, gate = xt, acc, sq, xt
        attT = [b[:, j, :].rearrange("p (a n) -> p a n", a=2) for b in (xt, sq) for j in (0, 1)]
        diag = xt[:, :, :].rearrange("p a (b n) -> p a b n", n=P)
        PS = ctx.enter_context(nc.psum_tensor("PS", [P, 8, 512], F32))

        la = part[:, 0:2, :]
        lb = part[:, 2:4, :]
        eb = (std, rstd)
        keep = rstd

        ident = cst[:, C_ID:C_ID + P]
        onesm = cst[:, C_ONE:C_ONE + P]

        raw_loaded = [sem(f"raw_loaded{i}") for i in range(RAW)]
        w_hi = sem("w_hi")
        w_ready = sem("w_ready")
        step_done = sem("step_done")
        consts_in = sem("consts_in")
        order_v, order_s, order_p = sem("order_v"), sem("order_s"), sem("order_p")
        tables = sem("tables")
        tables_done = sem("tables_done")
        layer_vecs = sem("layer_vecs")
        h_new = sem("h_new")
        f_scaled = sem("f_scaled")
        hsq = sem("hsq")
        hsq_mm = sem("hsq_mm")
        fsum_mm = sem("fsum_mm")
        std_ready = sem("std_ready")
        rstd_ready = sem("rstd_ready")
        x_ready = sem("x_ready")
        x_f32, x_hi = sem("x_f32"), sem("x_hi")
        gate_scaled = sem("gate_scaled")
        silu_ready = sem("silu_ready")
        ffn_read = sem("ffn_read")
        hid_ready = sem("hid_ready")
        fsq = sem("fsq")
        f_read = sem("f_read")
        fm_copied = sem("fm_copied")
        rot_mm = sem("rot_mm")
        roped = sem("roped")
        tm_copied = sem("tm_copied")
        ckv_f32, ckv_sum, ckv_std = sem("ckv_f32"), sem("ckv_sum"), sem("ckv_std")
        ckv_n, ckv_h, ckv_ready = sem("ckv_n"), sem("ckv_h"), sem("ckv_ready")
        widx_mm, widx_ready = sem("widx_mm"), sem("widx_ready")
        ik_copied = sem("ik_copied")
        idx_mm, idx_relu, idx_added = sem("idx_mm"), sem("idx_relu"), sem("idx_added")
        bias_ready = sem("bias_ready")
        score_mm = sem("score_mm")
        score_read = sem("score_read")
        exp_ready = sem("exp_ready")
        prob_ready = sem("prob_ready")
        turn_mm = sem("turn_mm")
        turned = sem("turned")
        head_mm = sem("head_mm")
        head_read = sem("head_read")
        alpha_mm, alpha_abs, alpha_log, alpha_min = (sem("alpha_mm"), sem("alpha_abs"),
                                                     sem("alpha_log"), sem("alpha_min"))
        decay_sum, decay_exp, decay_ready = sem("decay_sum"), sem("decay_exp"), sem("decay_ready")
        decay_b, decay_l = sem("decay_b"), sem("decay_l")
        kend_mm, kend_T = sem("kend_mm"), sem("kend_T")
        kv_mm, kv_read = sem("kv_mm"), sem("kv_read")
        att_mm, att_ready = sem("att_mm"), sem("att_ready")
        o_mm, o_sq, o_sum, o_std, o_done = (sem("o_mm"), sem("o_sq"), sem("o_sum"), sem("o_std"),
                                            sem("o_done"))
        diag_ready = sem("diag_ready")
        inv_mm = sem("inv_mm")
        y_hi, y_ready = sem("y_hi"), sem("y_ready")
        gate_bias = sem("gate_bias")
        gated = sem("gated")
        merged_a = sem("merged_a")
        gated_a = sem("gated_a")
        merged = sem("merged")
        out_done = sem("out_done")

        def at(li, per_layer, n):
            return li * per_layer + (n + 1)

        def past(li, per_layer, n):
            return li * per_layer + (n + 2)

        block = ctx.enter_context(nc.Block())

        @block.sync
        def _(sp):
            sp.dma_start(cst[:, :], consts).then_inc(consts_in, 16)
            sp.dma_start(acc[:, :].bitcast(I32),
                         positions.to_broadcast([P, SEQ])).then_inc(consts_in, 16)
            sp.dma_start(vec2[:, :, :], vecs).then_inc(consts_in, 16)
            sp.dma_start(wal2[96:112, :, :], walpha).then_inc(consts_in, 16)
            for k in range(KD):
                sp.dma_start(h[:, k, :], xT[k * P:(k + 1) * P, :]).then_inc(consts_in, 16)

            def load(li, s, src, i=0, per_iter=0):
                n = src.shape[-1]
                sp.wait_ge(w_ready, at(li, NS, s) + i * per_iter)
                sp.dma_start(wraw[:, s % RAW, 0:n], src).then_inc(raw_loaded[s % RAW], 16)

            def ffn(li, s0, w1, w2):
                with sp.Fori(0, FFN_IN // RAW) as i:
                    for c in range(RAW):
                        load(li, s0 + c, w1[li, i * RAW + c, :, :], i, RAW)
                with sp.Fori(0, 2) as i:
                    for m in range(4):
                        for c in range(3):
                            load(li, s0 + FFN_IN + 3 * m + c,
                                 w2[li, i * 4 + m, :, c * 1024:c * 1024 + OUT_SLABS[c] * P], i, 12)

            with sp.Fori(0, DEPTH) as li:
                ffn(li, S_FFN[0], w_in1, w_out1)
                for j, (_, slabs, _) in enumerate(proj_plan()):
                    load(li, S_PROJ + j, w_proj[li, j, :, 0:slabs * P])
                with sp.Fori(0, 2) as i:
                    for m in range(4):
                        for c in range(2):
                            load(li, S_MA + 2 * m + c,
                                 w_ma[li, i * 4 + m, :, c * 1024:c * 1024 + A_SLABS[c] * P], i, 8)
                with sp.Fori(0, 2) as i:
                    for m in range(4):
                        for c in range(3):
                            load(li, S_MBC + 3 * m + c,
                                 w_mbc[li, i * 4 + m, :, c * 1024:c * 1024 + BC_SLABS[c] * P], i, 12)
                with sp.Fori(0, 2) as i:
                    for c in range(4):
                        load(li, S_WOUT + c, w_wout[li, i * 4 + c, :, :], i, 4)
                ffn(li, S_FFN[1], w_in2, w_out2)
            for c in range(PAIR):
                load(DEPTH, c, w_in1[0, c, :, :])
            for k in range(KD):
                sp.wait_ge(h_new, 8 * 3 * DEPTH + k + 1)
                sp.dma_start(outT[k * P:(k + 1) * P, :], h[:, k, :]).then_inc(out_done, 16)
            sp.wait_ge(out_done, 16 * KD)

        @block.gpsimd
        def _(pool):
            lane = Lane(pool, order_p, "pool", per)
            pool.sem_inc(w_ready, RAW)

            def split(li, s, slabs, i=0, per_iter=0):
                n = slabs * P
                pool.wait_ge(w_hi, at(li, NS, s) + i * per_iter)
                nc.gpsimd.tensor_tensor(wlo[:, s % PAIR, 0:n], wraw[:, s % RAW, 0:n],
                                        whi[:, s % PAIR, 0:n].bitcast(F32),
                                        ALU.subtract).then_inc(w_ready, 1)

            def ffn(li, s0):
                with pool.Fori(0, FFN_IN // RAW) as i:
                    for c in range(RAW):
                        split(li, s0 + c + 2, 8, i, RAW)
                with pool.Fori(0, 2) as i:
                    for n in range(12):
                        split(li, s0 + FFN_IN + n + 2, OUT_SLABS[(n + 2) % 3], i, 12)

            def add_f(li, q):
                for k in range(KD):
                    pool.wait_ge(f_scaled, at(li, 24, 8 * q + k))
                    nc.gpsimd.tensor_tensor(h[:, k, :], h[:, k, :], f[:, k, :],
                                            ALU.add).then_inc(h_new, 1)

            plan = proj_plan()
            split(0, 0, 8)
            split(0, 1, 8)
            with pool.Fori(0, DEPTH) as li:
                ffn(li, S_FFN[0])
                add_f(li, 0)
                for j in range(PROJ):
                    split(li, S_PROJ + j + 2, plan[j + 2][1] if j + 2 < PROJ else
                          A_SLABS[j + 2 - PROJ])
                for n in range(MERGE_A):
                    split(li, S_MA + n + 2, A_SLABS[n % 2] if n + 2 < MERGE_A else 8)
                with pool.Fori(0, 2) as i:
                    for n in range(12):
                        split(li, S_MBC + n + 2, BC_SLABS[(n + 2) % 3], i, 12)
                with pool.Fori(0, 2) as i:
                    for c in range(4):
                        split(li, S_WOUT + c + 2, 8, i, 4)
                add_f(li, 1)
                ffn(li, S_FFN[1])
                add_f(li, 2)

        @block.scalar
        def _(act):
            lane = Lane(act, order_s, "act", per)
            did, ready = lane.did, lane.ready
            act.sem_inc(gated, 1)
            act.sem_inc(gated_a, 1)
            act.sem_inc(hsq, 1)

            def hi(li, s, slabs, i=0, per_iter=0):
                n, slot = slabs * P, s % RAW
                loads = li * (NS // RAW) + i * (per_iter // RAW) + s // RAW
                act.wait_ge(raw_loaded[slot], (loads + 1) * 16)
                act.wait_ge(step_done, at(li, NS, s) + i * per_iter)
                ready()
                did(nc.scalar.activation(whi[:, s % PAIR, 0:n], wraw[:, slot, 0:n], ACT.Copy),
                    w_hi, at(li, NS, s) + i * per_iter)

            def wait_step(li, s, i=0, per_iter=0):
                act.wait_ge(step_done, at(li, NS, s) + i * per_iter + PAIR)

            def prenorm(li, p):
                for k in range(KD):
                    act.wait_ge(h_new, at(li, 24, 8 * p + k))
                    act.wait_ge(hsq_mm, at(li, 24, 8 * p + k))
                    ready()
                    did(nc.scalar.activation(sq[:, k % 2, :], h[:, k, :], ACT.Square),
                        hsq, past(li, 24, 8 * p + k))
                    if p != 1:
                        g = V_PRE[p] + k
                        did(nc.scalar.activation(xhi[:, k, :], h[:, k, :], ACT.Copy,
                                                 scale=vec[:, g:g + 1]),
                            x_hi, at(li, 24, 8 * p + k))
                act.wait_ge(hsq_mm, at(li, 24, 8 * p + 7) + 2)
                root(li, 2 * p, C_EPS, 1.0)
                if p == 1:
                    for k in range(KD):
                        act.wait_ge(x_f32, at(li, 8, k))
                        did(nc.scalar.activation(xhi[:, k, :], xt[:, k % 2, :], ACT.Copy),
                            x_hi, at(li, 24, 8 * p + k))

            def root(li, z, eps, scale):
                ready()
                did(nc.scalar.activation(std[:, :], PS[:, 0, :], ACT.Sqrt,
                                         bias=cst[:, eps:eps + 1], scale=scale / DM),
                    std_ready, at(li, 6, z))

            def f_root(li, q, eps, scale):
                act.wait_ge(fsum_mm, at(li, 3, q))
                root(li, 2 * q + 1, eps, scale)

            def f_square(li, q, m, i, bank):
                act.wait_ge(f_read, at(li, 24, 8 * q + m) + i * 4 + 2)
                ready()
                did(nc.scalar.activation(sq[:, m % 2, :], PS[:, bank, :], ACT.Square),
                    fsq, at(li, 24, 8 * q + m) + i * 4)

            def ffn(li, fi):
                s0 = S_FFN[fi]
                with lane.loop(f"ffn_in{fi}", FFN_IN // 4) as i:
                    for c in range(4):
                        wait_step(li, s0 + c, i, 4)
                        hi(li, s0 + c + 2, 8, i, 4)
                        if c % 2 == 0:
                            act.wait_ge(gate_scaled, at(li, 2 * KF, fi * KF + c // 2) + i * 2)
                            did(nc.scalar.activation(silu[:, c // 2, :], silu[:, c // 2, :],
                                                     ACT.Silu),
                                silu_ready, at(li, 2 * KF, fi * KF + c // 2) + i * 2)
                with lane.loop(f"ffn_out{fi}", 2) as i:
                    for m in range(4):
                        for c in range(3):
                            n = 3 * m + c
                            wait_step(li, s0 + FFN_IN + n, i, 12)
                            hi(li, s0 + FFN_IN + n + 2, OUT_SLABS[(n + 2) % 3], i, 12)
                        f_square(li, 2 * fi, m, i, 4 + m)
                f_root(li, 2 * fi, C_EPS4, 4.0)

            plan = proj_plan()

            def roll(li, j):
                wait_step(li, S_PROJ + j)
                hi(li, S_PROJ + j + 2, plan[j + 2][1] if j + 2 < PROJ else A_SLABS[j + 2 - PROJ])

            class Fm:
                tile = 0
                rope = 0

            def copy_fm(li, kind, t, bank):
                c = Fm.tile
                Fm.tile += 1
                ready()
                if kind in ("iq", "aq", "ak", "bq", "bk"):
                    r = Fm.rope
                    Fm.rope += 1
                    act.wait_ge(roped, at(li, ROPED, r))
                    ins = nc.scalar.activation(xr[:, r % 2, :], PS[:, bank, :], ACT.Copy)
                elif kind == "misc":
                    Fm.rope += 1
                    ins = nc.scalar.activation(misc[:, :], PS[:, bank, :], ACT.Copy)
                elif kind == "ckv":
                    ins = nc.scalar.activation(ckv[:, :], PS[:, bank, :], ACT.Copy)
                elif kind == "cq":
                    ins = nc.scalar.activation(cq[:, t, :], PS[:, bank, :], ACT.Copy, scale=HD ** -0.5)
                elif kind == "ck":
                    ins = nc.scalar.activation(ck[:, t, :], PS[:, bank, :], ACT.Copy)
                else:
                    ins = nc.scalar.activation(cg[:, t, :], PS[:, bank, :], ACT.Silu)
                did(ins, fm_copied, at(li, NFM, c))

            def copy_tm(li, g, dest, col, n, banks=(0, 1, 2, 3)):
                for b in range(NB):
                    ready()
                    did(nc.scalar.activation(dest[:, b, col:col + n], PS[:, banks[b], 0:n], ACT.Copy),
                        tm_copied, at(li, 16, 4 * g + b))

            def attention(li, kind, prob, st, between):
                items, i0, g0 = ITEMS[kind], ITEM0[kind], GRP0[kind]

                def exponentials(n):
                    col = 0
                    act.wait_ge(score_read, at(li, NITEM, i0 + n))
                    for g, seg in enumerate(items[n][2]):
                        w = seg[4] * P
                        ins = nc.scalar.activation(prob[:, n % PROBS, col:col + w],
                                                   prob[:, n % PROBS, col:col + w], ACT.Exp,
                                                   bias=st[:, n % PROBS, 3:4], scale=-1.0,
                                                   accum_out=st[:, n % PROBS, 4 + g:5 + g])
                        if g == len(items[n][2]) - 1:
                            did(ins, exp_ready, at(li, NITEM, i0 + n))
                        else:
                            did(ins)
                        col += w

                grp = g0
                exponentials(0)
                for n in range(len(items)):
                    between(n)
                    if n + 1 < len(items):
                        exponentials(n + 1)
                    for blocks in groups_of(items[n][2]):
                        w = len(blocks) * P
                        act.wait_ge(turn_mm, at(li, NGRPS, grp))
                        ready()
                        did(nc.scalar.activation(turn[:, grp % 2, 0:w],
                                                 PS[:, TURN[kind][grp % 2], 0:w], ACT.Copy),
                            turned, at(li, NGRPS, grp))
                        grp += 1
                between(len(items))

            act.wait_ge(tables, 1)
            did(nc.scalar.activation(sinT[:, :], xt[:, 0, :], ACT.Sin), tables_done, 1)
            ready()
            did(nc.scalar.activation(cosT[:, :], xt[:, 1, :], ACT.Sin), tables_done, 2)
            hi(0, 0, 8)
            hi(0, 1, 8)
            with lane.loop("layer", DEPTH) as li:
                act.wait_ge(layer_vecs, at(li, 1, 0))
                prenorm(li, 0)
                ffn(li, 0)
                prenorm(li, 1)
                Fm.tile = Fm.rope = 0
                for j in range(J_CKV):
                    roll(li, j)
                    copy_fm(li, *plan[j][2], 5 + j % 3)
                    if j == 3:
                        act.wait_ge(roped, at(li, ROPED, 0) + 2)
                        act.dma_start(ik[HD:P, 0, :], ik[0:HD, 0, :]).then_inc(ik_copied, 16)

                def latent(n):
                    for j in range(J_CKV, J_C):
                        if IDX_DONE[j] != n - 1:
                            continue
                        roll(li, j)
                        if j == J_KA:
                            for t in range(4):
                                copy_fm(li, "ak", t, (3, 5, 6, 7)[t])
                        elif j == J_VA:
                            copy_tm(li, 0, va, 0, 512, (3, 5, 6, 7))
                        else:
                            copy_fm(li, *plan[j][2], 5 + j % 3)
                        if j == J_CKV:
                            ready()
                            did(nc.scalar.activation(sq[:, 0, :], ckv[:, :], ACT.Square), ckv_f32,
                                at(li, 1, 0))
                    if n == IDX_DONE[J_CKV] + 4:
                        act.wait_ge(ckv_sum, at(li, 1, 0))
                        did(nc.scalar.activation(std[:, :], PS[:, 3, :], ACT.Sqrt,
                                                 bias=cst[:, C_EPS:C_EPS + 1], scale=1.0 / P),
                            ckv_std, at(li, 1, 0))
                    if n == IDX_DONE[J_CKV] + 6:
                        act.wait_ge(ckv_n, at(li, 1, 0))
                        did(nc.scalar.activation(ckvhi[:, :], ckv[:, :], ACT.Copy), ckv_h,
                            at(li, 1, 0))

                for n in range(NIDX):
                    w = (n // 8 + 1) * P
                    act.wait_ge(idx_mm, at(li, NIDX, n))
                    if n >= 2:
                        act.wait_ge(idx_added, at(li, NIDX, n - 2))
                    did(nc.scalar.activation(relu[:, n % 2, 0:w], PS[:, n % 3, 0:w], ACT.Relu,
                                             scale=HD ** -0.5), idx_relu, at(li, NIDX, n))
                    latent(n)
                for j in range(J_C, J_B):
                    roll(li, j)
                    if j < J_VC:
                        copy_fm(li, *plan[j][2], 5 + j % 3)
                copy_tm(li, 1, vc, 0, 512)

                def decays(li, n):
                    if n == 0:
                        act.wait_ge(alpha_mm, at(li, 1, 0))
                        for t in range(2):
                            did(nc.scalar.activation(la[:, t, :], PS[:, 6 + t, :], ACT.Abs,
                                                     bias=vec[:, V_BA + t:V_BA + t + 1]),
                                alpha_abs, at(li, 2, t))
                        ready()
                        for t in range(2):
                            did(nc.scalar.activation(la[:, t, :], la[:, t, :], ACT.Exp, scale=-1.0))
                        ready()
                        for t in range(2):
                            did(nc.scalar.activation(la[:, t, :], la[:, t, :], ACT.Ln,
                                                     bias=cst[:, C_UNIT:C_UNIT + 1]),
                                alpha_log, at(li, 2, t))
                    if n == DECAY_AT + 1:
                        act.wait_ge(decay_sum, at(li, 2, 1))
                        for t in range(2):
                            did(nc.scalar.activation(dec[:, t, :], last[:, t, :], ACT.Exp,
                                                     scale=1 / TAU))
                            did(nc.scalar.activation(eb[t][:, :], lb[:, t, :], ACT.Exp,
                                                     scale=1 / TAU))
                            did(nc.scalar.activation(la[:, t, :], lb[:, t, :], ACT.Exp,
                                                     scale=-1 / TAU), decay_b, at(li, 2, t))
                    if n == DECAY_AT + 3:
                        act.wait_ge(decay_l, at(li, 2, 1))
                        for t in range(2):
                            did(nc.scalar.activation(lb[:, t, :], lb[:, t, :], ACT.Exp,
                                                     scale=-1 / TAU), decay_exp, at(li, 2, t))


                def queries_b(n):
                    decays(li, n)
                    for j in range(J_B, J_VB):
                        if A_DONE[j] == n - 1:
                            roll(li, j)
                            if j == J_B:
                                act.wait_ge(bias_ready, at(li, 1, 0))
                            copy_fm(li, *plan[j][2], 5 + j % 2)

                attention(li, "a", prob_a, st_a, queries_b)
                for b, step in enumerate((None, 0, 1, None)):
                    act.wait_ge(kend_mm, at(li, NB, b))
                    ready()
                    did(nc.scalar.activation(kendT[:, b, :], PS[:, 6 + b % 2, 0:256], ACT.Copy),
                        kend_T, at(li, NB, b))
                    if step is not None:
                        roll(li, J_VB + step)
                for j in range(J_VB + 2, J_VB + 4):
                    roll(li, j)
                copy_tm(li, 2, vb, 0, 512)
                act.wait_ge(o_mm, at(li, 1, 0))
                for hh in range(C_HEADS):
                    if hh >= 2:
                        act.wait_ge(o_sum, at(li, C_HEADS, hh - 2))
                    ready()
                    did(nc.scalar.activation(sq[:, hh % 2, :], PS[:, 4 + hh, :], ACT.Square),
                        o_sq, at(li, C_HEADS, hh))
                    roll(li, J_VB + 4 + hh)
                act.wait_ge(o_sum, at(li, C_HEADS, C_HEADS - 1))
                did(nc.scalar.activation(ms[:, :], PS[:, 2, 0:C_HEADS * NB], ACT.Sqrt,
                                         bias=cst[:, C_EPS:C_EPS + 1], scale=1.0 / P),
                    o_std, at(li, 1, 0))
                for b in range(NB):
                    ready()
                    did(nc.scalar.activation(vb[:, b, 512:768], PS[:, b // 2, b % 2 * 256:
                                                                  (b % 2 + 1) * 256], ACT.Copy),
                        tm_copied, at(li, 16, 12 + b))

                def split_y(t, dest, src):
                    did(nc.scalar.activation(dest, src, ACT.Copy), y_hi, at(li, 10, t))

                act.wait_ge(o_done, at(li, C_HEADS, 3))
                for t in range(4):
                    split_y(t, yhi[:, t, :], aq[:, t, :])

                def merge_a(n):
                    for s in range(MERGE_A):
                        if B_DONE[s] != n - 1:
                            continue
                        m = s // 2
                        wait_step(li, S_MA + s)
                        hi(li, S_MA + s + 2, A_SLABS[s % 2] if s + 2 < MERGE_A else 8)
                        if s % 2 == 0:
                            act.wait_ge(merged_a, past(li, KD, max(m - 2, -1)))
                            did(nc.scalar.activation(gate[:, m % 2, :], PS[:, 5, :], ACT.Sigmoid,
                                                     bias=vec[:, V_BG + 3 * m:V_BG + 3 * m + 1]),
                                gated_a, past(li, KD, m))

                attention(li, "b", prob_b, st_b, merge_a)
                act.wait_ge(merged_a, past(li, KD, KD - 1))
                ready()
                for t in range(4):
                    split_y(4 + t, yhi[:, t, :], cg[:, t, :])
                act.wait_ge(head_read, at(li, NHEAD, NHEAD - 1))
                for t in range(2):
                    split_y(8 + t, ybhi[:, t, :], bq[:, t, :])
                with lane.loop("merge", 2) as i:
                    act.wait_ge(gate_bias, at(li, 2, 0) + i)
                    for m in range(4):
                        for c in range(3):
                            n = 3 * m + c
                            wait_step(li, S_MBC + n, i, 12)
                            hi(li, S_MBC + n + 2, BC_SLABS[(n + 2) % 3], i, 12)
                            if c < 2:
                                act.wait_ge(merged, past(li, KD, m - 1) + i * 4)
                                did(nc.scalar.activation(
                                    gate[:, c, :], PS[:, c, :], ACT.Sigmoid,
                                    bias=bgate[:, 3 * m + 2 - c:3 * m + 3 - c]),
                                    gated, past(li, 16, 2 * m + c) + i * 8)
                with lane.loop("wout", 2) as i:
                    for m in range(4):
                        wait_step(li, S_WOUT + m, i, 4)
                        hi(li, S_WOUT + m + 2, 8, i, 4)
                        f_square(li, 1, m, i, 4 + m)
                f_root(li, 1, C_EPS, 1.0)
                prenorm(li, 2)
                ffn(li, 1)

        @block.tensor
        def _(pe):
            pe.sem_inc(step_done, PAIR)
            pe.sem_inc(hsq_mm, 2)
            pe.wait_ge(consts_in, 16 * N_IN)
            plan = proj_plan()

            def mm3(out, ahi, alo, bhi, blo, start, stop, shared=False):
                nc.tensor.matmul(out, ahi, blo, start=start, stop=False, skip_group_check=shared)
                nc.tensor.matmul(out, alo, bhi, start=False, stop=False, skip_group_check=shared)
                return nc.tensor.matmul(out, ahi, bhi, start=False, stop=stop,
                                        skip_group_check=shared)

            def want(li, s, i=0, per_iter=0):
                pe.wait_ge(w_ready, at(li, NS, s) + i * per_iter + RAW)

            def slab(s, k):
                return whi[:, s % PAIR, k * P:(k + 1) * P], wlo[:, s % PAIR, k * P:(k + 1) * P]

            def column(s, bank, slabs, khi, klo, k0=0, first=True, last=True, w0=0):
                for k in range(slabs):
                    a, b = slab(s, w0 + k)
                    ins = mm3(PS[:, bank, :], a, b, khi[:, k0 + k, :], klo[:, k0 + k, :],
                              first and k == 0, last and k == slabs - 1)
                return ins

            def sum_rows(bank, src):
                return nc.tensor.matmul(PS[:, bank, :], onesm, src, start=True, stop=True)

            def square_in(li, p, k):
                pe.wait_ge(hsq, past(li, 24, 8 * p + k))
                nc.tensor.matmul(PS[:, 0, :], onesm, sq[:, k % 2, :], start=k == 0,
                                 stop=k == KD - 1).then_inc(hsq_mm, 1)

            def postnorm(li, q):
                pe.wait_ge(f_read, at(li, 24, 8 * q + 7) + 4)
                sum_rows(0, acc[:, :]).then_inc(fsum_mm, 1)

            def ffn(li, fi):
                s0 = S_FFN[fi]

                def in_step(c, i):
                    want(li, s0 + c, i, 4)
                    if c % 2 == 0:
                        pe.wait_ge(ffn_read, at(li, 2 * KF, fi * KF + c // 2) + i * 2)
                    column(s0 + c, 1 + c, 8, xhi, xlo).then_inc(step_done, 1)

                want(li, s0)
                pe.wait_ge(ffn_read, at(li, 2 * KF, fi * KF))
                for k in range(KD):
                    square_in(li, 2 * fi, k)
                    pe.wait_ge(x_ready, at(li, 24, 16 * fi + k))
                    a, b = slab(s0, k)
                    ins = mm3(PS[:, 1, :], a, b, xhi[:, k, :], xlo[:, k, :], k == 0, k == KD - 1)
                ins.then_inc(step_done, 1)
                for c in range(1, 4):
                    in_step(c, 0)
                with pe.Fori(1, FFN_IN // 4) as i:
                    for c in range(4):
                        in_step(c, i)
                with pe.Fori(0, 2) as i:
                    for m in range(4):
                        pe.wait_ge(f_read, at(li, 24, 16 * fi + m) + i * 4)
                        for c in range(3):
                            s = s0 + FFN_IN + 3 * m + c
                            want(li, s, i, 12)
                            pe.wait_ge(hid_ready,
                                       past(li, 2 * KF, fi * KF + 8 * c + OUT_SLABS[c] - 1))
                            if m == 0 and c == 0:
                                pe.wait_ge(hid_ready, past(li, 2 * KF, fi * KF + KF - 1))
                            column(s, 4 + m, OUT_SLABS[c], hidhi, hidlo, 8 * c, c == 0,
                                   c == 2).then_inc(step_done, 1)
                postnorm(li, 2 * fi)

            with pe.Fori(0, DEPTH) as li:
                pe.wait_ge(layer_vecs, at(li, 1, 0))
                ffn(li, 0)
                for k in range(KD):
                    square_in(li, 1, k)
                bank_user = {}
                tile, rope, pending = 0, 0, []

                def rotate(bank=4):
                    c, r, src = pending.pop(0)
                    pe.wait_ge(fm_copied, at(li, NFM, c))
                    pe.wait_ge(roped, at(li, ROPED, r) + 1)
                    nc.tensor.matmul(PS[:, bank, :], cst[:, C_ROT:C_ROT + P], src, start=True,
                                     stop=True).then_inc(rot_mm, 1)

                def take(bank):
                    nonlocal tile
                    if bank in bank_user:
                        pe.wait_ge(fm_copied, at(li, NFM, bank_user[bank]))
                    bank_user[bank] = tile
                    tile += 1

                def fm_blocks(j, bank):
                    nonlocal rope
                    want(li, S_PROJ + j)
                    take(bank)
                    for k in range(KD):
                        if j == 0:
                            pe.wait_ge(x_ready, at(li, 24, 8 + k))
                        a, b = slab(S_PROJ + j, k)
                        ins = mm3(PS[:, bank, :], a, b, xhi[:, k, :], xlo[:, k, :], k == 0,
                                  k == KD - 1)
                        if k == KD - 1:
                            ins.then_inc(step_done, 1)
                            kind = plan[j][2][0]
                            if kind in ("iq", "aq", "bq", "bk", "misc"):
                                src = misc[:, :] if kind == "misc" else xr[:, rope % 2, :]
                                pending.append((tile - 1, rope, src))
                                rope += 1
                        yield

                def fm_step(j, bank):
                    for _ in fm_blocks(j, bank):
                        pass

                def go(blocks, n):
                    for _ in range(n):
                        next(blocks, None)

                def tm_blocks(j0, n, place):
                    for j in range(j0, j0 + 4):
                        s = S_PROJ + j
                        want(li, s)
                        for b in range(NB):
                            bank, col = place(b)
                            for k in (2 * (j - j0), 2 * (j - j0) + 1):
                                w = slice(k % 2 * n, (k % 2 + 1) * n)
                                ins = mm3(PS[:, bank, col:col + n], xhi[:, k, b * P:(b + 1) * P],
                                          xlo[:, k, b * P:(b + 1) * P], whi[:, s % PAIR, w],
                                          wlo[:, s % PAIR, w], k == 0 and col == 0,
                                          k == KD - 1 and (n == 512 or col > 0), n < 512)
                                if b == NB - 1 and k % 2:
                                    ins.then_inc(step_done, 1)
                                if n * (k % 2 + 1) >= 512:
                                    yield

                def attention(kind, q, kk, v, prob, blocks, per_item, before_blocks):
                    items, i0, g0 = ITEMS[kind], ITEM0[kind], GRP0[kind]
                    grp, before = g0, None

                    def scores(n):
                        back = 2 if kind == "a" else 1
                        if n >= back:
                            pe.wait_ge(score_read, at(li, NITEM, i0 + n - back))
                        _, b, segs = items[n]
                        banks = [n % 2] if kind == "a" else [0, 1, 2]
                        for bank, (qt, kt, half, first, nblk, _, _) in zip(banks, segs):
                            r = slice(half * HD, half * HD + HD)
                            ins = nc.tensor.matmul(
                                PS[:, bank, 0:nblk * P], q[r, qt, b * P:(b + 1) * P],
                                kk[r, kt, first * P:(first + nblk) * P], start=True, stop=True)
                        ins.then_inc(score_mm, 1)

                    def weigh(state):
                        hd, b, g, blks, first, last = state
                        pe.wait_ge(turned, at(li, NGRPS, g))
                        half = hd % 2
                        if first and b == 0 and hd >= 1:
                            pe.wait_ge(head_read, at(li, NHEAD, HEAD0[kind] + hd - 1))
                        for x, (_, kb, vcol) in enumerate(blks):
                            ins = nc.tensor.matmul(
                                PS[half * HD:half * HD + HD, 4, b * P:(b + 1) * P],
                                v[:, kb, vcol:vcol + HD], turn[:, g % 2, x * P:(x + 1) * P],
                                start=first and x == 0, stop=last and x == len(blks) - 1)
                        if last and b == NB - 1:
                            ins.then_inc(head_mm, 1)

                    scores(0)
                    scores(1)
                    for n, (hd, b, segs) in enumerate(items):
                        if n + 2 < len(items):
                            scores(n + 2)
                        pe.wait_ge(prob_ready, at(li, NITEM, i0 + n))
                        gs = groups_of(segs)
                        for x, blks in enumerate(gs):
                            if grp - g0 >= 2:
                                pe.wait_ge(turned, at(li, NGRPS, grp - 2))
                            for y, (col, _, _) in enumerate(blks):
                                ins = nc.tensor.matmul(
                                    PS[:, TURN[kind][grp % 2], y * P:(y + 1) * P],
                                    prob[:, n % PROBS, col:col + P], ident, start=True, stop=True,
                                    is_transpose=True)
                            ins.then_inc(turn_mm, 1)
                            if before is not None:
                                weigh(before)
                            before = (hd, b, grp, blks, x == 0, x == len(gs) - 1)
                            grp += 1
                            if x == 0:
                                before_blocks(n)
                            go(blocks, (x + 1) * per_item // len(gs) - x * per_item // len(gs))
                    weigh(before)

                for j in range(J_CKV):
                    fm_step(j, 5 + j % 3)
                    if j >= 1:
                        rotate()
                    if j == 3:
                        for b in range(NB):
                            ins = nc.tensor.matmul(PS[:, 1, b * 8:(b + 1) * 8],
                                                   misc[64:72, b * P:(b + 1) * P],
                                                   cst[64:72, C_ID + 64:C_ID + 72],
                                                   start=True, stop=True)
                        ins.then_inc(widx_mm, 1)
                rotate()

                def latent_blocks():
                    nonlocal tile, rope
                    yield from fm_blocks(J_CKV, 5 + J_CKV % 3)
                    for j in range(J_AQ, J_KA):
                        yield from fm_blocks(j, 5 + j % 3)
                    s = S_PROJ + J_KA
                    want(li, s)
                    pe.wait_ge(ckv_ready, at(li, 1, 0))
                    for t in range(4):
                        take((3, 5, 6, 7)[t])
                        a, b = slab(s, t)
                        ins = mm3(PS[:, (3, 5, 6, 7)[t], :], a, b, ckvhi[:, :], ckvlo[:, :], True,
                                  True)
                        if t == 3:
                            ins.then_inc(step_done, 1)
                        pending.append((tile - 1, rope, xr[:, rope % 2, :]))
                        rope += 1
                        yield
                    s = S_PROJ + J_VA
                    want(li, s)
                    for b in range(NB):
                        bank = (3, 5, 6, 7)[b]
                        pe.wait_ge(fm_copied, at(li, NFM, bank_user[bank]))
                        ins = mm3(PS[:, bank, :], ckvhi[:, b * P:(b + 1) * P],
                                  ckvlo[:, b * P:(b + 1) * P], whi[:, s % PAIR, 0:512],
                                  wlo[:, s % PAIR, 0:512], True, True)
                        if b == 3:
                            ins.then_inc(step_done, 1)
                        yield

                pe.wait_ge(widx_ready, at(li, 1, 0))
                pe.wait_ge(roped, at(li, ROPED, 4) + 2)
                pe.wait_ge(ik_copied, (li + 1) * 16)
                blocks = latent_blocks()
                for n in range(NIDX):
                    b, hd = n // 8, n % 8
                    r = slice((hd % 2) * HD, (hd % 2) * HD + HD)
                    if n >= 3:
                        pe.wait_ge(idx_relu, at(li, NIDX, n - 3))
                    nc.tensor.matmul(PS[:, n % 3, 0:(b + 1) * P], iq[r, hd // 2, b * P:(b + 1) * P],
                                     ik[r, 0, 0:(b + 1) * P], start=True,
                                     stop=True).then_inc(idx_mm, 1)
                    if n == IDX_DONE[J_CKV] + 2:
                        pe.wait_ge(ckv_f32, at(li, 1, 0))
                        sum_rows(3, sq[:, 0, :]).then_inc(ckv_sum, 1)
                    for j in range(J_AQ, J_KA):
                        if IDX_DONE[j] == n - 2:
                            rotate()
                    if IDX_DONE[J_KA] == n - 1:
                        for t in range(4):
                            rotate()
                    go(blocks, IDX_FILL)
                pe.wait_ge(tm_copied, at(li, 16, 3))
                for j in range(J_C, J_VC):
                    fm_step(j, 5 + j % 3)
                pe.wait_ge(idx_relu, at(li, NIDX, NIDX - 1))
                go(tm_blocks(J_VC, 512, lambda b: (b, 0)), 33)
                pe.wait_ge(fm_copied, at(li, NFM, tile - 1))
                for t in range(2):
                    ins = nc.tensor.matmul(PS[:, 6 + t, :], wal[96:112, t * P:(t + 1) * P],
                                           misc[96:112, :], start=True, stop=True)
                ins.then_inc(alpha_mm, 1)

                def b_blocks():
                    for j in range(J_B, J_VB):
                        if j == J_B + 1:
                            pe.wait_ge(alpha_min, at(li, 2, 1))
                        yield from fm_blocks(j, 5 + j % 2)

                def b_rotate(n):
                    for j in range(J_B, J_VB):
                        if rope_at(j) == n:
                            rotate(7)

                pe.wait_ge(tm_copied, at(li, 16, 7))
                pe.wait_ge(roped, at(li, ROPED, 12) + 2)
                pe.wait_ge(fm_copied, at(li, NFM, tile - 1))
                attention("a", aq, ak, va, prob_a, b_blocks(), A_FILL, b_rotate)
                b_rotate(len(ITEMS["a"]))
                pe.wait_ge(score_read, at(li, NITEM, ITEM0["b"] - 1))
                pe.wait_ge(decay_ready, at(li, 2, 1))
                pe.wait_ge(fm_copied, at(li, NFM, NFM - 1))
                pe.wait_ge(roped, at(li, ROPED, ROPED - 1) + 2)

                def key_end(b):
                    if b >= 2:
                        pe.wait_ge(kend_T, at(li, NB, b - 2))
                    for t in range(2):
                        ins = nc.tensor.matmul(PS[:, 6 + b % 2, t * P:(t + 1) * P],
                                               lb[:, t, b * P:(b + 1) * P], ident, start=True,
                                               stop=True, is_transpose=True)
                    ins.then_inc(kend_mm, 1)

                def key_value(n):
                    r = slice((n % 2) * CH, (n % 2) * CH + CH)
                    if n >= 2:
                        pe.wait_ge(kv_read, at(li, 7, n - 2))
                    for pr in range(2):
                        ins = nc.tensor.matmul(PS[:, 6 + n % 2, pr * 256:(pr + 1) * 256],
                                               kendT[r, n // 2, pr * P:(pr + 1) * P],
                                               vc[r, n // 2, pr * 256:(pr + 1) * 256],
                                               start=True, stop=True)
                    ins.then_inc(kv_mm, 1)

                def within(b):
                    if b >= 1:
                        pe.wait_ge(att_ready, at(li, NB, b - 1))
                    for hd in range(C_HEADS):
                        r = slice((hd % 2) * HD, (hd % 2) * HD + HD)
                        t = slice(b * P, (b + 1) * P)
                        ins = nc.tensor.matmul(PS[:, 4 + hd % 2, (hd // 2) * P:(hd // 2 + 1) * P],
                                               la[r, hd // 2, t], cq[r, hd // 2, t],
                                               start=True, stop=True)
                    ins.then_inc(att_mm, 1)

                def output(b):
                    pe.wait_ge(att_ready, at(li, NB, NB - 1))
                    for hd in range(C_HEADS):
                        r = slice((hd % 2) * HD, (hd % 2) * HD + HD)
                        ins = nc.tensor.matmul(PS[:, 4 + hd, b * P:(b + 1) * P],
                                               vc[:, b, hd * P:(hd + 1) * P],
                                               attT[b][:, hd % 2, (hd // 2) * P:
                                                    (hd // 2 + 1) * P],
                                               start=True, stop=False, skip_group_check=True)
                        for n in (2 * b, 2 * b + 1):
                            if n == 0:
                                continue
                            ins = nc.tensor.matmul(PS[:, 4 + hd, n * CH:(n + 1) * CH],
                                                   state[r, n, hd // 2, :],
                                                   cq[r, hd // 2, n * CH:(n + 1) * CH],
                                                   start=False, stop=n % 2 == 1,
                                                   skip_group_check=True)
                    if b == NB - 1:
                        ins.then_inc(o_mm, 1)

                values = tm_blocks(J_VB, 512, lambda b: (b, 0))
                for b in range(NB):
                    key_end(b)
                    go(values, 6)
                pe.wait_ge(kend_T, at(li, NB, NB - 1))
                for b in range(NB):
                    for n in (2 * b, 2 * b + 1):
                        if n < 7:
                            key_value(n)
                            go(values, 1)
                    within(b)
                go(values, 32)
                pe.wait_ge(kv_read, at(li, 7, 6))
                for b in range(NB):
                    output(b)
                pe.wait_ge(tm_copied, at(li, 16, 11))
                values = tm_blocks(J_VB + 4, 256, lambda b: (b // 2, b % 2 * 256))
                for hd in range(C_HEADS):
                    go(values, 4 if hd == 0 else 3)
                    pe.wait_ge(o_sq, at(li, C_HEADS, hd))
                    for b in range(NB):
                        ins = nc.tensor.matmul(PS[:, 2, hd * NB + b:hd * NB + b + 1],
                                               sq[:, hd % 2, b * P:(b + 1) * P], onesm[:, 0:1],
                                               start=True, stop=True)
                    ins.then_inc(o_sum, 1)
                go(values, 16)
                for hd in range(C_HEADS):
                    pe.wait_ge(diag_ready, at(li, C_HEADS, hd))
                    if hd >= 2:
                        pe.wait_ge(o_done, at(li, C_HEADS, hd - 2))
                    sum_rows(3 - hd % 2, diag[:, hd % 2, :, :].rearrange("p b n -> p (b n)")
                             ).then_inc(inv_mm, 1)
                pe.wait_ge(tm_copied, at(li, 16, 15))

                def a_blocks():
                    for m in range(KD):
                        for c in range(2):
                            s = S_MA + 2 * m + c
                            want(li, s)
                            if c == 0:
                                pe.wait_ge(gated_a, past(li, KD, m - 1))
                            else:
                                pe.wait_ge(merged_a, past(li, KD, m - 1))
                                pe.wait_ge(y_ready, at(li, 10, 3))
                            src = (xhi, xlo) if c == 0 else (yhi, ylo)
                            for k in range(A_SLABS[c]):
                                a, b = slab(s, k)
                                ins = mm3(PS[:, 5 + c, :], a, b, src[0][:, k, :], src[1][:, k, :],
                                          k == 0, k == A_SLABS[c] - 1)
                                if k == A_SLABS[c] - 1:
                                    ins.then_inc(step_done, 1)
                                yield

                pe.wait_ge(o_done, at(li, C_HEADS, 3))
                attention("b", bq, bk, vb, prob_b, a_blocks(), B_FILL, lambda n: None)
                with pe.Fori(0, 2) as i:
                    pe.wait_ge(score_read, at(li, NITEM, NITEM - 1))
                    pe.wait_ge(merged_a, past(li, KD, KD - 1))
                    pe.wait_ge(head_read, at(li, NHEAD, NHEAD - 1))
                    for m in range(4):
                        s = S_MBC + 3 * m
                        for c in range(2):
                            pe.wait_ge(gated, past(li, 16, 2 * m - 1) + i * 8)
                            want(li, s + c, i, 12)
                            column(s + c, c, 8, xhi, xlo).then_inc(step_done, 1)
                        pe.wait_ge(y_ready, at(li, 10, 9))
                        pe.wait_ge(merged, past(li, KD, m - 1) + i * 4)
                        want(li, s + 2, i, 12)
                        column(s + 2, 2, 4, yhi, ylo)
                        column(s + 2, 3, 2, ybhi, yblo, w0=4).then_inc(step_done, 1)
                with pe.Fori(0, 2) as i:
                    for m in range(4):
                        pe.wait_ge(merged, past(li, KD, KD - 1))
                        s = S_WOUT + m
                        pe.wait_ge(f_read, at(li, 24, 8 + m) + i * 4)
                        want(li, s, i, 4)
                        column(s, 4 + m, 8, mghi, mglo).then_inc(step_done, 1)
                postnorm(li, 1)
                ffn(li, 1)

        @block.vector
        def _(dve):
            lane = Lane(dve, order_v, "dve", per)
            did, ready = lane.did, lane.ready
            TT, TS, STT = (nc.vector.tensor_tensor, nc.vector.tensor_scalar,
                           nc.vector.scalar_tensor_tensor)
            dve.sem_inc(hid_ready, 1)
            dve.sem_inc(merged_a, 1)
            dve.sem_inc(merged, 1)
            dve.sem_inc(ffn_read, 2)
            dve.sem_inc(f_read, 4)
            dve.sem_inc(roped, 2)
            dve.wait_ge(consts_in, 16 * N_IN)

            def wait_step(li, s, i=0, per_iter=0):
                dve.wait_ge(step_done, at(li, NS, s) + i * per_iter + PAIR)

            ang, turns = sq[:, 0, :], sq[:, 1, :]
            TWO_PI = 2 * np.pi
            C1 = 6.28125
            C2 = float(np.float32(round((TWO_PI - C1) * 2 ** 20) / 2 ** 20))
            C3 = TWO_PI - C1 - C2
            MAGIC = 1.5 * 2.0 ** 23
            did(nc.vector.tensor_copy(ang, acc[:, :].bitcast(I32)))
            ready()
            did(TS(ang, ang, cst[:, C_FREQ:C_FREQ + 1], None, ALU.mult))
            ready()
            did(TS(turns, ang, 1 / TWO_PI, MAGIC, ALU.mult, ALU.add))
            ready()
            did(TS(turns, turns, -MAGIC, None, ALU.add))
            for c in (C1, C2, C3):
                ready()
                did(STT(out=ang, in0=turns, scalar=-c, in1=ang, op0=ALU.mult, op1=ALU.add))
            LIM = 3.1415925
            ready()
            did(TS(xt[:, 0, :], ang, LIM, -LIM, ALU.min, ALU.max))
            ready()
            did(TS(ang, ang, np.pi / 2, None, ALU.add))
            ready()
            did(TS(turns, ang, np.pi, -TWO_PI, ALU.is_gt, ALU.mult))
            ready()
            did(TT(ang, ang, turns, ALU.add))
            ready()
            did(TS(xt[:, 1, :], ang, LIM, -LIM, ALU.min, ALU.max), tables, 1)
            dve.wait_ge(tables_done, 2)
            dve.sem_inc(h_new, 8)

            def ffn_x(li, p, k):
                g = V_PRE[p] + k
                dve.wait_ge(x_hi, at(li, 24, 8 * p + k))
                did(STT(out=xlo[:, k, :], in0=h[:, k, :], scalar=vec[:, g:g + 1],
                        in1=xhi[:, k, :].bitcast(F32), op0=ALU.mult, op1=ALU.subtract),
                    x_ready, at(li, 24, 8 * p + k))

            def mixer_x(li):
                inverse(li, 2)

                def scaled(k):
                    g = V_PRE[1] + k
                    did(STT(out=xt[:, k % 2, :], in0=h[:, k, :], scalar=vec[:, g:g + 1],
                            in1=rstd[:, :], op0=ALU.mult, op1=ALU.mult), x_f32, at(li, 8, k))

                ready()
                scaled(0)
                scaled(1)
                for k in range(KD):
                    dve.wait_ge(x_hi, at(li, 24, 8 + k))
                    dve.wait_ge(x_f32, at(li, 8, k))
                    did(TT(xlo[:, k, :], xt[:, k % 2, :], xhi[:, k, :].bitcast(F32), ALU.subtract),
                        x_ready, at(li, 24, 8 + k))
                    if k + 2 < KD:
                        ready()
                        scaled(k + 2)

            def inverse(li, z):
                dve.wait_ge(std_ready, at(li, 6, z))
                ready()
                did(nc.vector.reciprocal(rstd[:, :], std[:, :]))

            def f_tile(li, q, m, i, bank):
                dve.wait_ge(fsq, at(li, 24, 8 * q + m) + i * 4)
                ready()
                did(TT(acc[:, :], acc[:, :], sq[:, m % 2, :], ALU.add))
                did(TS(f[:, bass.ds(i * 4 + m, 1), :], PS[:, bank:bank + 1, :], 1.0, None, ALU.mult),
                    f_read, at(li, 24, 8 * q + m) + i * 4 + 4)

            def postnorm(li, q, p):
                inverse(li, 2 * q + 1)
                ready()
                for k in range(KD):
                    g = V_POST[q] + k
                    did(STT(out=f[:, k, :], in0=f[:, k, :], scalar=vec[:, g:g + 1],
                            in1=rstd[:, :], op0=ALU.mult, op1=ALU.mult),
                        f_scaled, at(li, 24, 8 * q + k))
                    if p == 2 and k >= 3:
                        dve.wait_ge(h_new, at(li, 24, 8 * (q + 1) + k - 3))
                        ffn_x(li, p, k - 3)
                if p == 2:
                    for k in range(KD - 3, KD):
                        dve.wait_ge(h_new, at(li, 24, 8 * (q + 1) + k))
                        ffn_x(li, p, k)

            def ffn(li, fi):
                s0 = S_FFN[fi]
                inverse(li, 4 * fi)
                with lane.loop(f"ffn_in{fi}", FFN_IN // 4) as i:
                    for c in range(2):
                        t = fi * KF + c
                        wait_step(li, s0 + 2 * c, i, 4)
                        ready()
                        did(TT(silu[:, c, :], PS[:, 1 + 2 * c, :], rstd[:, :], ALU.mult),
                            gate_scaled, at(li, 2 * KF, t) + i * 2)
                        wait_step(li, s0 + 2 * c + 1, i, 4)
                        did(TT(hf[:, 0, :], PS[:, 2 + 2 * c, :], rstd[:, :], ALU.mult),
                            ffn_read, at(li, 2 * KF, t) + i * 2 + 2)
                        dve.wait_ge(silu_ready, at(li, 2 * KF, t) + i * 2)
                        ready()
                        did(TT(hf[:, 0, :], hf[:, 0, :], silu[:, c, :], ALU.mult))
                        j = i * 2 + c
                        ready()
                        did(TS(hidhi[:, bass.ds(j, 1), :], hf[:, :, :], 1.0, None, ALU.mult))
                        ready()
                        did(TT(hidlo[:, bass.ds(j, 1), :], hf[:, :, :],
                               hidhi[:, bass.ds(j, 1), :].bitcast(F32), ALU.subtract),
                            hid_ready, past(li, 2 * KF, t) + i * 2)
                ready()
                did(nc.vector.memset(acc[:, :], 0.0))
                with lane.loop(f"ffn_out{fi}", 2) as i:
                    for m in range(4):
                        f_tile(li, 2 * fi, m, i, 4 + m)

            rope_n = [0]

            def rope(li, c, dest, src, bank=4, rows=P):
                r = rope_n[0]
                rope_n[0] += 1
                dve.wait_ge(fm_copied, at(li, NFM, c))
                ready()
                did(TT(dest, src, cosT[0:rows, :], ALU.mult))
                dve.wait_ge(rot_mm, at(li, ROPED, r))
                did(TT(rt[0:rows, :], PS[0:rows, bank, :], sinT[0:rows, :], ALU.mult))
                ready()
                did(TT(dest, dest, rt[0:rows, :], ALU.add), roped, at(li, ROPED, r) + 2)

            def attention(li, kind, prob, st, out, between):
                items, i0 = ITEMS[kind], ITEM0[kind]
                grp_end = []
                grp = GRP0[kind]
                for _, _, segs in items:
                    grp += len(groups_of(segs))
                    grp_end.append(grp - 1)

                def masked(n):
                    hd, b, segs = items[n]
                    dve.wait_ge(score_mm, at(li, NITEM, i0 + n))
                    if n >= PROBS:
                        dve.wait_ge(turn_mm, at(li, NGRPS, grp_end[n - PROBS]))
                    col = 0
                    for g, (_, _, _, first, nblk, mask, _) in enumerate(segs):
                        w = nblk * P
                        bank = n % 2 if kind == "a" else g
                        m = score[:, b, 0:w] if mask is None else cst[:, mask:mask + w]
                        lane.settle()
                        one = len(segs) == 1
                        ins = nc.vector.tensor_tensor_reduce(
                            out=prob[:, n % PROBS, col:col + w], in0=PS[:, bank, 0:w], in1=m,
                            scale=-(HD ** -0.5), scalar=3.0e38, op0=ALU.add, op1=ALU.min,
                            accum_out=st[:, n % PROBS, 3:4] if one else st[:, n % PROBS, g:g + 1])
                        if one:
                            did(ins, score_read, at(li, NITEM, i0 + n))
                        else:
                            did(ins)
                        col += w
                    if not one:
                        ready()
                        did(nc.vector.tensor_reduce(st[:, n % PROBS, 3:4], st[:, n % PROBS, 0:3], AX.X,
                                                    ALU.min), score_read, at(li, NITEM, i0 + n))

                def normal(n):
                    hd, b, segs = items[n]
                    w = sum(s[4] for s in segs) * P
                    dve.wait_ge(exp_ready, at(li, NITEM, i0 + n))
                    total = st[:, n % PROBS, 4:5]
                    if len(segs) > 1:
                        ready()
                        did(nc.vector.tensor_reduce(st[:, n % PROBS, 7:8], st[:, n % PROBS, 4:7], AX.X,
                                                    ALU.add))
                        total = st[:, n % PROBS, 7:8]
                    ready()
                    did(nc.vector.reciprocal(st[:, n % PROBS, 8:9], total))
                    ready()
                    did(TS(prob[:, n % PROBS, 0:w], prob[:, n % PROBS, 0:w], st[:, n % PROBS, 8:9], None,
                           ALU.mult), prob_ready, at(li, NITEM, i0 + n))

                def take_head(hd):
                    r = slice((hd % 2) * HD, (hd % 2) * HD + HD)
                    dve.wait_ge(head_mm, at(li, NHEAD, HEAD0[kind] + hd))
                    ready()
                    did(nc.vector.tensor_copy(out[r, hd // 2, :], PS[r, 4, :]),
                        head_read, at(li, NHEAD, HEAD0[kind] + hd))

                masked(0)
                for n in range(len(items)):
                    if n + 1 < len(items):
                        masked(n + 1)
                    normal(n)
                    if n % NB == 0 and n:
                        take_head(n // NB - 1)
                    between(n)
                take_head(len(items) // NB - 1)
                between(len(items))

            with lane.loop("layer", DEPTH) as li:
                ready()
                did(TS(vec[:, :], vec2[:, bass.ds(li, 1), :].rearrange("p a n -> p (a n)"), 1.0,
                       None, ALU.mult))
                ready()
                did(TS(wal[96:112, :], wal2[96:112, bass.ds(li, 1), :].rearrange(
                    "p a n -> p (a n)"), 1.0, None, ALU.mult), layer_vecs, at(li, 1, 0))
                for k in range(KD):
                    ffn_x(li, 0, k)
                ffn(li, 0)
                postnorm(li, 0, 1)
                mixer_x(li)
                rope_n[0] = 0
                rope(li, 0, ik[0:HD, 0, :], misc[0:HD, :], rows=HD)
                for t in range(4):
                    if t == 1:
                        dve.wait_ge(widx_mm, at(li, 1, 0))
                        ready()
                        did(TS(widx[:, :], PS[:, 1, 0:32], 8 ** -0.5, None, ALU.mult),
                            widx_ready, at(li, 1, 0))
                    rope(li, 1 + t, iq[:, t, :], xr[:, (1 + t) % 2, :])

                def latent(n):
                    if n == IDX_DONE[J_CKV] + 5:
                        dve.wait_ge(ckv_std, at(li, 1, 0))
                        ready()
                        did(nc.vector.reciprocal(rstd[:, :], std[:, :]))
                        ready()
                        did(STT(out=ckv[:, :], in0=ckv[:, :], scalar=vec[:, V_KVN:V_KVN + 1],
                                in1=rstd[:, :], op0=ALU.mult, op1=ALU.mult), ckv_n, at(li, 1, 0))
                    if n == IDX_DONE[J_CKV] + 7:
                        dve.wait_ge(ckv_h, at(li, 1, 0))
                        ready()
                        did(TT(ckvlo[:, :], ckv[:, :], ckvhi[:, :].bitcast(F32), ALU.subtract),
                            ckv_ready, at(li, 1, 0))
                    for t in range(4):
                        if n == IDX_DONE[J_AQ + t] + 2:
                            rope(li, 6 + t, aq[:, t, :], xr[:, (5 + t) % 2, :])
                    if n == IDX_DONE[J_KA] + 1:
                        for t in range(4):
                            rope(li, 10 + t, ak[:, t, :], xr[:, (9 + t) % 2, :])

                for n in range(NIDX):
                    b, hd = n // 8, n % 8
                    w = (b + 1) * P
                    dve.wait_ge(idx_relu, at(li, NIDX, n))
                    ready()
                    wcol = widx[:, b * 8 + hd:b * 8 + hd + 1]
                    if hd == 0:
                        ins = TS(score[:, b, 0:w], relu[:, n % 2, 0:w], wcol, None, ALU.mult)
                    else:
                        ins = STT(out=score[:, b, 0:w], in0=relu[:, n % 2, 0:w], scalar=wcol,
                                  in1=score[:, b, 0:w], op0=ALU.mult, op1=ALU.add)
                    did(ins, idx_added, at(li, NIDX, n))
                    latent(n)
                cau = cst[:, C_CAU:C_CAU + P]
                ready()
                did(nc.vector.tensor_copy(score[:, 0, 0:P], cau))
                for b in range(1, NB):
                    w = (b + 1) * P
                    did(TT(score[:, b, b * P:w], score[:, b, b * P:w], cau, ALU.add))
                    for _ in range(TOPK // 8):
                        lane.settle()
                        did(nc.vector.max(top8[:, :], score[:, b, 0:w]))
                        lane.settle()
                        did(nc.vector.match_replace(score[:, b, 0:w], top8[:, :], score[:, b, 0:w],
                                                    TAKEN))
                    ready()
                    ins = TS(score[:, b, 0:w], score[:, b, 0:w], -1.0e38, NEG, ALU.is_gt, ALU.mult)
                    if b == NB - 1:
                        did(ins, bias_ready, at(li, 1, 0))
                    else:
                        did(ins)

                def decays(n):
                    if n == 0:
                        dve.wait_ge(alpha_abs, at(li, 2, 1))
                        for t in range(2):
                            did(TS(lb[:, t, :], PS[:, 6 + t, :], vec[:, V_BA + t:V_BA + t + 1],
                                   0.0, ALU.add, ALU.min), alpha_min, at(li, 2, t))
                        did(nc.vector.memset(keep[:, :], 1.0))
                        ready()
                        did(nc.vector.memset(keep[:, :].rearrange("p (n c) -> p n c", c=CH)
                                             [:, :, 0], 0.0))
                    for t in range(2):
                        if n == DECAY_AT - 1 + t:
                            dve.wait_ge(alpha_log, at(li, 2, t))
                            ready()
                            did(TT(la[:, t, :], lb[:, t, :], la[:, t, :], ALU.subtract))
                            ready()
                            did(nc.vector.tensor_tensor_scan(lb[:, t, :], keep[:, :], la[:, t, :],
                                                             0.0, ALU.mult, ALU.add))
                            ready()
                            did(TS(last[:, t, :], lb[:, t, :].rearrange("p (n c) -> p n c", c=CH)
                                   [:, :, CH - 1], 1.0, None, ALU.mult), decay_sum, at(li, 2, t))
                        if n == DECAY_AT + 1 + t:
                            dve.wait_ge(decay_b, at(li, 2, t))
                            ready()
                            for c0 in range(8):
                                c = slice(c0 * CH, (c0 + 1) * CH)
                                ins = TS(lb[:, t, c], lb[:, t, c], last[:, t, c0:c0 + 1], None,
                                         ALU.subtract)
                                if c0 < 7:
                                    did(ins)
                                else:
                                    did(ins, decay_l, at(li, 2, t))
                            did(TT(cq[:, t, :], eb[t][:, :], cq[:, t, :], ALU.mult))
                            did(TT(la[:, t, :], la[:, t, :], ck[:, t, :], ALU.mult))
                        if n == DECAY_AT + 3 + t:
                            dve.wait_ge(decay_exp, at(li, 2, t))
                            ready()
                            did(TT(lb[:, t, :], lb[:, t, :], ck[:, t, :], ALU.mult), decay_ready,
                                at(li, 2, t))

                def rope_b(n):
                    decays(n)
                    for j in range(J_B, J_VB):
                        if rope_at(j) == n:
                            t = j - J_B
                            dest = bq[:, t, :] if t < 6 else bk[:, t - 6, :]
                            rope(li, 22 + t, dest, xr[:, (13 + t) % 2, :], 7)

                attention(li, "a", prob_a, st_a, aq, rope_b)
                def next_state(n):
                    dve.wait_ge(kv_mm, at(li, 7, n))
                    ready()
                    for pr in range(2):
                        for half in range(2):
                            r = slice(half * HD, half * HD + HD)
                            kv = PS[r, 6 + n % 2, pr * 256 + half * P:pr * 256 + (half + 1) * P]
                            if n == 0:
                                ins = nc.vector.tensor_copy(state[r, 1, pr, :], kv)
                            else:
                                ins = STT(out=state[r, n + 1, pr, :], in0=state[r, n, pr, :],
                                          scalar=dec[r, pr, n:n + 1], in1=kv, op0=ALU.mult,
                                          op1=ALU.add)
                            if pr == 1 and half == 1:
                                did(ins, kv_read, at(li, 7, n))
                            else:
                                did(ins)

                for b in range(NB):
                    for n in (2 * b, 2 * b + 1):
                        if n < 7:
                            next_state(n)
                    dve.wait_ge(att_mm, at(li, NB, b))
                    did(TT(attT[b], PS[:, 4:6, 0:256],
                           cst[:, C_GLA:C_GLA + 512].rearrange("p (a n) -> p a n", a=2), ALU.mult),
                        att_ready, at(li, NB, b))
                dve.wait_ge(o_std, at(li, 1, 0))
                ready()
                did(nc.vector.reciprocal(inv[:, :], ms[:, :]))

                def diagonal(hd):
                    if hd >= 2:
                        dve.wait_ge(inv_mm, at(li, C_HEADS, hd - 2))
                    did(TT(diag[:, hd % 2, :, :], ident.unsqueeze(1).to_broadcast([P, NB, P]),
                           inv[:, hd * NB:(hd + 1) * NB].unsqueeze(2).to_broadcast([P, NB, P]),
                           ALU.mult), diag_ready, at(li, C_HEADS, hd))

                ready()
                diagonal(0)
                diagonal(1)
                for hd in range(C_HEADS):
                    did(TT(cg[:, hd, :], PS[:, 4 + hd, :], cg[:, hd, :], ALU.mult))
                    dve.wait_ge(inv_mm, at(li, C_HEADS, hd))
                    ready()
                    did(STT(out=cg[:, hd, :], in0=cg[:, hd, :], scalar=vec[:, V_CN:V_CN + 1],
                            in1=PS[:, 3 - hd % 2, :], op0=ALU.mult, op1=ALU.mult), o_done,
                        at(li, C_HEADS, hd))
                    if hd + 2 < C_HEADS:
                        diagonal(hd + 2)

                def split_y(t, dest, src, hi):
                    dve.wait_ge(y_hi, at(li, 10, t))
                    did(TT(dest, src, hi.bitcast(F32), ALU.subtract), y_ready, at(li, 10, t))

                for t in range(4):
                    split_y(t, ylo[:, t, :], aq[:, t, :], yhi[:, t, :])

                def merge_a(n):
                    for s in range(1, MERGE_A, 2):
                        if B_DONE[s] == n - 1:
                            m = s // 2
                            wait_step(li, S_MA + s)
                            dve.wait_ge(gated_a, past(li, KD, m))
                            did(TT(part[:, m, :], gate[:, m % 2, :], PS[:, 6, :], ALU.mult),
                                merged_a, past(li, KD, m))

                attention(li, "b", prob_b, st_b, bq, merge_a)
                for t in range(4):
                    split_y(4 + t, ylo[:, t, :], cg[:, t, :], yhi[:, t, :])
                for t in range(2):
                    split_y(8 + t, yblo[:, t, :], bq[:, t, :], ybhi[:, t, :])
                with lane.loop("merge", 2) as i:
                    ready()
                    did(TS(bgate[:, :], vec[:, bass.ds(i * 12 + V_BG, 12)], 1.0, None, ALU.mult),
                        gate_bias, at(li, 2, 0) + i)
                    for m in range(4):
                        j = i * 4 + m
                        wait_step(li, S_MBC + 3 * m + 2, i, 12)
                        dve.wait_ge(gated, past(li, 16, 2 * m + 1) + i * 8)
                        ready()
                        for c in range(2):
                            did(TT(gate[:, c, :], gate[:, c, :], PS[:, 2 + c, :], ALU.mult))
                        ready()
                        did(TT(gate[:, 0, :], gate[:, 0, :], gate[:, 1, :], ALU.add))
                        ready()
                        did(TT(gate[:, 0:1, :], gate[:, 0:1, :], part[:, bass.ds(j, 1), :], ALU.add))
                        ready()
                        did(TS(mghi[:, bass.ds(j, 1), :], gate[:, 0:1, :], 1.0, None, ALU.mult))
                        ready()
                        did(TT(mglo[:, bass.ds(j, 1), :], gate[:, 0:1, :],
                               mghi[:, bass.ds(j, 1), :].bitcast(F32), ALU.subtract),
                            merged, past(li, KD, m) + i * 4)
                ready()
                did(nc.vector.memset(acc[:, :], 0.0))
                with lane.loop("wout", 2) as i:
                    for m in range(4):
                        f_tile(li, 1, m, i, 4 + m)
                postnorm(li, 1, 2)
                ffn(li, 1)
                postnorm(li, 2, None)


def columns(w, tiles, kt):
    d = w.shape[0]
    w = w.reshape(d, kt, P, tiles, P).transpose(0, 3, 2, 1, 4)
    return np.ascontiguousarray(w).reshape(d, tiles, P, kt * P)


def rows(w, n, k2):
    d, r, _ = w.shape
    w = w.reshape(d, r // P // k2, k2, P, n).transpose(0, 1, 3, 2, 4)
    return np.ascontiguousarray(w).reshape(d, r // P // k2, P, k2 * n)


def ffn_in(w):
    w = columns(np.asarray(w), 2 * KF, KD).reshape(DEPTH, 2, KF, P, KD * P)
    return np.ascontiguousarray(w.transpose(0, 2, 1, 3, 4)).reshape(DEPTH, 2 * KF, P, KD * P)


def layout(x, positions, ffn1_pre_g, ffn1_w_in, ffn1_w_out, ffn1_post_g, mix_pre_g, w_in,
           a_kv_norm_g, a_w_kv_up, c_w_alpha_up, c_b_alpha, c_norm_g, w_branch_a, w_branch_b,
           w_branch_c, w_gate, b_gate, w_out, mix_post_g, ffn2_pre_g, ffn2_w_in, ffn2_w_out,
           ffn2_post_g):
    w = np.asarray(w_in)
    part = [w[:, :, OFF[i]:OFF[i + 1]] for i in range(len(SIZES))]
    aq, ackv, iq, ik, iw, bqkv, cq, ck, cv, cg, ca = part
    z = np.zeros
    misc = np.concatenate([ik, iw, z((DEPTH, DM, 24), w.dtype), ca, z((DEPTH, DM, 16), w.dtype)], 2)
    kv = np.asarray(a_w_kv_up).reshape(DEPTH, 1, P, A_HEADS, 2, HD)
    wk = kv[..., 0, :].reshape(DEPTH, 1, P, 512)
    wv = kv[..., 1, :].reshape(DEPTH, 1, P, 512)
    bq, bk, bv = bqkv[:, :, :768], bqkv[:, :, 768:1536], bqkv[:, :, 1536:]
    parts = [columns(np.concatenate([misc, iq, ackv, aq], 2), 10, KD), wk, wv,
             columns(np.concatenate([cq, ck, cg], 2), 8, KD), rows(cv, 512, 2),
             columns(np.concatenate([bq, bk], 2), 12, KD), rows(bv[:, :, :512], 512, 2),
             rows(bv[:, :, 512:], 256, 2)]
    proj = np.concatenate([np.concatenate([p, z(p.shape[:3] + (1024 - p.shape[3],), w.dtype)], 3)
                           for p in parts], 1)
    gates = columns(np.asarray(w_gate), 24, KD).reshape(DEPTH, 3, KD, P, KD * P)
    merge_a = np.concatenate([gates[:, 0], columns(np.asarray(w_branch_a), KD, 4)], 3)
    merge_bc = np.concatenate([gates[:, 2], gates[:, 1], columns(np.asarray(w_branch_c), KD, 4),
                               columns(np.asarray(w_branch_b), KD, 2)], 3)

    def vec(g):
        return np.asarray(g).reshape(DEPTH, -1, P).transpose(2, 0, 1)

    bg = np.asarray(b_gate).reshape(DEPTH, 3, KD, P).transpose(3, 0, 2, 1).reshape(P, DEPTH, 24)
    vecs = np.concatenate([vec(ffn1_pre_g), vec(ffn1_post_g), vec(mix_pre_g), vec(mix_post_g),
                           vec(ffn2_pre_g), vec(ffn2_post_g), vec(a_kv_norm_g), vec(c_norm_g),
                           vec(c_b_alpha), bg], 2)
    arrays = {
        "xT": np.asarray(x)[0].T, "positions": np.asarray(positions), "consts": constants(),
        "vecs": vecs, "walpha": np.asarray(c_w_alpha_up).transpose(1, 0, 2),
        "w_in1": ffn_in(ffn1_w_in), "w_out1": columns(np.asarray(ffn1_w_out), KD, KF),
        "w_proj": proj, "w_ma": merge_a, "w_mbc": merge_bc, "w_wout": columns(np.asarray(w_out), KD, KD),
        "w_in2": ffn_in(ffn2_w_in), "w_out2": columns(np.asarray(ffn2_w_out), KD, KF),
    }
    return {k: np.ascontiguousarray(v) for k, v in arrays.items()}


def kernel(**inputs):
    import concourse.bacc as bacc
    from concourse.bass_utils import run_bass_kernel_spmd

    arrays = layout(**inputs)

    def build(per):
        nc = bacc.Bacc("TRN2", target_bir_lowering=False, num_devices=1)
        args = [nc.dram_tensor(f"in_{k}", v.shape, mybir.dt.from_np(v.dtype),
                               kind="ExternalInput").ap() for k, v in arrays.items()]
        out = nc.dram_tensor("outT", (DM, SEQ), F32, kind="ExternalOutput").ap()
        trunk_kernel(nc, *args, out, per)
        return nc

    per = {}
    build(per)
    nc = build(per)
    r = run_bass_kernel_spmd(nc, [{f"in_{k}": v for k, v in arrays.items()}], core_ids=[0])
    return r.results[0]["outT"].T[None]
```

```python
from contextlib import ExitStack

import numpy as np
import concourse.bass as bass
from concourse import mybir

F32 = mybir.dt.float32
F32R = mybir.dt.float32r
I32 = mybir.dt.int32
ALU = mybir.AluOpType
ACT = mybir.ActivationFunctionType
AX = mybir.AxisListType

P = 128
DEPTH, SEQ, DM, DFF = 2, 512, 1024, 2816
HD, ROT, THETA, EPS = 64, 16, 500000.0, 1e-6
A_HEADS, B_HEADS, C_HEADS, GROUPS = 8, 4, 4, 3
TOPK = min(256, SEQ // 4)
KD = DM // P
KF = DFF // P
NB = SEQ // P
CH = 64
NEG = -1.0e30
TAKEN = -3.0e38
TAU = 16.0
SIZES = (512, 128, 512, 64, 8, 2304, 256, 256, 512, 512, 16)
OFF = [0] + np.cumsum(SIZES).tolist()

FFN_IN, FFN_OUT, PROJ, MERGE_A, MERGE_BC, WOUT = 2 * KF, 3 * KD, 44, 2 * KD, 3 * KD, KD
S_PROJ = FFN_IN + FFN_OUT
S_MA = S_PROJ + PROJ
S_MBC = S_MA + MERGE_A
S_WOUT = S_MBC + MERGE_BC
S_FFN = (0, S_WOUT + WOUT)
NS = S_FFN[1] + FFN_IN + FFN_OUT
RAW, PAIR = 4, 2
PROBS = 3
OUT_SLABS = (8, 8, 6)
OUT_BANKS = (5, 6, 7, 4)
A_SLABS = (8, 4)
BC_SLABS = (8, 8, 6)

V_PRE, V_POST = (0, 16, 32), (8, 24, 40)
V_KVN, V_CN, V_BA, V_BG = 48, 49, 50, 52
NV = V_BG + 24

(C_ID, C_ROT, C_ONE, C_G0, C_CAU, C_G1, C_G2, C_GLA) = (0, 128, 256, 384, 512, 640, 1152, 1664)
C_FREQ, C_EPS, C_EPS4, C_UNIT = 1792, 1793, 1794, 1795
NCST = 1796

ROPED = 25
NFM = 34


def constants():
    c = np.zeros((P, NCST), np.float32)
    c[:, C_ID:C_ID + P] = np.eye(P)
    for base in (0, HD):
        for d in range(ROT // 2):
            c[base + d + ROT // 2, C_ROT + base + d] = -1.0
            c[base + d, C_ROT + base + d + ROT // 2] = 1.0
            f = np.float32(THETA) ** np.float32(-2.0 * d / ROT)
            c[base + d, C_FREQ] = f
            c[base + d + ROT // 2, C_FREQ] = f
    c[:, C_ONE:C_ONE + P] = 1.0
    q, k = np.arange(P)[:, None], np.arange(P)[None, :]
    causal = k <= q
    c[:, C_CAU:C_CAU + P] = np.where(causal, 0, NEG)
    c[:, C_G0:C_G0 + P] = np.where(k >= q, 0, NEG)
    c[:, C_G0 + P:C_G0 + 2 * P] = np.where(causal, 0, NEG)
    for col, dil in ((C_G1, 4), (C_G2, 16)):
        same = (q - k) % dil == 0
        for b in range(3):
            c[:, col + b * P:col + (b + 1) * P] = np.where(same, 0, NEG)
        c[:, col + 3 * P:col + 4 * P] = np.where(same & causal, 0, NEG)
    intra = (q <= k) & (q // CH == k // CH)
    c[:, C_GLA:C_GLA + P] = intra
    c[:, C_EPS], c[:, C_EPS4], c[:, C_UNIT] = EPS, 4 * EPS, 1.0
    return c


def proj_plan():
    steps = [("fm", 8, ("misc", 0))]
    steps += [("fm", 8, ("iq", t)) for t in range(4)]
    steps += [("fm", 8, ("ckv", 0))]
    steps += [("fm", 8, ("aq", t)) for t in range(4)]
    steps += [("ka", 4, None), ("va", 4, None)]
    steps += [("fm", 8, ("cq", t)) for t in range(2)]
    steps += [("fm", 8, ("ck", t)) for t in range(2)]
    steps += [("fm", 8, ("cg", t)) for t in range(4)]
    steps += [("tm", 8, None)] * 4
    steps += [("fm", 8, ("bq", t)) for t in range(6)]
    steps += [("fm", 8, ("bk", t)) for t in range(6)]
    steps += [("tm", 8, None)] * 4 + [("tm", 4, None)] * 4
    assert len(steps) == PROJ
    return steps


J_CKV, J_AQ, J_KA, J_VA, J_C, J_VC, J_B, J_VB = 5, 6, 10, 11, 12, 20, 24, 36


def behind(n, first, total, items):
    def until(n):
        return first + (total - first) * (n + 1) // items
    return first if n < 0 else until(n) - until(n - 1)


def finished(steps, blocks, first, items):
    done, total, ends, n = {}, 0, [], -1
    reached = first
    for j, size in zip(steps, blocks):
        total += size
        while reached < total:
            n += 1
            reached += behind(n, first, sum(blocks), items)
        done[j] = n
    return done


SUM_AT, EXP_AT, REL_AT, END_AT, KEY_AT = (2, 5), (4, 7), (7, 10), (11, 12), (17, 18)
GATE_AT = 21

IDX_FILL, A_FILL, B_FILL = (9, 44, 26), (9, 96, 31), (12, 96, 15)
IDX_DONE = finished(range(J_CKV, J_VA), (8, 8, 8, 8, 8, 4), IDX_FILL[0], IDX_FILL[2])
KA_AT = IDX_DONE[J_KA] + 1
IDX_DONE[J_VA] = KA_AT + 3
A_DONE = finished(range(J_B, J_VB), (8,) * 12, A_FILL[0], A_FILL[2])
B_DONE = finished(range(MERGE_A), A_SLABS * KD, B_FILL[0], B_FILL[2])


def gate_at(m):
    return min(B_DONE[2 * m] + 2, B_HEADS * NB)


def rope_at(j):
    return min(A_DONE[j] + 3, A_HEADS * NB)


def place_b(head):
    return head if head < 2 * B_HEADS else head ^ 1


def attention_items(kind):
    items = []
    if kind == "a":
        for pair in range(A_HEADS // 2):
            for b in range(NB):
                for h in (2 * pair, 2 * pair + 1):
                    items.append((h, b, [(h // 2, h // 2, h % 2, 0, b + 1, None, h * HD)]))
        return items
    for h in range(B_HEADS):
        for b in range(NB):
            segs = []
            for g in range(GROUPS):
                head = g * B_HEADS + h
                first = max(b - 1, 0) if g == 0 else 0
                n = b + 1 - first
                end = (C_G0 + 2 * P, C_G1 + 4 * P, C_G2 + 4 * P)[g]
                at = place_b(head)
                segs.append((at // 2, at // 2, at % 2, first, n, end - n * P, head * HD))
            items.append((h, b, segs))
    return items


def groups_of(segs):
    blocks, col = [], 0
    for (_, _, _, first, n, _, vcol) in segs:
        for j in range(n):
            blocks.append((col, first + j, vcol))
            col += P
    return [blocks[i:i + 4] for i in range(0, len(blocks), 4)]


ITEMS = {"a": attention_items("a"), "b": attention_items("b")}
ITEM0 = {"a": 0, "b": len(ITEMS["a"])}
NITEM = len(ITEMS["a"]) + len(ITEMS["b"])
NGRP = {k: sum(len(groups_of(s)) for _, _, s in ITEMS[k]) for k in "ab"}
GRP0 = {"a": 0, "b": NGRP["a"]}
TURN = {"a": (2, 3), "b": (3, 7)}
NGRPS = NGRP["a"] + NGRP["b"]
PAIR0 = {"a": 0, "b": A_HEADS // 2}
NPAIR = (A_HEADS + B_HEADS) // 2
NIDX = NB * 8


class Lane:

    def __init__(self, eng, order, name, per):
        self.eng, self.order, self.name, self.per = eng, order, name, per
        self.turns, self.n, self.last = 0, 0, None

    def ready(self):
        if self.last is not None:
            self.eng.wait_ge(*self.last)

    def settle(self):
        self.ready()
        self.n += 1
        self.eng.sem_inc(self.order, 1)
        self.last = (self.order, self.turns + self.n)

    def did(self, ins, sem=None, value=None):
        if sem is None:
            sem, self.n = self.order, self.n + 1
            value = self.turns + self.n
        ins.then_inc(sem, 1)
        self.last = (sem, value)

    def fence(self):
        if self.last is None or self.last[0] is not self.order:
            self.settle()

    def loop(self, key, stop, start=0):
        return _Loop(self, (self.name, key), start, stop)


class _Loop:
    def __init__(self, lane, key, start, stop):
        self.lane, self.key, self.start, self.stop = lane, key, start, stop

    def __enter__(self):
        lane = self.lane
        lane.fence()
        self.turns, self.n = lane.turns, lane.n
        self.cm = lane.eng.Fori(self.start, self.stop)
        i = self.cm.__enter__()
        per = lane.per.get(self.key, 0)
        lane.turns = self.turns + i * per
        lane.n -= self.start * per
        lane.last = (lane.order, lane.turns + lane.n)
        return i

    def __exit__(self, *exc):
        lane = self.lane
        lane.fence()
        lane.per[self.key] = lane.n - self.n + self.start * lane.per.get(self.key, 0)
        self.cm.__exit__(*exc)
        lane.turns = self.turns
        lane.n = self.n + (self.stop - self.start) * lane.per[self.key]
        lane.last = (lane.order, lane.turns + lane.n)


def trunk_kernel(nc, xT, positions, consts, vecs, walpha, w_in1, w_out1, w_proj, w_ma, w_mbc, w_wout,
                 w_in2, w_out2, outT, per):
    ctx = ExitStack()
    with ctx:
        def sb(name, shape, dt=F32, scope=ctx):
            return scope.enter_context(nc.sbuf_tensor(name, shape, dt))

        def sem(name):
            return ctx.enter_context(nc.semaphore(name))

        h = sb("h", [P, KD, SEQ])
        xhi = sb("xhi", [P, KD, SEQ], F32R)
        with ExitStack() as s:
            f = sb("f", [P, KD, SEQ], F32, s)
        xlo = sb("xlo", [P, KD, SEQ], F32R)
        wraw = sb("wraw", [P, RAW, 1024])
        whi = sb("whi", [P, PAIR, 1024], F32R)
        wlo = sb("wlo", [P, PAIR, 1024], F32R)
        cst = sb("cst", [P, NCST])
        cosT = sb("cosT", [P, SEQ])
        sinT = sb("sinT", [P, SEQ])
        cosr = sb("cosr", [P, SEQ])
        sinr = sb("sinr", [P, SEQ])
        vec2 = sb("vec2", [P, DEPTH, NV])
        vec = sb("vec", [P, NV])
        bgate = sb("bgate", [P, 12])
        wal = sb("wal", [P, 256])
        sq = sb("sq", [P, 2, SEQ])
        acc = sb("acc", [P, SEQ])
        xdiag = sb("xdiag", [P, NB, P])
        rstd = sb("rstd", [P, SEQ])
        xinv = sb("xinv", [P, NB])
        spare = sb("spare", [P, 1])
        xt = sb("xt", [P, 2, SEQ])
        last = sb("last", [P, 2, 8])
        dec = sb("dec", [P, 2, 8])
        ms = sb("ms", [P, C_HEADS * NB])
        inv = sb("inv", [P, C_HEADS * NB])

        with ExitStack() as s:
            hidhi = sb("hidhi", [P, KF, SEQ], F32R, s)
            hidlo = sb("hidlo", [P, KF, SEQ], F32R, s)
            silu = sb("silu", [P, 2, SEQ], F32, s)
            hf = sb("hf", [P, 1, SEQ], F32, s)
        misc = sb("misc", [P, SEQ])
        with ExitStack() as s:
            yhi = sb("yhi", [P, 4, SEQ], F32R, s)
            ylo = sb("ylo", [P, 4, SEQ], F32R, s)
        cq = sb("cq", [P, 2, SEQ])
        ck = sb("ck", [P, 2, SEQ])
        vc = sb("vc", [P, NB, 512])
        with ExitStack() as s:
            mghi = sb("mghi", [P, KD, SEQ], F32R, s)
            mglo = sb("mglo", [P, KD, SEQ], F32R, s)
        part = sb("part", [P, KD, SEQ])
        aq = part[:, 4:KD, :]
        cg = sb("cg", [P, 4, SEQ])
        with ExitStack() as s:
            iq = sb("iq", [P, 4, SEQ], F32, s)
            ik = sb("ik", [P, 1, SEQ], F32, s)
            relu = sb("relu", [P, 2, SEQ], F32, s)
            ckv = sb("ckv", [P, SEQ], F32, s)
            ckvhi = sb("ckvhi", [P, SEQ], F32R, s)
            ckvlo = sb("ckvlo", [P, SEQ], F32R, s)
            widx = sb("widx", [P, NB * 8], F32, s)
        bq = sb("bq", [P, 6, SEQ])
        bk = sb("bk", [P, 6, SEQ])
        with ExitStack() as s:
            ak = sb("ak", [P, 4, SEQ], F32, s)
            va = sb("va", [P, NB, 512], F32, s)
            score = sb("score", [P, NB, SEQ], F32, s)
            prob_a = sb("prob_a", [P, PROBS, 512], F32, s)
            st_a = sb("st_a", [P, PROBS, 16], F32, s)
            top8 = sb("top8", [P, 8], F32, s)
        with ExitStack() as s:
            ybhi = sb("ybhi", [P, 2, SEQ], F32R, s)
            yblo = sb("yblo", [P, 2, SEQ], F32R, s)
        vb = sb("vb", [P, NB, 768])
        with ExitStack() as s:
            kendT = sb("kendT", [P, NB, 256], F32, s)
            state = sb("state", [P, 8, 2, P], F32, s)
        prob_b = sb("prob_b", [P, PROBS, 1280])
        st_b = sb("st_b", [P, PROBS, 16])
        xr, rt, turn, gate = xt, acc, sq, xt
        attT = [b[:, j, :].rearrange("p (a n) -> p a n", a=2) for b in (xt, sq) for j in (0, 1)]
        diag = xt[:, :, :].rearrange("p a (b n) -> p a b n", n=P)
        PS = ctx.enter_context(nc.psum_tensor("PS", [P, 8, 512], F32))

        la = part[:, 0:2, :]
        lb = part[:, 2:4, :]
        xd = xdiag[:, :, :].rearrange("p b n -> p (b n)")
        eb = (xd, misc)
        keep = misc

        ident = cst[:, C_ID:C_ID + P]
        onesm = cst[:, C_ONE:C_ONE + P]

        raw_loaded = [sem(f"raw_loaded{i}") for i in range(RAW)]
        w_hi = sem("w_hi")
        w_ready = sem("w_ready")
        step_done = sem("step_done")
        angles_in = sem("angles_in")
        x_in = sem("x_in")
        consts_in = sem("consts_in")
        order_v, order_s = sem("order_v"), sem("order_s")
        tables = sem("tables")
        tables_done = sem("tables_done")
        layer_vecs = sem("layer_vecs")
        h_new = sem("h_new")
        f_scaled = sem("f_scaled")
        hsq = sem("hsq")
        hsq_added = sem("hsq_added")
        hsum_mm = sem("hsum_mm")
        xdiag_ready = sem("xdiag_ready")
        rms_mm = sem("rms_mm")
        walpha_in = sem("walpha_in")
        cg_scaled = sem("cg_scaled")
        agate_scaled = sem("agate_scaled")
        mgate_scaled = sem("mgate_scaled")
        fsum_mm = sem("fsum_mm")
        std_ready = sem("std_ready")
        x_ready = sem("x_ready")
        x_hi = sem("x_hi")
        gate_scaled = sem("gate_scaled")
        silu_ready = sem("silu_ready")
        ffn_read = sem("ffn_read")
        hid_ready = sem("hid_ready")
        fsq = sem("fsq")
        fsq_added = sem("fsq_added")
        f_read = sem("f_read")
        fm_copied = sem("fm_copied")
        rot_mm = sem("rot_mm")
        roped = sem("roped")
        tm_copied = sem("tm_copied")
        ckv_f32, ckv_sq, ckv_sum, ckv_std = (sem("ckv_f32"), sem("ckv_sq"), sem("ckv_sum"),
                                             sem("ckv_std"))
        ckv_diag, ckv_inv = sem("ckv_diag"), sem("ckv_inv")
        ckv_n, ckv_h, ckv_ready = sem("ckv_n"), sem("ckv_h"), sem("ckv_ready")
        widx_mm, widx_ready = sem("widx_mm"), sem("widx_ready")
        ik_copied = sem("ik_copied")
        idx_mm, idx_relu, idx_added = sem("idx_mm"), sem("idx_relu"), sem("idx_added")
        bias_ready = sem("bias_ready")
        score_mm = sem("score_mm")
        score_read = sem("score_read")
        exp_ready = sem("exp_ready")
        prob_ready = sem("prob_ready")
        turn_mm = sem("turn_mm")
        turned = sem("turned")
        head_mm = sem("head_mm")
        head_read = sem("head_read")
        alpha_mm, alpha_abs, alpha_log, alpha_min = (sem("alpha_mm"), sem("alpha_abs"),
                                                     sem("alpha_log"), sem("alpha_min"))
        decay_sum, decay_exp, decay_ready = sem("decay_sum"), sem("decay_exp"), sem("decay_ready")
        decay_b, decay_l = sem("decay_b"), sem("decay_l")
        kend_mm, kend_T = sem("kend_mm"), sem("kend_T")
        kv_mm, kv_read = sem("kv_mm"), sem("kv_read")
        att_mm, att_ready = sem("att_mm"), sem("att_ready")
        o_mm, o_sq, o_sum, o_std, o_done = (sem("o_mm"), sem("o_sq"), sem("o_sum"), sem("o_std"),
                                            sem("o_done"))
        diag_ready = sem("diag_ready")
        inv_mm = sem("inv_mm")
        y_hi, y_ready = sem("y_hi"), sem("y_ready")
        gate_bias = sem("gate_bias")
        gated = sem("gated")
        merged_a = sem("merged_a")
        gated_a = sem("gated_a")
        merged = sem("merged")
        out_done = sem("out_done")

        def at(li, per_layer, n):
            return li * per_layer + (n + 1)

        def past(li, per_layer, n):
            return li * per_layer + (n + 2)

        block = ctx.enter_context(nc.Block())

        @block.sync
        def _(sp):
            sp.dma_start(acc[:, :].bitcast(I32),
                         positions.to_broadcast([P, SEQ])).then_inc(angles_in, 16)
            sp.dma_start(cst[:, C_FREQ:NCST], consts[:, C_FREQ:NCST]).then_inc(angles_in, 16)
            sp.dma_start(vec2[:, :, :], vecs).then_inc(x_in, 16)
            for k in range(KD):
                sp.dma_start(h[:, k, :], xT[k * P:(k + 1) * P, :]).then_inc(x_in, 16)

            def load(li, s, src, i=0, per_iter=0):
                n = src.shape[-1]
                sp.wait_ge(w_ready, at(li, NS, s) + i * per_iter)
                sp.dma_start(wraw[:, s % RAW, 0:n], src).then_inc(raw_loaded[s % RAW], 16)

            def ffn(li, s0, w1, w2):
                with sp.Fori(0, FFN_IN // RAW) as i:
                    for c in range(RAW):
                        load(li, s0 + c, w1[li, i * RAW + c, :, :], i, RAW)
                with sp.Fori(0, 2) as i:
                    for m in range(4):
                        for c in range(3):
                            load(li, s0 + FFN_IN + 3 * m + c,
                                 w2[li, i * 4 + m, :, c * 1024:c * 1024 + OUT_SLABS[c] * P], i, 12)

            with sp.Fori(0, DEPTH) as li:
                ffn(li, S_FFN[0], w_in1, w_out1)
                sp.dma_start(wal[96:112, :], walpha[:, li, :]).then_inc(walpha_in, 16)
                for j, (_, slabs, _) in enumerate(proj_plan()):
                    load(li, S_PROJ + j, w_proj[li, j, :, 0:slabs * P])
                with sp.Fori(0, 2) as i:
                    for m in range(4):
                        for c in range(2):
                            load(li, S_MA + 2 * m + c,
                                 w_ma[li, i * 4 + m, :, c * 1024:c * 1024 + A_SLABS[c] * P], i, 8)
                with sp.Fori(0, 2) as i:
                    for m in range(4):
                        for c in range(3):
                            load(li, S_MBC + 3 * m + c,
                                 w_mbc[li, i * 4 + m, :, c * 1024:c * 1024 + BC_SLABS[c] * P], i, 12)
                with sp.Fori(0, 2) as i:
                    for c in range(4):
                        load(li, S_WOUT + c, w_wout[li, i * 4 + c, :, :], i, 4)
                ffn(li, S_FFN[1], w_in2, w_out2)
            for c in range(PAIR):
                load(DEPTH, c, w_in1[0, c, :, :])
            for k in range(KD):
                sp.wait_ge(h_new, 8 * 3 * DEPTH + k + 1)
                sp.dma_start(outT[k * P:(k + 1) * P, :], h[:, k, :]).then_inc(out_done, 16)
            sp.wait_ge(out_done, 16 * KD)

        @block.gpsimd
        def _(pool):
            pool.sem_inc(w_ready, RAW)

            def split(li, s, slabs, i=0, per_iter=0):
                n = slabs * P
                pool.wait_ge(w_hi, at(li, NS, s) + i * per_iter)
                nc.gpsimd.tensor_tensor(wlo[:, s % PAIR, 0:n], wraw[:, s % RAW, 0:n],
                                        whi[:, s % PAIR, 0:n].bitcast(F32),
                                        ALU.subtract).then_inc(w_ready, 1)

            def ffn(li, s0):
                with pool.Fori(0, FFN_IN // RAW) as i:
                    for c in range(RAW):
                        split(li, s0 + c + 2, 8, i, RAW)
                with pool.Fori(0, 2) as i:
                    for n in range(12):
                        split(li, s0 + FFN_IN + n + 2, OUT_SLABS[(n + 2) % 3], i, 12)

            def add_f(li, q):
                for k in range(KD):
                    pool.wait_ge(f_scaled, at(li, 24, 8 * q + k))
                    nc.gpsimd.tensor_tensor(h[:, k, :], h[:, k, :], f[:, k, :],
                                            ALU.add).then_inc(h_new, 1)

            plan = proj_plan()
            split(0, 0, 8)
            split(0, 1, 8)
            with pool.Fori(0, DEPTH) as li:
                ffn(li, S_FFN[0])
                add_f(li, 0)
                for j in range(PROJ):
                    split(li, S_PROJ + j + 2, plan[j + 2][1] if j + 2 < PROJ else
                          A_SLABS[j + 2 - PROJ])
                for n in range(MERGE_A):
                    split(li, S_MA + n + 2, A_SLABS[n % 2] if n + 2 < MERGE_A else 8)
                with pool.Fori(0, 2) as i:
                    for n in range(12):
                        split(li, S_MBC + n + 2, BC_SLABS[(n + 2) % 3], i, 12)
                with pool.Fori(0, 2) as i:
                    for c in range(4):
                        split(li, S_WOUT + c + 2, 8, i, 4)
                add_f(li, 1)
                ffn(li, S_FFN[1])
                add_f(li, 2)

        @block.scalar
        def _(act):
            lane = Lane(act, order_s, "act", per)
            did, ready = lane.did, lane.ready
            act.sem_inc(gated, 1)
            act.sem_inc(gated_a, 1)
            act.sem_inc(hsq, 1)

            def hi(li, s, slabs, i=0, per_iter=0):
                n, slot = slabs * P, s % RAW
                loads = li * (NS // RAW) + i * (per_iter // RAW) + s // RAW
                act.wait_ge(raw_loaded[slot], (loads + 1) * 16)
                act.wait_ge(step_done, at(li, NS, s) + i * per_iter)
                ready()
                did(nc.scalar.activation(whi[:, s % PAIR, 0:n], wraw[:, slot, 0:n], ACT.Copy),
                    w_hi, at(li, NS, s) + i * per_iter)

            def wait_step(li, s, i=0, per_iter=0):
                act.wait_ge(step_done, at(li, NS, s) + i * per_iter + PAIR)

            def prenorm(li, p, s0):
                def square(k):
                    act.wait_ge(hsq_added, at(li, 24, 8 * p + k))
                    ready()
                    did(nc.scalar.activation(sq[:, k % 2, :], h[:, k, :], ACT.Square),
                        hsq, past(li, 24, 8 * p + k))

                for k in range(KD):
                    g = V_PRE[p] + k
                    act.wait_ge(h_new, at(li, 24, 8 * p + k))
                    did(nc.scalar.activation(xhi[:, k, :], h[:, k, :], ACT.Copy,
                                             scale=vec[:, g:g + 1]), x_hi, at(li, 24, 8 * p + k))
                square(0)
                square(1)
                wait_step(li, s0)
                hi(li, s0 + 2, 8)
                for k in range(2, KD):
                    square(k)
                wait_step(li, s0 + 1)
                hi(li, s0 + 3, 8)
                act.wait_ge(hsum_mm, at(li, 3, p))
                root(li, 2 * p, C_EPS, 1.0)

            def root(li, z, eps, scale):
                ready()
                did(nc.scalar.activation(ms[:, 0:NB], PS[:, 0, 0:NB], ACT.Sqrt,
                                         bias=cst[:, eps:eps + 1], scale=scale / DM),
                    std_ready, at(li, 6, z))

            def load_sqrt():
                ready()
                did(nc.scalar.activation(spare[:, :], cst[:, C_UNIT:C_UNIT + 1], ACT.Sqrt))

            def f_root(li, q, eps, scale):
                act.wait_ge(fsum_mm, at(li, 3, q))
                root(li, 2 * q + 1, eps, scale)

            def f_square(li, q, m, i, bank):
                act.wait_ge(f_read, at(li, 24, 8 * q + m) + i * 4 + 2)
                ready()
                did(nc.scalar.activation(sq[:, m % 2, :], PS[:, bank, :], ACT.Square),
                    fsq, at(li, 24, 8 * q + m) + i * 4)

            def ffn(li, fi):
                s0 = S_FFN[fi]

                def gate(c, i=0):
                    act.wait_ge(gate_scaled, at(li, 2 * KF, fi * KF + c) + i * 2)
                    did(nc.scalar.activation(silu[:, c, :], silu[:, c, :], ACT.Silu),
                        silu_ready, at(li, 2 * KF, fi * KF + c) + i * 2)

                prenorm(li, 2 * fi, s0)
                for c in range(2):
                    wait_step(li, s0 + c + 2)
                    hi(li, s0 + c + 4, 8)
                    gate(c)
                with lane.loop(f"ffn_in{fi}", FFN_IN // 4, 1) as i:
                    for c in range(4):
                        wait_step(li, s0 + c, i, 4)
                        hi(li, s0 + c + 2, 8, i, 4)
                        if c % 2 == 0:
                            gate(c // 2, i)
                load_sqrt()
                with lane.loop(f"ffn_out{fi}", 2) as i:
                    for m in range(4):
                        for c in range(3):
                            n = 3 * m + c
                            wait_step(li, s0 + FFN_IN + n, i, 12)
                            if c == 2:
                                f_square(li, 2 * fi, m, i, OUT_BANKS[m])
                            hi(li, s0 + FFN_IN + n + 2, OUT_SLABS[(n + 2) % 3], i, 12)
                f_root(li, 2 * fi, C_EPS4, 4.0)

            plan = proj_plan()

            def roll(li, j):
                wait_step(li, S_PROJ + j)
                hi(li, S_PROJ + j + 2, plan[j + 2][1] if j + 2 < PROJ else A_SLABS[j + 2 - PROJ])

            class Fm:
                tile = 0
                rope = 0

            def copy_fm(li, kind, t, bank):
                c = Fm.tile
                Fm.tile += 1
                ready()
                if kind in ("iq", "aq", "ak", "bq", "bk"):
                    r = Fm.rope
                    Fm.rope += 1
                    act.wait_ge(roped, at(li, ROPED, r))
                    ins = nc.scalar.activation(xr[:, r % 2, :], PS[:, bank, :], ACT.Copy)
                elif kind == "misc":
                    Fm.rope += 1
                    ins = nc.scalar.activation(misc[:, :], PS[:, bank, :], ACT.Copy)
                elif kind == "ckv":
                    ins = nc.scalar.activation(ckv[:, :], PS[:, bank, :], ACT.Copy)
                elif kind == "cq":
                    ins = nc.scalar.activation(cq[:, t, :], PS[:, bank, :], ACT.Copy, scale=HD ** -0.5)
                elif kind == "ck":
                    ins = nc.scalar.activation(ck[:, t, :], PS[:, bank, :], ACT.Copy)
                else:
                    ins = nc.scalar.activation(cg[:, t, :], PS[:, bank, :], ACT.Copy)
                did(ins, fm_copied, at(li, NFM, c))

            def copy_tm(li, g, dest, col, n, place=lambda b: (b, 0)):
                for b in range(NB):
                    bank, c = place(b)
                    ready()
                    did(nc.scalar.activation(dest[:, b, col:col + n], PS[:, bank, c:c + n], ACT.Copy,
                                             scale=1.0 if dest is va else xinv[:, b:b + 1]),
                        tm_copied, at(li, 16, 4 * g + b))

            def attention(li, kind, prob, st, between):
                items, i0, g0 = ITEMS[kind], ITEM0[kind], GRP0[kind]

                def exponentials(n):
                    col = 0
                    act.wait_ge(score_read, at(li, NITEM, i0 + n))
                    for g, seg in enumerate(items[n][2]):
                        w = seg[4] * P
                        ins = nc.scalar.activation(prob[:, n % PROBS, col:col + w],
                                                   prob[:, n % PROBS, col:col + w], ACT.Exp,
                                                   bias=st[:, n % PROBS, 3:4], scale=-1.0,
                                                   accum_out=st[:, n % PROBS, 4 + g:5 + g])
                        if g == len(items[n][2]) - 1:
                            did(ins, exp_ready, at(li, NITEM, i0 + n))
                        else:
                            did(ins)
                        col += w

                grp = g0
                exponentials(0)
                for n in range(len(items)):
                    between(n)
                    if n + 1 < len(items):
                        exponentials(n + 1)
                    for blocks in groups_of(items[n][2]):
                        w = len(blocks) * P
                        act.wait_ge(turn_mm, at(li, NGRPS, grp))
                        ready()
                        did(nc.scalar.activation(turn[:, grp % 2, 0:w],
                                                 PS[:, TURN[kind][grp % 2], 0:w], ACT.Copy),
                            turned, at(li, NGRPS, grp))
                        grp += 1
                between(len(items))

            hi(0, 0, 8)
            hi(0, 1, 8)
            act.wait_ge(x_in, 16 * (KD + 1))
            act.dma_start(cst[:, 0:C_FREQ], consts[:, 0:C_FREQ]).then_inc(consts_in, 16)
            act.wait_ge(tables, 1)
            did(nc.scalar.activation(sinT[:, :], xt[:, 0, :], ACT.Sin), tables_done, 1)
            ready()
            did(nc.scalar.activation(cosT[:, :], xt[:, 1, :], ACT.Sin), tables_done, 2)
            with lane.loop("layer", DEPTH) as li:
                act.wait_ge(layer_vecs, at(li, 1, 0))
                ffn(li, 0)
                prenorm(li, 1, S_PROJ)
                Fm.tile = Fm.rope = 0
                for j in range(J_CKV):
                    if j >= 2:
                        roll(li, j)
                    copy_fm(li, *plan[j][2], 5 + j % 3)
                    if j == 3:
                        act.wait_ge(roped, at(li, ROPED, 0) + 2)
                        act.dma_start(ik[HD:P, 0, :], ik[0:HD, 0, :]).then_inc(ik_copied, 16)

                def latent(n):
                    for j in range(J_CKV, J_C):
                        if IDX_DONE[j] != n - 1:
                            continue
                        if j == J_VA:
                            wait_step(li, S_PROJ + j)
                            copy_tm(li, 0, va, 0, 512, lambda b: ((3, 5, 6, 7)[b], 0))
                        roll(li, j)
                        if j == J_KA:
                            copy_fm(li, "ak", 0, 3)
                            copy_fm(li, "ak", 1, 5)
                        elif j != J_VA:
                            copy_fm(li, *plan[j][2], 5 + j % 3)
                    if n == KA_AT + 2:
                        copy_fm(li, "ak", 2, 6)
                    if n == KA_AT + 3:
                        copy_fm(li, "ak", 3, 7)
                    if n == IDX_DONE[J_CKV] + 3:
                        act.wait_ge(ckv_f32, at(li, 1, 0))
                        did(nc.scalar.activation(sq[:, 0, :], ckv[:, :], ACT.Square), ckv_sq,
                            at(li, 1, 0))
                    if n == IDX_DONE[J_CKV] + 6:
                        act.wait_ge(ckv_sum, at(li, 1, 0))
                        did(nc.scalar.activation(ms[:, 0:NB], PS[:, 3, 0:NB], ACT.Sqrt,
                                                 bias=cst[:, C_EPS:C_EPS + 1], scale=1.0 / P),
                            ckv_std, at(li, 1, 0))
                    if n == IDX_DONE[J_CKV] + 10:
                        act.wait_ge(ckv_n, at(li, 1, 0))
                        did(nc.scalar.activation(ckvhi[:, :], ckv[:, :], ACT.Copy), ckv_h,
                            at(li, 1, 0))

                for n in range(NIDX):
                    w = (n // 8 + 1) * P
                    act.wait_ge(idx_mm, at(li, NIDX, n))
                    if n >= 2:
                        act.wait_ge(idx_added, at(li, NIDX, n - 2))
                    did(nc.scalar.activation(relu[:, n % 2, 0:w], PS[:, n % 3, 0:w], ACT.Relu,
                                             scale=(8 * HD) ** -0.5), idx_relu, at(li, NIDX, n))
                    latent(n)
                for j in range(J_C, J_B):
                    if j == J_B - 1:
                        wait_step(li, S_PROJ + j)
                        copy_tm(li, 1, vc, 0, 512)
                    roll(li, j)
                    if j < J_VC:
                        copy_fm(li, *plan[j][2], 5 + j % 3)
                    if j == J_VC:
                        act.wait_ge(alpha_mm, at(li, 1, 0))
                        for t in range(2):
                            did(nc.scalar.activation(la[:, t, :], PS[:, 6 + t, :], ACT.Abs,
                                                     bias=vec[:, V_BA + t:V_BA + t + 1]),
                                alpha_abs, at(li, 2, t))
                        ready()
                        for t in range(2):
                            did(nc.scalar.activation(la[:, t, :], la[:, t, :], ACT.Exp, scale=-1.0))
                        ready()
                        for t in range(2):
                            did(nc.scalar.activation(la[:, t, :], la[:, t, :], ACT.Ln,
                                                     bias=cst[:, C_UNIT:C_UNIT + 1]),
                                alpha_log, at(li, 2, t))

                def decays(li, n):
                    for t in range(2):
                        if n == EXP_AT[t]:
                            act.wait_ge(decay_sum, at(li, 2, t))
                            did(nc.scalar.activation(dec[:, t, :], last[:, t, :], ACT.Exp,
                                                     scale=1 / TAU))
                            did(nc.scalar.activation(eb[t][:, 0:SEQ], lb[:, t, :], ACT.Exp,
                                                     scale=1 / TAU))
                            did(nc.scalar.activation(la[:, t, :], lb[:, t, :], ACT.Exp,
                                                     scale=-1 / TAU), decay_b, at(li, 2, t))
                        if n == END_AT[t]:
                            act.wait_ge(decay_l, at(li, 2, t))
                            did(nc.scalar.activation(lb[:, t, :], lb[:, t, :], ACT.Exp,
                                                     scale=-1 / TAU), decay_exp, at(li, 2, t))

                def queries_b(n):
                    decays(li, n)
                    for j in range(J_B, J_VB):
                        if A_DONE[j] == n - 1:
                            roll(li, j)
                            if j == J_B:
                                act.wait_ge(bias_ready, at(li, 1, 0))
                            copy_fm(li, *plan[j][2], 5 + j % 2)

                attention(li, "a", prob_a, st_a, queries_b)
                for b, step in enumerate((0, 1, None, None)):
                    act.wait_ge(kend_mm, at(li, NB, b))
                    ready()
                    did(nc.scalar.activation(kendT[:, b, :], PS[:, 6 + b % 2, 0:256], ACT.Copy),
                        kend_T, at(li, NB, b))
                    if step is not None:
                        roll(li, J_VB + step)
                for j in range(J_VB + 2, J_VB + 4):
                    roll(li, j)
                copy_tm(li, 2, vb, 0, 512)
                act.wait_ge(cg_scaled, at(li, 1, 0))
                for t in range(4):
                    did(nc.scalar.activation(cg[:, t, :], cg[:, t, :], ACT.Silu))
                act.wait_ge(o_mm, at(li, 1, 0))

                def o_square(hh):
                    if hh >= 2:
                        act.wait_ge(o_sum, at(li, C_HEADS, hh - 2))
                    ready()
                    did(nc.scalar.activation(sq[:, hh % 2, :], PS[:, 4 + hh, :], ACT.Square),
                        o_sq, at(li, C_HEADS, hh))

                for hh in range(C_HEADS):
                    o_square(hh)
                roll(li, J_VB + 4)
                act.wait_ge(o_sum, at(li, C_HEADS, C_HEADS - 1))
                did(nc.scalar.activation(ms[:, :], PS[:, 2, 0:C_HEADS * NB], ACT.Sqrt,
                                         bias=cst[:, C_EPS:C_EPS + 1], scale=1.0 / P),
                    o_std, at(li, 1, 0))
                for j in range(J_VB + 5, PROJ):
                    roll(li, j)
                copy_tm(li, 3, vb, 512, 256, lambda b: (b // 2, b % 2 * 256))

                def split_y(t, dest, src):
                    did(nc.scalar.activation(dest, src, ACT.Copy), y_hi, at(li, 10, t))

                act.wait_ge(o_done, at(li, C_HEADS, 3))
                for t in range(4):
                    split_y(t, yhi[:, t, :], aq[:, t, :])

                def merge_a(n):
                    for s in range(MERGE_A):
                        if B_DONE[s] != n - 1:
                            continue
                        wait_step(li, S_MA + s)
                        hi(li, S_MA + s + 2, A_SLABS[s % 2] if s + 2 < MERGE_A else 8)
                    for m in range(KD):
                        if gate_at(m) == n:
                            act.wait_ge(agate_scaled, at(li, KD, m))
                            did(nc.scalar.activation(gate[:, m % 2, :], gate[:, m % 2, :],
                                                     ACT.Sigmoid,
                                                     bias=vec[:, V_BG + 3 * m:V_BG + 3 * m + 1]),
                                gated_a, past(li, KD, m))

                attention(li, "b", prob_b, st_b, merge_a)
                act.wait_ge(merged_a, past(li, KD, KD - 1))
                ready()
                for t in range(4):
                    split_y(4 + t, yhi[:, t, :], cg[:, t, :])
                act.wait_ge(head_read, at(li, NPAIR, NPAIR - 1))
                for t in range(2):
                    split_y(8 + t, ybhi[:, t, :], bq[:, t, :])
                with lane.loop("merge", 2) as i:
                    act.wait_ge(gate_bias, at(li, 2, 0) + i)
                    for m in range(4):
                        for c in range(3):
                            n = 3 * m + c
                            wait_step(li, S_MBC + n, i, 12)
                            hi(li, S_MBC + n + 2, BC_SLABS[(n + 2) % 3], i, 12)
                            if c < 2:
                                act.wait_ge(mgate_scaled, past(li, 16, 2 * m + c) + i * 8)
                                did(nc.scalar.activation(
                                    gate[:, c, :], gate[:, c, :], ACT.Sigmoid,
                                    bias=bgate[:, 3 * m + 2 - c:3 * m + 3 - c]),
                                    gated, past(li, 16, 2 * m + c) + i * 8)
                load_sqrt()
                with lane.loop("wout", 2) as i:
                    for m in range(4):
                        wait_step(li, S_WOUT + m, i, 4)
                        f_square(li, 1, m, i, 4 + m)
                        hi(li, S_WOUT + m + 2, 8, i, 4)
                f_root(li, 1, C_EPS, 1.0)
                ffn(li, 1)

        @block.tensor
        def _(pe):
            pe.sem_inc(step_done, PAIR)
            plan = proj_plan()

            def mm3(out, ahi, alo, bhi, blo, start, stop, shared=False):
                nc.tensor.matmul(out, ahi, blo, start=start, stop=False, skip_group_check=shared)
                nc.tensor.matmul(out, alo, bhi, start=False, stop=False, skip_group_check=shared)
                return nc.tensor.matmul(out, ahi, bhi, start=False, stop=stop,
                                        skip_group_check=shared)

            def want(li, s, i=0, per_iter=0):
                pe.wait_ge(w_ready, at(li, NS, s) + i * per_iter + RAW)

            def slab(s, k):
                return whi[:, s % PAIR, k * P:(k + 1) * P], wlo[:, s % PAIR, k * P:(k + 1) * P]

            def column(s, bank, slabs, khi, klo, k0=0, first=True, last=True, w0=0, within=None):
                for k in range(slabs):
                    if within is not None and k == within[0]:
                        within[1]()
                    a, b = slab(s, w0 + k)
                    ins = mm3(PS[:, bank, :], a, b, khi[:, k0 + k, :], klo[:, k0 + k, :],
                              first and k == 0, last and k == slabs - 1)
                return ins

            def sum_rows(bank, src):
                return nc.tensor.matmul(PS[:, bank, :], onesm, src, start=True, stop=True)

            def token_sums(bank, col, src, start, stop):
                for b in range(NB):
                    ins = nc.tensor.matmul(PS[:, bank, col + b:col + b + 1],
                                           src[:, b * P:(b + 1) * P], onesm[:, 0:1],
                                           start=start and b == 0, stop=stop and b == NB - 1,
                                           skip_group_check=True)
                return ins

            def spread(li, z):
                pe.wait_ge(xdiag_ready, at(li, 6, z))
                sum_rows(0, xd).then_inc(rms_mm, 1)

            def lead(li, p, s0, bank):
                want(li, s0)
                for k in range(KD):
                    pe.wait_ge(x_ready, at(li, 24, 8 * p + k))
                    a, b = slab(s0, k)
                    ins = mm3(PS[:, bank, :], a, b, xhi[:, k, :], xlo[:, k, :], k == 0, k == KD - 1)
                ins.then_inc(step_done, 1)

            def h_sums(li, p):
                pe.wait_ge(consts_in, 16)
                pe.wait_ge(hsq_added, at(li, 24, 8 * p + 7) + 2)
                token_sums(0, 0, acc, True, True).then_inc(hsum_mm, 1)

            def postnorm(li, q):
                pe.wait_ge(fsq_added, at(li, 24, 8 * q + 7))
                token_sums(0, 0, acc, True, True).then_inc(fsum_mm, 1)
                spread(li, 2 * q + 1)

            def ffn(li, fi):
                s0 = S_FFN[fi]

                def in_step(c, i, within=None):
                    want(li, s0 + c, i, 4)
                    if c % 2 == 0:
                        pe.wait_ge(ffn_read, at(li, 2 * KF, fi * KF + c // 2) + i * 2)
                    column(s0 + c, 1 + c, 8, xhi, xlo, within=within).then_inc(step_done, 1)

                pe.wait_ge(ffn_read, at(li, 2 * KF, fi * KF))
                lead(li, 2 * fi, s0, 1)
                in_step(1, 0)
                in_step(2, 0, (4, lambda: h_sums(li, 2 * fi)))
                in_step(3, 0, (2, lambda: spread(li, 4 * fi)))
                with pe.Fori(1, FFN_IN // 4) as i:
                    for c in range(4):
                        in_step(c, i)
                with pe.Fori(0, 2) as i:
                    for m in range(4):
                        pe.wait_ge(f_read, at(li, 24, 16 * fi + m) + i * 4)
                        for c in range(3):
                            s = s0 + FFN_IN + 3 * m + c
                            want(li, s, i, 12)
                            pe.wait_ge(hid_ready,
                                       past(li, 2 * KF, fi * KF + 8 * c + OUT_SLABS[c] - 1))
                            column(s, OUT_BANKS[m], OUT_SLABS[c], hidhi, hidlo, 8 * c, c == 0,
                                   c == 2).then_inc(step_done, 1)
                postnorm(li, 2 * fi)

            with pe.Fori(0, DEPTH) as li:
                pe.wait_ge(layer_vecs, at(li, 1, 0))
                ffn(li, 0)
                bank_user = {}
                tile, rope, pending = 0, 0, []

                def rotate(bank=4):
                    c, r, src = pending.pop(0)
                    pe.wait_ge(fm_copied, at(li, NFM, c))
                    pe.wait_ge(roped, at(li, ROPED, r) + 1)
                    nc.tensor.matmul(PS[:, bank, :], cst[:, C_ROT:C_ROT + P], src, start=True,
                                     stop=True).then_inc(rot_mm, 1)

                def take(bank):
                    nonlocal tile
                    if bank in bank_user:
                        pe.wait_ge(fm_copied, at(li, NFM, bank_user[bank]))
                    bank_user[bank] = tile
                    tile += 1

                def fm_blocks(j, bank, within=None):
                    want(li, S_PROJ + j)
                    take(bank)
                    for k in range(KD):
                        if within is not None and k == within[0]:
                            within[1]()
                        a, b = slab(S_PROJ + j, k)
                        ins = mm3(PS[:, bank, :], a, b, xhi[:, k, :], xlo[:, k, :], k == 0,
                                  k == KD - 1)
                        if k == KD - 1:
                            ins.then_inc(step_done, 1)
                            if plan[j][2][0] in ("iq", "aq", "bq", "bk"):
                                to_rotate(xr[:, rope % 2, :])
                        yield

                def to_rotate(src):
                    nonlocal rope
                    pending.append((tile - 1, rope, src))
                    rope += 1

                def fm_step(j, bank, within=None):
                    for _ in fm_blocks(j, bank, within):
                        pass

                def go(blocks, n):
                    for _ in range(n):
                        next(blocks, None)

                def tm_blocks(j0, n, place):
                    for j in range(j0, j0 + 4):
                        s = S_PROJ + j
                        want(li, s)
                        for b in range(NB):
                            bank, col = place(b)
                            for k in (2 * (j - j0), 2 * (j - j0) + 1):
                                w = slice(k % 2 * n, (k % 2 + 1) * n)
                                ins = mm3(PS[:, bank, col:col + n], xhi[:, k, b * P:(b + 1) * P],
                                          xlo[:, k, b * P:(b + 1) * P], whi[:, s % PAIR, w],
                                          wlo[:, s % PAIR, w], k == 0 and col == 0,
                                          k == KD - 1 and (n == 512 or col > 0), n < 512)
                                if b == NB - 1 and k % 2:
                                    ins.then_inc(step_done, 1)
                                if n * (k % 2 + 1) >= 512:
                                    yield

                def attention(kind, q, kk, v, prob, blocks, fill, before_scores, before_blocks):
                    items, i0, g0 = ITEMS[kind], ITEM0[kind], GRP0[kind]
                    grp, before = g0, None

                    def scores(n):
                        if n >= 2 or n and kind == "b":
                            pe.wait_ge(score_read, at(li, NITEM, i0 + n - (2 if kind == "a" else 1)))
                        _, b, segs = items[n]
                        banks = [n % 2] if kind == "a" else [0, 1, 2]
                        for bank, (qt, kt, half, first, nblk, _, _) in zip(banks, segs):
                            r = slice(half * HD, half * HD + HD)
                            ins = nc.tensor.matmul(
                                PS[:, bank, 0:nblk * P], q[r, qt, b * P:(b + 1) * P],
                                kk[r, kt, first * P:(first + nblk) * P], start=True, stop=True)
                        ins.then_inc(score_mm, 1)

                    def weigh(state):
                        hd, b, g, blks, first, last = state
                        pe.wait_ge(turned, at(li, NGRPS, g))
                        half = hd % 2
                        if first and b == 0 and half == 0 and hd:
                            pe.wait_ge(head_read, at(li, NPAIR, PAIR0[kind] + hd // 2 - 1))
                        for x, (_, kb, vcol) in enumerate(blks):
                            ins = nc.tensor.matmul(
                                PS[half * HD:half * HD + HD, 4, b * P:(b + 1) * P],
                                v[:, kb, vcol:vcol + HD], turn[:, g % 2, x * P:(x + 1) * P],
                                start=first and x == 0, stop=last and x == len(blks) - 1)
                        if last and b == NB - 1 and half:
                            ins.then_inc(head_mm, 1)

                    go(blocks, fill[0] // 3)
                    before_scores()
                    scores(0)
                    if kind == "a":
                        scores(1)
                    go(blocks, fill[0] // 3)
                    if kind == "b":
                        scores(1)
                    go(blocks, fill[0] - 2 * (fill[0] // 3))
                    for n, (hd, b, segs) in enumerate(items):
                        if kind == "b" and n + 2 < len(items):
                            scores(n + 2)
                        if kind == "a" and n % 2 == 0 and n + 2 < len(items):
                            scores(n + 2)
                            scores(n + 3)
                        pe.wait_ge(prob_ready, at(li, NITEM, i0 + n))
                        gs = groups_of(segs)
                        for x, blks in enumerate(gs):
                            if grp - g0 >= 2:
                                pe.wait_ge(turned, at(li, NGRPS, grp - 2))
                            for y, (col, _, _) in enumerate(blks):
                                ins = nc.tensor.matmul(
                                    PS[:, TURN[kind][grp % 2], y * P:(y + 1) * P],
                                    prob[:, n % PROBS, col:col + P], ident, start=True, stop=True,
                                    is_transpose=True)
                            ins.then_inc(turn_mm, 1)
                            if before is not None:
                                weigh(before)
                            before = (hd, b, grp, blks, x == 0, x == len(gs) - 1)
                            grp += 1
                            if x == 0:
                                before_blocks(n)
                            here = behind(n, *fill)
                            go(blocks, (x + 1) * here // len(gs) - x * here // len(gs))
                    weigh(before)

                take(5)
                to_rotate(misc[:, :])
                lead(li, 1, S_PROJ, 5)
                for j in range(1, J_CKV):
                    fm_step(j, 5 + j % 3, {2: (4, lambda: h_sums(li, 1)),
                                           3: (2, lambda: spread(li, 2))}.get(j))
                    if j >= 2:
                        rotate()
                    if j == 3:
                        for b in range(NB):
                            ins = nc.tensor.matmul(PS[:, 1, b * 8:(b + 1) * 8],
                                                   misc[64:72, b * P:(b + 1) * P],
                                                   cst[64:72, C_ID + 64:C_ID + 72],
                                                   start=True, stop=True)
                        ins.then_inc(widx_mm, 1)

                def latent_blocks():
                    yield from fm_blocks(J_CKV, 5 + J_CKV % 3)
                    for j in range(J_AQ, J_KA):
                        yield from fm_blocks(j, 5 + j % 3)
                    s = S_PROJ + J_KA
                    want(li, s)
                    pe.wait_ge(ckv_ready, at(li, 1, 0))
                    for t in range(4):
                        take((3, 5, 6, 7)[t])
                        a, b = slab(s, t)
                        ins = mm3(PS[:, (3, 5, 6, 7)[t], :], a, b, ckvhi[:, :], ckvlo[:, :], True,
                                  True)
                        if t == 3:
                            ins.then_inc(step_done, 1)
                        to_rotate(xr[:, rope % 2, :])
                        yield

                def values_a(b):
                    s = S_PROJ + J_VA
                    bank = (3, 5, 6, 7)[b]
                    if b == 0:
                        want(li, s)
                    pe.wait_ge(fm_copied, at(li, NFM, bank_user[bank]))
                    ins = mm3(PS[:, bank, :], ckvhi[:, b * P:(b + 1) * P],
                              ckvlo[:, b * P:(b + 1) * P], whi[:, s % PAIR, 0:512],
                              wlo[:, s % PAIR, 0:512], True, True)
                    if b == 3:
                        ins.then_inc(step_done, 1)

                blocks = latent_blocks()
                for _ in range(2):
                    go(blocks, IDX_FILL[0] // 3)
                    rotate()
                go(blocks, IDX_FILL[0] - 2 * (IDX_FILL[0] // 3))
                pe.wait_ge(widx_ready, at(li, 1, 0))
                pe.wait_ge(roped, at(li, ROPED, 4) + 2)
                pe.wait_ge(ik_copied, (li + 1) * 16)
                for n in range(NIDX):
                    b, hd = n // 8, n % 8
                    r = slice((hd % 2) * HD, (hd % 2) * HD + HD)
                    if n >= 3:
                        pe.wait_ge(idx_relu, at(li, NIDX, n - 3))
                    nc.tensor.matmul(PS[:, n % 3, 0:(b + 1) * P], iq[r, hd // 2, b * P:(b + 1) * P],
                                     ik[r, 0, 0:(b + 1) * P], start=True,
                                     stop=True).then_inc(idx_mm, 1)
                    if n == IDX_DONE[J_CKV] + 4:
                        pe.wait_ge(ckv_sq, at(li, 1, 0))
                        token_sums(3, 0, sq[:, 0, :], True, True).then_inc(ckv_sum, 1)
                    if n == IDX_DONE[J_CKV] + 8:
                        pe.wait_ge(ckv_diag, at(li, 1, 0))
                        sum_rows(3, xd).then_inc(ckv_inv, 1)
                    for j in range(J_AQ, J_KA):
                        if IDX_DONE[j] == n - 2:
                            rotate()
                    if KA_AT <= n < KA_AT + 4:
                        rotate()
                    if n == KA_AT + 2:
                        values_a(0)
                        values_a(1)
                        values_a(2)
                    if n == KA_AT + 3:
                        values_a(3)
                    go(blocks, behind(n, *IDX_FILL))
                pe.wait_ge(tm_copied, at(li, 16, 3))
                for j in range(J_C, J_VC):
                    fm_step(j, 5 + j % 3)
                pe.wait_ge(idx_relu, at(li, NIDX, NIDX - 1))
                values = tm_blocks(J_VC, 512, lambda b: (b, 0))
                go(values, 8)
                pe.wait_ge(walpha_in, (li + 1) * 16)
                pe.wait_ge(fm_copied, at(li, NFM, tile - 1))
                for t in range(2):
                    ins = nc.tensor.matmul(PS[:, 6 + t, :], wal[96:112, t * P:(t + 1) * P],
                                           misc[96:112, :], start=True, stop=True)
                ins.then_inc(alpha_mm, 1)
                go(values, 32)

                def b_blocks():
                    for j in range(J_B, J_VB):
                        if j == J_B + 1:
                            pe.wait_ge(alpha_min, at(li, 2, 1))
                        yield from fm_blocks(j, 5 + j % 2)

                def b_rotate(n):
                    for j in range(J_B, J_VB):
                        if rope_at(j) == n:
                            rotate(7)

                def a_ready():
                    pe.wait_ge(tm_copied, at(li, 16, 7))
                    pe.wait_ge(roped, at(li, ROPED, 12) + 2)

                pe.wait_ge(fm_copied, at(li, NFM, tile - 1))
                attention("a", aq, ak, va, prob_a, b_blocks(), A_FILL, a_ready, b_rotate)
                pe.wait_ge(score_read, at(li, NITEM, ITEM0["b"] - 1))
                values = tm_blocks(J_VB, 512, lambda b: (b, 0))
                go(values, 3)
                b_rotate(len(ITEMS["a"]))
                go(values, 3)
                pe.wait_ge(decay_ready, at(li, 2, 1))
                pe.wait_ge(fm_copied, at(li, NFM, NFM - 1))
                pe.wait_ge(roped, at(li, ROPED, ROPED - 1) + 2)

                def key_end(b):
                    if b >= 2:
                        pe.wait_ge(kend_T, at(li, NB, b - 2))
                    for t in range(2):
                        ins = nc.tensor.matmul(PS[:, 6 + b % 2, t * P:(t + 1) * P],
                                               lb[:, t, b * P:(b + 1) * P], ident, start=True,
                                               stop=True, is_transpose=True)
                    ins.then_inc(kend_mm, 1)

                def key_value(n):
                    r = slice((n % 2) * CH, (n % 2) * CH + CH)
                    if n >= 2:
                        pe.wait_ge(kv_read, at(li, 7, n - 2))
                    for pr in range(2):
                        ins = nc.tensor.matmul(PS[:, 6 + n % 2, pr * 256:(pr + 1) * 256],
                                               kendT[r, n // 2, pr * P:(pr + 1) * P],
                                               vc[r, n // 2, pr * 256:(pr + 1) * 256],
                                               start=True, stop=True)
                    ins.then_inc(kv_mm, 1)

                def within(b):
                    if b >= 1:
                        pe.wait_ge(att_ready, at(li, NB, b - 1))
                    for hd in range(C_HEADS):
                        r = slice((hd % 2) * HD, (hd % 2) * HD + HD)
                        t = slice(b * P, (b + 1) * P)
                        ins = nc.tensor.matmul(PS[:, 4 + hd % 2, (hd // 2) * P:(hd // 2 + 1) * P],
                                               la[r, hd // 2, t], cq[r, hd // 2, t],
                                               start=True, stop=True)
                    ins.then_inc(att_mm, 1)

                def output(b):
                    pe.wait_ge(att_ready, at(li, NB, NB - 1))
                    for hd in range(C_HEADS):
                        r = slice((hd % 2) * HD, (hd % 2) * HD + HD)
                        ins = nc.tensor.matmul(PS[:, 4 + hd, b * P:(b + 1) * P],
                                               vc[:, b, hd * P:(hd + 1) * P],
                                               attT[b][:, hd % 2, (hd // 2) * P:
                                                    (hd // 2 + 1) * P],
                                               start=True, stop=False, skip_group_check=True)
                        for n in (2 * b, 2 * b + 1):
                            if n == 0:
                                continue
                            ins = nc.tensor.matmul(PS[:, 4 + hd, n * CH:(n + 1) * CH],
                                                   state[r, n, hd // 2, :],
                                                   cq[r, hd // 2, n * CH:(n + 1) * CH],
                                                   start=False, stop=n % 2 == 1,
                                                   skip_group_check=True)
                    if b == NB - 1:
                        ins.then_inc(o_mm, 1)

                for b in range(NB):
                    key_end(b)
                    if b < NB - 1:
                        go(values, 6)
                pe.wait_ge(kend_T, at(li, NB, NB - 1))
                for b in range(NB):
                    for n in (2 * b, 2 * b + 1):
                        if n < 7:
                            key_value(n)
                            go(values, 1)
                    within(b)
                go(values, 32)
                pe.wait_ge(kv_read, at(li, 7, 6))
                for b in range(NB):
                    output(b)
                pe.wait_ge(tm_copied, at(li, 16, 11))
                values = tm_blocks(J_VB + 4, 256, lambda b: (b // 2, b % 2 * 256))
                for hd in range(C_HEADS):
                    go(values, (2, 0, 1, 1)[hd])
                    pe.wait_ge(o_sq, at(li, C_HEADS, hd))
                    token_sums(2, hd * NB, sq[:, hd % 2, :], True, True).then_inc(o_sum, 1)
                for hd in range(C_HEADS):
                    go(values, (5, 1, 2, 16)[hd])
                    pe.wait_ge(diag_ready, at(li, C_HEADS, hd))
                    if hd >= 2:
                        pe.wait_ge(o_done, at(li, C_HEADS, hd - 2))
                    sum_rows(3 - hd % 2, diag[:, hd % 2, :, :].rearrange("p b n -> p (b n)")
                             ).then_inc(inv_mm, 1)

                def a_blocks():
                    for m in range(KD):
                        for c in range(2):
                            s = S_MA + 2 * m + c
                            want(li, s)
                            if c == 0:
                                if m >= 1:
                                    pe.wait_ge(agate_scaled, at(li, KD, m - 1))
                            else:
                                pe.wait_ge(merged_a, past(li, KD, m - 1))
                                pe.wait_ge(y_ready, at(li, 10, 3))
                            src = (xhi, xlo) if c == 0 else (yhi, ylo)
                            for k in range(A_SLABS[c]):
                                a, b = slab(s, k)
                                ins = mm3(PS[:, 5 + c, :], a, b, src[0][:, k, :], src[1][:, k, :],
                                          k == 0, k == A_SLABS[c] - 1)
                                if k == A_SLABS[c] - 1:
                                    ins.then_inc(step_done, 1)
                                yield

                def b_ready():
                    pe.wait_ge(tm_copied, at(li, 16, 15))
                    pe.wait_ge(o_done, at(li, C_HEADS, 3))

                pe.wait_ge(o_done, at(li, C_HEADS, 1))
                attention("b", bq, bk, vb, prob_b, a_blocks(), B_FILL, b_ready, lambda n: None)
                with pe.Fori(0, 2) as i:
                    pe.wait_ge(score_read, at(li, NITEM, NITEM - 1))
                    for m in range(4):
                        s = S_MBC + 3 * m
                        for c in range(2):
                            pe.wait_ge(mgate_scaled, past(li, 16, 2 * m - 1) + i * 8)
                            want(li, s + c, i, 12)
                            column(s + c, c, 8, xhi, xlo).then_inc(step_done, 1)
                        pe.wait_ge(y_ready, at(li, 10, 9))
                        pe.wait_ge(merged, past(li, KD, m - 1) + i * 4)
                        want(li, s + 2, i, 12)
                        column(s + 2, 2, 4, yhi, ylo)
                        column(s + 2, 3, 2, ybhi, yblo, w0=4).then_inc(step_done, 1)
                with pe.Fori(0, 2) as i:
                    for m in range(4):
                        s = S_WOUT + m
                        pe.wait_ge(f_read, at(li, 24, 8 + m) + i * 4)
                        want(li, s, i, 4)
                        for k in range(KD):
                            if m == 0:
                                pe.wait_ge(merged, past(li, KD, k))
                            a, b = slab(s, k)
                            ins = mm3(PS[:, 4 + m, :], a, b, mghi[:, k, :], mglo[:, k, :],
                                      k == 0, k == KD - 1)
                        ins.then_inc(step_done, 1)
                postnorm(li, 1)
                ffn(li, 1)

        @block.vector
        def _(dve):
            lane = Lane(dve, order_v, "dve", per)
            did, ready = lane.did, lane.ready
            TT, TS, STT = (nc.vector.tensor_tensor, nc.vector.tensor_scalar,
                           nc.vector.scalar_tensor_tensor)
            dve.sem_inc(hid_ready, 1)
            dve.sem_inc(hsq_added, 2)
            dve.sem_inc(mgate_scaled, 1)
            dve.sem_inc(merged_a, 1)
            dve.sem_inc(merged, 1)
            dve.sem_inc(ffn_read, 2)
            dve.sem_inc(f_read, 4)
            dve.sem_inc(roped, 2)
            dve.wait_ge(angles_in, 32)

            def wait_step(li, s, i=0, per_iter=0):
                dve.wait_ge(step_done, at(li, NS, s) + i * per_iter + PAIR)

            ang, turns = sq[:, 0, :], sq[:, 1, :]
            TWO_PI = 2 * np.pi
            C1 = 6.28125
            C2 = float(np.float32(round((TWO_PI - C1) * 2 ** 20) / 2 ** 20))
            C3 = TWO_PI - C1 - C2
            MAGIC = 1.5 * 2.0 ** 23
            did(nc.vector.tensor_copy(ang, acc[:, :].bitcast(I32)))
            ready()
            did(TS(ang, ang, cst[:, C_FREQ:C_FREQ + 1], None, ALU.mult))
            ready()
            did(TS(turns, ang, 1 / TWO_PI, MAGIC, ALU.mult, ALU.add))
            ready()
            did(TS(turns, turns, -MAGIC, None, ALU.add))
            for c in (C1, C2, C3):
                ready()
                did(STT(out=ang, in0=turns, scalar=-c, in1=ang, op0=ALU.mult, op1=ALU.add))
            LIM = 3.1415925
            ready()
            did(TS(xt[:, 0, :], ang, LIM, -LIM, ALU.min, ALU.max))
            ready()
            did(TS(ang, ang, np.pi / 2, None, ALU.add))
            ready()
            did(TS(turns, ang, np.pi, -TWO_PI, ALU.is_gt, ALU.mult))
            ready()
            did(TT(ang, ang, turns, ALU.add))
            ready()
            did(TS(xt[:, 1, :], ang, LIM, -LIM, ALU.min, ALU.max), tables, 1)
            dve.wait_ge(x_in, 16 * (KD + 1))
            dve.sem_inc(h_new, 8)

            def ffn_x(li, p, k):
                g = V_PRE[p] + k
                dve.wait_ge(x_hi, at(li, 24, 8 * p + k))
                did(STT(out=xlo[:, k, :], in0=h[:, k, :], scalar=vec[:, g:g + 1],
                        in1=xhi[:, k, :].bitcast(F32), op0=ALU.mult, op1=ALU.subtract),
                    x_ready, at(li, 24, 8 * p + k))

            def spread(inverse):
                return TT(xdiag[:, :, :], ident.unsqueeze(1).to_broadcast([P, NB, P]),
                          inverse.unsqueeze(2).to_broadcast([P, NB, P]), ALU.mult)

            def inverse(li, z):
                dve.wait_ge(std_ready, at(li, 6, z))
                ready()
                did(nc.vector.reciprocal(xinv[:, :], ms[:, 0:NB]))
                ready()
                did(spread(xinv[:, :]), xdiag_ready, at(li, 6, z))
                dve.wait_ge(rms_mm, at(li, 6, z))

            def prenorm(li, p):
                for k in range(KD):
                    dve.wait_ge(hsq, past(li, 24, 8 * p + k))
                    ready()
                    if k == 0:
                        ins = TS(acc[:, :], sq[:, 0, :], 1.0, None, ALU.mult)
                    else:
                        ins = TT(acc[:, :], acc[:, :], sq[:, k % 2, :], ALU.add)
                    did(ins, hsq_added, at(li, 24, 8 * p + k) + 2)
                inverse(li, 2 * p)
                ready()
                did(TS(rstd[:, :], PS[:, 0, :], 1.0, None, ALU.mult))

            def f_tile(li, q, m, i, bank):
                dve.wait_ge(fsq, at(li, 24, 8 * q + m) + i * 4)
                ready()
                did(TT(acc[:, :], acc[:, :], sq[:, m % 2, :], ALU.add), fsq_added,
                    at(li, 24, 8 * q + m) + i * 4)
                did(TS(f[:, bass.ds(i * 4 + m, 1), :], PS[:, bank:bank + 1, :], 1.0, None, ALU.mult),
                    f_read, at(li, 24, 8 * q + m) + i * 4 + 4)

            def postnorm(li, q, p):
                inverse(li, 2 * q + 1)
                ready()
                for k in range(KD):
                    g = V_POST[q] + k
                    did(STT(out=f[:, k, :], in0=f[:, k, :], scalar=vec[:, g:g + 1],
                            in1=PS[:, 0, :], op0=ALU.mult, op1=ALU.mult),
                        f_scaled, at(li, 24, 8 * q + k))
                    if p is not None and k >= 3:
                        dve.wait_ge(h_new, at(li, 24, 8 * (q + 1) + k - 3))
                        ffn_x(li, p, k - 3)
                if p is not None:
                    for k in range(KD - 3, KD):
                        dve.wait_ge(h_new, at(li, 24, 8 * (q + 1) + k))
                        ffn_x(li, p, k)

            def ffn(li, fi):
                s0 = S_FFN[fi]
                prenorm(li, 2 * fi)
                with lane.loop(f"ffn_in{fi}", FFN_IN // 4) as i:
                    for c in range(2):
                        t = fi * KF + c
                        wait_step(li, s0 + 2 * c, i, 4)
                        ready()
                        did(TT(silu[:, c, :], PS[:, 1 + 2 * c, :], rstd[:, :], ALU.mult),
                            gate_scaled, at(li, 2 * KF, t) + i * 2)
                        wait_step(li, s0 + 2 * c + 1, i, 4)
                        did(TT(hf[:, 0, :], PS[:, 2 + 2 * c, :], rstd[:, :], ALU.mult),
                            ffn_read, at(li, 2 * KF, t) + i * 2 + 2)
                        dve.wait_ge(silu_ready, at(li, 2 * KF, t) + i * 2)
                        ready()
                        did(TT(hf[:, 0, :], hf[:, 0, :], silu[:, c, :], ALU.mult))
                        j = i * 2 + c
                        ready()
                        did(TS(hidhi[:, bass.ds(j, 1), :], hf[:, :, :], 1.0, None, ALU.mult))
                        ready()
                        did(TT(hidlo[:, bass.ds(j, 1), :], hf[:, :, :],
                               hidhi[:, bass.ds(j, 1), :].bitcast(F32), ALU.subtract),
                            hid_ready, past(li, 2 * KF, t) + i * 2)
                ready()
                did(nc.vector.memset(acc[:, :], 0.0))
                with lane.loop(f"ffn_out{fi}", 2) as i:
                    for m in range(4):
                        f_tile(li, 2 * fi, m, i, OUT_BANKS[m])

            rope_n = [0]

            def rope(li, c, dest, src, bank=4, rows=P, cos=cosr, sin=sinr):
                r = rope_n[0]
                rope_n[0] += 1
                dve.wait_ge(fm_copied, at(li, NFM, c))
                ready()
                did(TT(dest, src, cos[0:rows, :], ALU.mult))
                dve.wait_ge(rot_mm, at(li, ROPED, r))
                did(TT(rt[0:rows, :], PS[0:rows, bank, :], sin[0:rows, :], ALU.mult))
                ready()
                did(TT(dest, dest, rt[0:rows, :], ALU.add), roped, at(li, ROPED, r) + 2)

            def attention(li, kind, prob, st, out, between):
                items, i0 = ITEMS[kind], ITEM0[kind]
                grp_end = []
                grp = GRP0[kind]
                for _, _, segs in items:
                    grp += len(groups_of(segs))
                    grp_end.append(grp - 1)

                def masked(n):
                    hd, b, segs = items[n]
                    dve.wait_ge(score_mm, at(li, NITEM, i0 + n))
                    if n >= PROBS:
                        dve.wait_ge(turn_mm, at(li, NGRPS, grp_end[n - PROBS]))
                    col = 0
                    for g, (_, _, _, first, nblk, mask, _) in enumerate(segs):
                        w = nblk * P
                        bank = n % 2 if kind == "a" else g
                        m = score[:, b, 0:w] if mask is None else cst[:, mask:mask + w]
                        lane.settle()
                        one = len(segs) == 1
                        ins = nc.vector.tensor_tensor_reduce(
                            out=prob[:, n % PROBS, col:col + w], in0=PS[:, bank, 0:w], in1=m,
                            scale=-(HD ** -0.5), scalar=3.0e38, op0=ALU.add, op1=ALU.min,
                            accum_out=st[:, n % PROBS, 3:4] if one else st[:, n % PROBS, g:g + 1])
                        if one:
                            did(ins, score_read, at(li, NITEM, i0 + n))
                        else:
                            did(ins)
                        col += w
                    if not one:
                        ready()
                        did(nc.vector.tensor_reduce(st[:, n % PROBS, 3:4], st[:, n % PROBS, 0:3], AX.X,
                                                    ALU.min), score_read, at(li, NITEM, i0 + n))

                def normal(n):
                    hd, b, segs = items[n]
                    w = sum(s[4] for s in segs) * P
                    dve.wait_ge(exp_ready, at(li, NITEM, i0 + n))
                    total = st[:, n % PROBS, 4:5]
                    if len(segs) > 1:
                        ready()
                        did(nc.vector.tensor_reduce(st[:, n % PROBS, 7:8], st[:, n % PROBS, 4:7], AX.X,
                                                    ALU.add))
                        total = st[:, n % PROBS, 7:8]
                    ready()
                    did(nc.vector.reciprocal(st[:, n % PROBS, 8:9], total))
                    ready()
                    did(TS(prob[:, n % PROBS, 0:w], prob[:, n % PROBS, 0:w], st[:, n % PROBS, 8:9], None,
                           ALU.mult), prob_ready, at(li, NITEM, i0 + n))

                def take_pair(pair):
                    dve.wait_ge(head_mm, at(li, NPAIR, PAIR0[kind] + pair))
                    ready()
                    did(nc.vector.tensor_copy(out[:, pair, :], PS[:, 4, :]),
                        head_read, at(li, NPAIR, PAIR0[kind] + pair))

                masked(0)
                for n in range(len(items)):
                    if n + 1 < len(items):
                        masked(n + 1)
                    normal(n)
                    if n % (2 * NB) == 0 and n:
                        take_pair(n // (2 * NB) - 1)
                    between(n)
                take_pair(len(items) // (2 * NB) - 1)
                between(len(items))

            with lane.loop("layer", DEPTH) as li:
                ready()
                did(TS(vec[:, :], vec2[:, bass.ds(li, 1), :].rearrange("p a n -> p (a n)"), 1.0,
                       None, ALU.mult), layer_vecs, at(li, 1, 0))
                for k in range(KD):
                    ffn_x(li, 0, k)
                ffn(li, 0)
                postnorm(li, 0, 1)
                prenorm(li, 1)
                dve.wait_ge(tables_done, 2)
                ready()
                did(TT(cosr[:, :], cosT[:, :], rstd[:, :], ALU.mult))
                did(TT(sinr[:, :], sinT[:, :], rstd[:, :], ALU.mult))
                rope_n[0] = 0
                rope(li, 0, ik[0:HD, 0, :], misc[0:HD, :], rows=HD)
                did(TT(misc[96:112, :], misc[96:112, :], rstd[96:112, :], ALU.mult))
                for t in range(4):
                    if t == 1:
                        dve.wait_ge(widx_mm, at(li, 1, 0))
                        ready()
                        did(TT(widx[:, :].rearrange("p (b n) -> p b n", n=8),
                               PS[:, 1, 0:32].rearrange("p (b n) -> p b n", n=8),
                               xinv[:, :].unsqueeze(2).to_broadcast([P, NB, 8]), ALU.mult),
                            widx_ready, at(li, 1, 0))
                    rope(li, 1 + t, iq[:, t, :], xr[:, (1 + t) % 2, :])

                def latent(n):
                    if n == IDX_DONE[J_CKV] + 2:
                        dve.wait_ge(fm_copied, at(li, NFM, J_CKV))
                        did(TT(ckv[:, :], ckv[:, :], rstd[:, :], ALU.mult), ckv_f32, at(li, 1, 0))
                    if n == IDX_DONE[J_CKV] + 7:
                        dve.wait_ge(ckv_std, at(li, 1, 0))
                        ready()
                        did(nc.vector.reciprocal(inv[:, 0:NB], ms[:, 0:NB]))
                        ready()
                        did(spread(inv[:, 0:NB]), ckv_diag, at(li, 1, 0))
                    if n == IDX_DONE[J_CKV] + 9:
                        dve.wait_ge(ckv_inv, at(li, 1, 0))
                        ready()
                        did(STT(out=ckv[:, :], in0=ckv[:, :], scalar=vec[:, V_KVN:V_KVN + 1],
                                in1=PS[:, 3, :], op0=ALU.mult, op1=ALU.mult), ckv_n, at(li, 1, 0))
                    if n == IDX_DONE[J_CKV] + 11:
                        dve.wait_ge(ckv_h, at(li, 1, 0))
                        ready()
                        did(TT(ckvlo[:, :], ckv[:, :], ckvhi[:, :].bitcast(F32), ALU.subtract),
                            ckv_ready, at(li, 1, 0))
                    for t in range(4):
                        if n == IDX_DONE[J_AQ + t] + 2:
                            rope(li, 6 + t, aq[:, t, :], xr[:, (5 + t) % 2, :])
                    if KA_AT <= n < KA_AT + 4:
                        t = n - KA_AT
                        rope(li, 10 + t, ak[:, t, :], xr[:, (9 + t) % 2, :], 4, P, cosT, sinT)

                for n in range(NIDX):
                    b, hd = n // 8, n % 8
                    w = (b + 1) * P
                    dve.wait_ge(idx_relu, at(li, NIDX, n))
                    ready()
                    wcol = widx[:, b * 8 + hd:b * 8 + hd + 1]
                    if hd == 0:
                        ins = TS(score[:, b, 0:w], relu[:, n % 2, 0:w], wcol, None, ALU.mult)
                    else:
                        ins = STT(out=score[:, b, 0:w], in0=relu[:, n % 2, 0:w], scalar=wcol,
                                  in1=score[:, b, 0:w], op0=ALU.mult, op1=ALU.add)
                    did(ins, idx_added, at(li, NIDX, n))
                    latent(n)
                cau = cst[:, C_CAU:C_CAU + P]
                ready()
                did(nc.vector.tensor_copy(score[:, 0, 0:P], cau))
                for b in range(1, NB):
                    w = (b + 1) * P
                    did(TT(score[:, b, b * P:w], score[:, b, b * P:w], cau, ALU.add))
                    for _ in range(TOPK // 8):
                        lane.settle()
                        did(nc.vector.max(top8[:, :], score[:, b, 0:w]))
                        lane.settle()
                        did(nc.vector.match_replace(score[:, b, 0:w], top8[:, :], score[:, b, 0:w],
                                                    TAKEN))
                    ready()
                    ins = TS(score[:, b, 0:w], score[:, b, 0:w], -1.0e38, NEG, ALU.is_gt, ALU.mult)
                    if b == NB - 1:
                        did(ins, bias_ready, at(li, 1, 0))
                    else:
                        did(ins)

                dve.wait_ge(alpha_abs, at(li, 2, 1))
                for t in range(2):
                    did(TS(lb[:, t, :], PS[:, 6 + t, :], vec[:, V_BA + t:V_BA + t + 1], 0.0,
                           ALU.add, ALU.min), alpha_min, at(li, 2, t))

                def decays(n):
                    for t in range(2):
                        if n == SUM_AT[t]:
                            if t == 0:
                                did(nc.vector.memset(keep[:, :], 1.0))
                                ready()
                                did(nc.vector.memset(keep[:, :].rearrange("p (n c) -> p n c", c=CH)
                                                     [:, :, 0], 0.0))
                            dve.wait_ge(alpha_log, at(li, 2, t))
                            ready()
                            did(TT(la[:, t, :], lb[:, t, :], la[:, t, :], ALU.subtract))
                            ready()
                            did(nc.vector.tensor_tensor_scan(lb[:, t, :], keep[:, :], la[:, t, :],
                                                             0.0, ALU.mult, ALU.add))
                            ready()
                            did(TS(last[:, t, :], lb[:, t, :].rearrange("p (n c) -> p n c", c=CH)
                                   [:, :, CH - 1], 1.0, None, ALU.mult), decay_sum, at(li, 2, t))
                        if n == SUM_AT[t] + 1:
                            did(TT(cq[:, t, :], cq[:, t, :], rstd[:, :], ALU.mult))
                            did(TT(ck[:, t, :], ck[:, t, :], rstd[:, :], ALU.mult))
                        if n == REL_AT[t]:
                            dve.wait_ge(decay_b, at(li, 2, t))
                            ready()
                            by_chunk = lb[:, t, :].rearrange("p (n c) -> p n c", c=CH)
                            did(TT(by_chunk, by_chunk,
                                   last[:, t, :].unsqueeze(2).to_broadcast([P, SEQ // CH, CH]),
                                   ALU.subtract), decay_l, at(li, 2, t))
                            did(TT(cq[:, t, :], eb[t][:, 0:SEQ], cq[:, t, :], ALU.mult))
                            did(TT(la[:, t, :], la[:, t, :], ck[:, t, :], ALU.mult))
                        if n == KEY_AT[t]:
                            dve.wait_ge(decay_exp, at(li, 2, t))
                            ready()
                            did(TT(lb[:, t, :], lb[:, t, :], ck[:, t, :], ALU.mult), decay_ready,
                                at(li, 2, t))

                def rope_b(n):
                    decays(n)
                    if GATE_AT <= n < GATE_AT + 4:
                        t = n - GATE_AT
                        ins = TT(cg[:, t, :], cg[:, t, :], rstd[:, :], ALU.mult)
                        if t < 3:
                            did(ins)
                        else:
                            did(ins, cg_scaled, at(li, 1, 0))
                    for j in range(J_B, J_VB):
                        if rope_at(j) == n:
                            t = j - J_B
                            dest = bq[:, t, :] if t < 6 else bk[:, t - 6, :]
                            rope(li, 22 + t, dest, xr[:, (13 + t) % 2, :], 7)

                attention(li, "a", prob_a, st_a, aq, rope_b)
                def next_state(n):
                    dve.wait_ge(kv_mm, at(li, 7, n))
                    ready()
                    for pr in range(2):
                        for half in range(2):
                            r = slice(half * HD, half * HD + HD)
                            kv = PS[r, 6 + n % 2, pr * 256 + half * P:pr * 256 + (half + 1) * P]
                            if n == 0:
                                ins = nc.vector.tensor_copy(state[r, 1, pr, :], kv)
                            else:
                                ins = STT(out=state[r, n + 1, pr, :], in0=state[r, n, pr, :],
                                          scalar=dec[r, pr, n:n + 1], in1=kv, op0=ALU.mult,
                                          op1=ALU.add)
                            if pr == 1 and half == 1:
                                did(ins, kv_read, at(li, 7, n))
                            else:
                                did(ins)

                for b in range(NB):
                    for n in (2 * b, 2 * b + 1):
                        if n < 7:
                            next_state(n)
                    dve.wait_ge(att_mm, at(li, NB, b))
                    did(TT(attT[b].rearrange("p a (m n) -> p a m n", n=P),
                           PS[:, 4:6, 0:256].rearrange("p a (m n) -> p a m n", n=P),
                           cst[:, C_GLA:C_GLA + P].unsqueeze(1).unsqueeze(1).to_broadcast(
                               [P, 2, 2, P]), ALU.mult),
                        att_ready, at(li, NB, b))
                for hd in range(C_HEADS):
                    dve.wait_ge(o_sq, at(li, C_HEADS, hd))
                    did(TT(cg[:, hd, :], PS[:, 4 + hd, :], cg[:, hd, :], ALU.mult))
                dve.wait_ge(o_std, at(li, 1, 0))
                ready()
                did(nc.vector.reciprocal(inv[:, :], ms[:, :]))

                def diagonal(hd):
                    if hd >= 2:
                        dve.wait_ge(inv_mm, at(li, C_HEADS, hd - 2))
                    did(TT(diag[:, hd % 2, :, :], ident.unsqueeze(1).to_broadcast([P, NB, P]),
                           inv[:, hd * NB:(hd + 1) * NB].unsqueeze(2).to_broadcast([P, NB, P]),
                           ALU.mult), diag_ready, at(li, C_HEADS, hd))

                ready()
                diagonal(0)
                diagonal(1)
                for hd in range(C_HEADS):
                    dve.wait_ge(inv_mm, at(li, C_HEADS, hd))
                    ready()
                    did(STT(out=cg[:, hd, :], in0=cg[:, hd, :], scalar=vec[:, V_CN:V_CN + 1],
                            in1=PS[:, 3 - hd % 2, :], op0=ALU.mult, op1=ALU.mult), o_done,
                        at(li, C_HEADS, hd))
                    if hd + 2 < C_HEADS:
                        diagonal(hd + 2)

                def split_y(t, dest, src, hi):
                    dve.wait_ge(y_hi, at(li, 10, t))
                    did(TT(dest, src, hi.bitcast(F32), ALU.subtract), y_ready, at(li, 10, t))

                for t in range(4):
                    split_y(t, ylo[:, t, :], aq[:, t, :], yhi[:, t, :])

                def merge_a(n):
                    for m in range(KD):
                        if B_DONE[2 * m] == n - 1:
                            wait_step(li, S_MA + 2 * m)
                            ready()
                            did(TT(gate[:, m % 2, :], PS[:, 5, :], rstd[:, :], ALU.mult),
                                agate_scaled, at(li, KD, m))
                        if max(B_DONE[2 * m + 1] + 1, gate_at(m)) == n:
                            wait_step(li, S_MA + 2 * m + 1)
                            dve.wait_ge(gated_a, past(li, KD, m))
                            did(TT(part[:, m, :], gate[:, m % 2, :], PS[:, 6, :], ALU.mult),
                                merged_a, past(li, KD, m))

                attention(li, "b", prob_b, st_b, bq, merge_a)
                for t in range(4):
                    split_y(4 + t, ylo[:, t, :], cg[:, t, :], yhi[:, t, :])
                for t in range(2):
                    split_y(8 + t, yblo[:, t, :], bq[:, t, :], ybhi[:, t, :])
                with lane.loop("merge", 2) as i:
                    ready()
                    did(TS(bgate[:, :], vec[:, bass.ds(i * 12 + V_BG, 12)], 1.0, None, ALU.mult),
                        gate_bias, at(li, 2, 0) + i)
                    for m in range(4):
                        j = i * 4 + m
                        for c in range(2):
                            wait_step(li, S_MBC + 3 * m + c, i, 12)
                            ready()
                            did(TT(gate[:, c, :], PS[:, c, :], rstd[:, :], ALU.mult), mgate_scaled,
                                past(li, 16, 2 * m + c) + i * 8)
                        wait_step(li, S_MBC + 3 * m + 2, i, 12)
                        dve.wait_ge(gated, past(li, 16, 2 * m + 1) + i * 8)
                        ready()
                        for c in range(2):
                            did(TT(gate[:, c, :], gate[:, c, :], PS[:, 2 + c, :], ALU.mult))
                        ready()
                        did(TT(gate[:, 0, :], gate[:, 0, :], gate[:, 1, :], ALU.add))
                        ready()
                        did(TT(gate[:, 0:1, :], gate[:, 0:1, :], part[:, bass.ds(j, 1), :], ALU.add))
                        ready()
                        did(TS(mghi[:, bass.ds(j, 1), :], gate[:, 0:1, :], 1.0, None, ALU.mult))
                        ready()
                        did(TT(mglo[:, bass.ds(j, 1), :], gate[:, 0:1, :],
                               mghi[:, bass.ds(j, 1), :].bitcast(F32), ALU.subtract),
                            merged, past(li, KD, m) + i * 4)
                ready()
                did(nc.vector.memset(acc[:, :], 0.0))
                with lane.loop("wout", 2) as i:
                    for m in range(4):
                        f_tile(li, 1, m, i, 4 + m)
                postnorm(li, 1, 2)
                ffn(li, 1)
                postnorm(li, 2, None)


def columns(w, tiles, kt):
    d = w.shape[0]
    w = w.reshape(d, kt, P, tiles, P).transpose(0, 3, 2, 1, 4)
    return np.ascontiguousarray(w).reshape(d, tiles, P, kt * P)


def rows(w, n, k2):
    d, r, _ = w.shape
    w = w.reshape(d, r // P // k2, k2, P, n).transpose(0, 1, 3, 2, 4)
    return np.ascontiguousarray(w).reshape(d, r // P // k2, P, k2 * n)


def ffn_in(w):
    w = columns(np.asarray(w), 2 * KF, KD).reshape(DEPTH, 2, KF, P, KD * P)
    return np.ascontiguousarray(w.transpose(0, 2, 1, 3, 4)).reshape(DEPTH, 2 * KF, P, KD * P)


def layout(x, positions, ffn1_pre_g, ffn1_w_in, ffn1_w_out, ffn1_post_g, mix_pre_g, w_in,
           a_kv_norm_g, a_w_kv_up, c_w_alpha_up, c_b_alpha, c_norm_g, w_branch_a, w_branch_b,
           w_branch_c, w_gate, b_gate, w_out, mix_post_g, ffn2_pre_g, ffn2_w_in, ffn2_w_out,
           ffn2_post_g):
    w = np.asarray(w_in)
    part = [w[:, :, OFF[i]:OFF[i + 1]] for i in range(len(SIZES))]
    aq, ackv, iq, ik, iw, bqkv, cq, ck, cv, cg, ca = part
    z = np.zeros
    misc = np.concatenate([ik, iw, z((DEPTH, DM, 24), w.dtype), ca, z((DEPTH, DM, 16), w.dtype)], 2)
    kv = np.asarray(a_w_kv_up).reshape(DEPTH, 1, P, A_HEADS, 2, HD)
    wk = kv[..., 0, :].reshape(DEPTH, 1, P, 512)
    wv = kv[..., 1, :].reshape(DEPTH, 1, P, 512)
    order = [place_b(head) for head in range(GROUPS * B_HEADS)]
    bq, bk = (bqkv[:, :, i:i + 768].reshape(DEPTH, DM, -1, HD)[:, :, order].reshape(DEPTH, DM, 768)
              for i in (0, 768))
    bv = bqkv[:, :, 1536:]
    parts = [columns(np.concatenate([misc, iq, ackv, aq], 2), 10, KD), wk, wv,
             columns(np.concatenate([cq, ck, cg], 2), 8, KD), rows(cv, 512, 2),
             columns(np.concatenate([bq, bk], 2), 12, KD), rows(bv[:, :, :512], 512, 2),
             rows(bv[:, :, 512:], 256, 2)]
    proj = np.concatenate([np.concatenate([p, z(p.shape[:3] + (1024 - p.shape[3],), w.dtype)], 3)
                           for p in parts], 1)
    gates = columns(np.asarray(w_gate), 24, KD).reshape(DEPTH, 3, KD, P, KD * P)
    merge_a = np.concatenate([gates[:, 0], columns(np.asarray(w_branch_a), KD, 4)], 3)
    merge_bc = np.concatenate([gates[:, 2], gates[:, 1], columns(np.asarray(w_branch_c), KD, 4),
                               columns(np.asarray(w_branch_b), KD, 2)], 3)

    def vec(g):
        return np.asarray(g).reshape(DEPTH, -1, P).transpose(2, 0, 1)

    bg = np.asarray(b_gate).reshape(DEPTH, 3, KD, P).transpose(3, 0, 2, 1).reshape(P, DEPTH, 24)
    vecs = np.concatenate([vec(ffn1_pre_g), vec(ffn1_post_g), vec(mix_pre_g), vec(mix_post_g),
                           vec(ffn2_pre_g), vec(ffn2_post_g), vec(a_kv_norm_g), vec(c_norm_g),
                           vec(c_b_alpha), bg], 2)
    arrays = {
        "xT": np.asarray(x)[0].T, "positions": np.asarray(positions), "consts": constants(),
        "vecs": vecs, "walpha": np.asarray(c_w_alpha_up).transpose(1, 0, 2),
        "w_in1": ffn_in(ffn1_w_in), "w_out1": columns(np.asarray(ffn1_w_out), KD, KF),
        "w_proj": proj, "w_ma": merge_a, "w_mbc": merge_bc, "w_wout": columns(np.asarray(w_out), KD, KD),
        "w_in2": ffn_in(ffn2_w_in), "w_out2": columns(np.asarray(ffn2_w_out), KD, KF),
    }
    return {k: np.ascontiguousarray(v) for k, v in arrays.items()}


def kernel(**inputs):
    import concourse.bacc as bacc
    from concourse.bass_utils import run_bass_kernel_spmd

    arrays = layout(**inputs)

    def build(per):
        nc = bacc.Bacc("TRN2", target_bir_lowering=False, num_devices=1)
        args = [nc.dram_tensor(f"in_{k}", v.shape, mybir.dt.from_np(v.dtype),
                               kind="ExternalInput").ap() for k, v in arrays.items()]
        out = nc.dram_tensor("outT", (DM, SEQ), F32, kind="ExternalOutput").ap()
        trunk_kernel(nc, *args, out, per)
        return nc

    per = {}
    build(per)
    nc = build(per)
    r = run_bass_kernel_spmd(nc, [{f"in_{k}": v for k, v in arrays.items()}], core_ids=[0])
    return r.results[0]["outT"].T[None]
```
